# Optimizing a Trainium2 kernel written in Bass

```python
import math
import jax, jax.numpy as jnp
from jax import lax
import numpy as np

D_MODEL = 1024
BATCH = 1
SEQ = 1024
DEPTH = 1
DEC_BATCH = 8
DEC_SEQ = 8
PAST_LEN = 1024
PAGE_SIZE = 128

H_M = 4
DH_M = D_MODEL // 2 // H_M
W_M = H_M * DH_M
H_S = 8
DH_S = D_MODEL // 2 // H_S
W_S = H_S * DH_S
N_IN = 4 * W_M + 2 * H_M + 3 * W_S
MLSTM_CHUNK = 64
SB_QBLOCK = 128
SB_BIAS_INIT = -7.0
GATE_SOFTCAP = 15.0
PEER_HEADS = 8
PEER_NKEYS = 128
PEER_NEXPERTS = PEER_NKEYS * PEER_NKEYS
PEER_DKEY = 256
PEER_TOPK = 16
PEER_BLOCK = 128
EPS = 1e-6

kernel_name = 'hymba_mlstm_stickbreak_peer_step'

def rmsnorm(x, g):
    x = x.astype(jnp.float32)
    return x * lax.rsqrt(jnp.mean(x * x, axis=-1, keepdims=True) + EPS) * g

def softcap(a):
    return GATE_SOFTCAP * jnp.tanh(a / GATE_SOFTCAP)

def split_proj(proj):
    sizes = (W_M, W_M, W_M, W_M, H_M, H_M, W_S, W_S, W_S)
    idx, acc = [], 0
    for s in sizes[:-1]:
        acc += s
        idx.append(acc)
    return jnp.split(proj, idx, axis=-1)

def mlstm_chunkwise(q, k, v, i_pre, logf, C0, n0, m0):
    Bn, Hn, T, d = q.shape
    L = math.gcd(T, MLSTM_CHUNK)
    nc = T // L

    def chunks(a):
        return jnp.moveaxis(a.reshape(a.shape[:2] + (nc, L) + a.shape[3:]), 2, 0)

    causal = jnp.tril(jnp.ones((L, L), dtype=bool))

    def step(carry, inp):
        C, n, m = carry
        qc, kc, vc, ic, fc = inp
        b = jnp.cumsum(fc, axis=-1)
        D = jnp.where(causal, b[..., :, None] - b[..., None, :] + ic[..., None, :], -jnp.inf)
        inter = b + m[..., None]
        mt = jnp.maximum(inter, jnp.max(D, axis=-1))
        w_intra = jnp.exp(D - mt[..., None])
        w_inter = jnp.exp(inter - mt)
        S = jnp.einsum('bhtd,bhsd->bhts', qc, kc) * w_intra
        num = w_inter[..., None] * jnp.einsum('bhvk,bhtk->bhtv', C, qc) + jnp.einsum('bhts,bhsv->bhtv', S, vc)
        dot = w_inter * jnp.einsum('bhk,bhtk->bht', n, qc) + jnp.sum(S, axis=-1)
        h = num / jnp.maximum(jnp.abs(dot), jnp.exp(-mt))[..., None]
        mL = mt[..., -1]
        decay = jnp.exp(b[..., -1:] - b + ic - mL[..., None])
        carry_scale = jnp.exp(b[..., -1] + m - mL)
        C_new = carry_scale[..., None, None] * C + jnp.einsum('bhs,bhsv,bhsk->bhvk', decay, vc, kc)
        n_new = carry_scale[..., None] * n + jnp.einsum('bhs,bhsk->bhk', decay, kc)
        return (C_new, n_new, mL), h

    (C, n, m), hs = lax.scan(step, (C0, n0, m0),
                             (chunks(q), chunks(k), chunks(v), chunks(i_pre), chunks(logf)))
    h = jnp.moveaxis(hs, 0, 2).reshape(Bn, Hn, T, d)
    return h, C, n, m

def stick_breaking(q, k, v, sb_bias, q_offset):
    Bn, Tq, Hn, d = q.shape
    Tk = k.shape[1]
    QB = math.gcd(Tq, SB_QBLOCK)
    nb = Tq // QB
    scale = d ** -0.5
    key_pos = jnp.arange(Tk)
    qb = jnp.moveaxis(q.reshape(Bn, nb, QB, Hn, d), 1, 0)
    bias = sb_bias.astype(jnp.float32)[None, :, None, None]

    def block(args):
        qblk, start = args
        q_pos = q_offset + start + jnp.arange(QB)
        visible = key_pos[None, :] < q_pos[:, None]
        z = jnp.einsum('bqhd,bkhd->bhqk', qblk, k) * scale + bias
        log_1m = jnp.where(visible, jax.nn.log_sigmoid(-z), 0.0)
        between = lax.cumsum(log_1m, axis=3, reverse=True) - log_1m
        A = jnp.where(visible, jnp.exp(jax.nn.log_sigmoid(z) + between), 0.0)
        return jnp.einsum('bhqk,bkhd->bqhd', A, v)

    out = lax.map(block, (qb, jnp.arange(nb) * QB))
    return jnp.moveaxis(out, 0, 1).reshape(Bn, Tq, Hn, d)

def peer(xf, w_query, sub_keys_a, sub_keys_b, expert_u, expert_v):
    T = xf.shape[0]
    qry = (xf @ w_query).reshape(T, PEER_HEADS, 2, PEER_DKEY // 2)
    sa = jnp.einsum('thd,nd->thn', qry[:, :, 0], sub_keys_a)
    sb = jnp.einsum('thd,nd->thn', qry[:, :, 1], sub_keys_b)
    va, ia = lax.top_k(sa, PEER_TOPK)
    vb, ib = lax.top_k(sb, PEER_TOPK)
    cand = (va[..., :, None] + vb[..., None, :]).reshape(T, PEER_HEADS, PEER_TOPK * PEER_TOPK)
    cand_idx = (ia[..., :, None] * PEER_NKEYS + ib[..., None, :]).reshape(T, PEER_HEADS, PEER_TOPK * PEER_TOPK)
    top_s, pos = lax.top_k(cand, PEER_TOPK)
    experts = jnp.take_along_axis(cand_idx, pos, axis=-1).reshape(T, PEER_HEADS * PEER_TOPK)
    gates = jax.nn.softmax(top_s.astype(jnp.float32), axis=-1).reshape(T, PEER_HEADS * PEER_TOPK)
    PB = math.gcd(T, PEER_BLOCK)
    nb = T // PB

    def block(args):
        xb, eb, gb = args
        act = jax.nn.gelu(jnp.einsum('tkd,td->tk', expert_u[eb], xb), approximate=False)
        return jnp.einsum('tk,tkd->td', gb * act, expert_v[eb])

    out = lax.map(block, (xf.reshape(nb, PB, D_MODEL), experts.reshape(nb, PB, -1), gates.reshape(nb, PB, -1)))
    return out.reshape(T, D_MODEL)

def decoder_layer(x, c, k_past, v_past, C0, n0, m0, q_offset, w_ada, b_ada, g_mix, g_ffn, w_in, b_gates,
                  g_q, g_k, sb_bias, g_head, w_out, w_query, sub_keys_a, sub_keys_b, expert_u, expert_v):
    Bn, T, _ = x.shape
    x = x.astype(jnp.float32)
    mod = jax.nn.silu(c.astype(jnp.float32)) @ w_ada + b_ada
    shift_a, scale_a, gate_a, shift_f, scale_f, gate_f = jnp.split(mod[:, None, :], 6, axis=-1)

    h = rmsnorm(x, g_mix) * (1.0 + scale_a) + shift_a
    mq, mk, mv, mo, mi, mf, sq, sk, sv = split_proj(h @ w_in)

    def heads_m(a):
        return a.reshape(Bn, T, H_M, DH_M).transpose(0, 2, 1, 3)

    i_pre = softcap(mi + b_gates[:H_M]).transpose(0, 2, 1)
    logf = jax.nn.log_sigmoid(softcap(mf + b_gates[H_M:])).transpose(0, 2, 1)
    hm, C, n, m = mlstm_chunkwise(heads_m(mq), heads_m(mk) * DH_M ** -0.5, heads_m(mv), i_pre, logf,
                                  C0.astype(jnp.float32), n0.astype(jnp.float32), m0.astype(jnp.float32))
    hm = rmsnorm(hm, g_head[:, None, :]).transpose(0, 2, 1, 3).reshape(Bn, T, W_M) * jax.nn.sigmoid(mo)

    q_s = rmsnorm(sq.reshape(Bn, T, H_S, DH_S), g_q)
    k_s = rmsnorm(sk.reshape(Bn, T, H_S, DH_S), g_k)
    v_s = sv.reshape(Bn, T, H_S, DH_S)
    if k_past is None:
        k_all, v_all = k_s, v_s
    else:
        k_all = jnp.concatenate([k_past.astype(jnp.float32), k_s], axis=1)
        v_all = jnp.concatenate([v_past.astype(jnp.float32), v_s], axis=1)
    hs = stick_breaking(q_s, k_all, v_all, sb_bias, q_offset).reshape(Bn, T, W_S)

    x = x + gate_a * (jnp.concatenate([hm, hs], axis=-1) @ w_out)

    hf = rmsnorm(x, g_ffn) * (1.0 + scale_f) + shift_f
    x = x + gate_f * peer(hf.reshape(Bn * T, D_MODEL), w_query, sub_keys_a, sub_keys_b,
                          expert_u, expert_v).reshape(Bn, T, D_MODEL)
    return x, k_s, v_s, C, n, m

def setup_inputs(seed: int = 0) -> dict:
    key = jax.random.key(seed)
    ks = jax.random.split(key, 32)
    n_pages = PAST_LEN // PAGE_SIZE
    n_pool = (DEC_BATCH * n_pages * 5 + 3) // 4
    nrm = jax.random.normal
    f32 = jnp.float32
    page_table = jax.random.permutation(ks[0], n_pool)[:DEC_BATCH * n_pages].reshape(DEC_BATCH, n_pages).astype(jnp.int32)
    f_bias = jnp.linspace(3.0, 6.0, H_M)[None, :] + 0.1 * nrm(ks[1], (DEPTH, H_M), f32)
    i_bias = 0.1 * nrm(ks[2], (DEPTH, H_M), f32)
    return {
        'x_prompt': nrm(ks[3], (BATCH, SEQ, D_MODEL), f32),
        'x_sample': nrm(ks[4], (DEC_BATCH, DEC_SEQ, D_MODEL), f32),
        'cache_sb_k': nrm(ks[5], (DEPTH, n_pool, PAGE_SIZE, H_S, DH_S), f32),
        'cache_sb_v': nrm(ks[6], (DEPTH, n_pool, PAGE_SIZE, H_S, DH_S), f32),
        'state_mlstm_C': 0.3 * nrm(ks[7], (DEPTH, DEC_BATCH, H_M, DH_M, DH_M), f32),
        'state_mlstm_n': 0.3 * nrm(ks[8], (DEPTH, DEC_BATCH, H_M, DH_M), f32),
        'state_mlstm_m': nrm(ks[9], (DEPTH, DEC_BATCH, H_M), f32),
        'page_table': page_table,
        'c_prompt': nrm(ks[10], (BATCH, D_MODEL), f32),
        'c_sample': nrm(ks[11], (DEC_BATCH, D_MODEL), f32),
        'w_ada': nrm(ks[12], (DEPTH, D_MODEL, 6 * D_MODEL), f32) * D_MODEL ** -0.5,
        'b_ada': 0.02 * nrm(ks[13], (DEPTH, 6 * D_MODEL), f32),
        'norm_mix_g': 1.0 + 0.02 * nrm(ks[14], (DEPTH, D_MODEL), f32),
        'norm_ffn_g': 1.0 + 0.02 * nrm(ks[15], (DEPTH, D_MODEL), f32),
        'w_in': nrm(ks[16], (DEPTH, D_MODEL, N_IN), f32) * D_MODEL ** -0.5,
        'b_gates': jnp.concatenate([i_bias, f_bias], axis=-1),
        'qnorm_g': 1.0 + 0.02 * nrm(ks[17], (DEPTH, H_S, DH_S), f32),
        'knorm_g': 1.0 + 0.02 * nrm(ks[18], (DEPTH, H_S, DH_S), f32),
        'sb_bias': SB_BIAS_INIT + 0.3 * nrm(ks[26], (DEPTH, H_S), f32),
        'mlstm_head_g': 1.0 + 0.02 * nrm(ks[19], (DEPTH, H_M, DH_M), f32),
        'w_out': nrm(ks[20], (DEPTH, D_MODEL, D_MODEL), f32) * D_MODEL ** -0.5,
        'w_query': nrm(ks[21], (DEPTH, D_MODEL, PEER_HEADS * PEER_DKEY), f32) * D_MODEL ** -0.5,
        'sub_keys_a': nrm(ks[22], (DEPTH, PEER_NKEYS, PEER_DKEY // 2), f32) * (PEER_DKEY // 2) ** -0.5,
        'sub_keys_b': nrm(ks[23], (DEPTH, PEER_NKEYS, PEER_DKEY // 2), f32) * (PEER_DKEY // 2) ** -0.5,
        'expert_u': nrm(ks[24], (DEPTH, PEER_NEXPERTS, D_MODEL), f32) * D_MODEL ** -0.5,
        'expert_v': 0.5 * nrm(ks[25], (DEPTH, PEER_NEXPERTS, D_MODEL), f32),
    }

def reference(x_prompt, x_sample, cache_sb_k, cache_sb_v, state_mlstm_C, state_mlstm_n, state_mlstm_m,
              page_table, c_prompt, c_sample, w_ada, b_ada, norm_mix_g, norm_ffn_g, w_in, b_gates,
              qnorm_g, knorm_g, sb_bias, mlstm_head_g, w_out, w_query, sub_keys_a, sub_keys_b, expert_u, expert_v):
    bp = x_prompt.shape[0]
    bs = x_sample.shape[0]
    past_len = page_table.shape[1] * cache_sb_k.shape[2]
    yp, ys = x_prompt, x_sample
    kp_l, vp_l, Cp_l, np_l, mp_l = [], [], [], [], []
    ks_l, vs_l, Cs_l, ns_l, ms_l = [], [], [], [], []
    for l in range(DEPTH):
        lw = (w_ada[l], b_ada[l], norm_mix_g[l], norm_ffn_g[l], w_in[l], b_gates[l], qnorm_g[l],
              knorm_g[l], sb_bias[l], mlstm_head_g[l], w_out[l], w_query[l], sub_keys_a[l], sub_keys_b[l],
              expert_u[l], expert_v[l])
        C0 = jnp.zeros((bp, H_M, DH_M, DH_M), jnp.float32)
        n0 = jnp.zeros((bp, H_M, DH_M), jnp.float32)
        m0 = jnp.zeros((bp, H_M), jnp.float32)
        yp, kp, vp, Cp, np_, mp = decoder_layer(yp, c_prompt, None, None, C0, n0, m0, 0, *lw)
        k_past = cache_sb_k[l][page_table].reshape(bs, past_len, H_S, DH_S)
        v_past = cache_sb_v[l][page_table].reshape(bs, past_len, H_S, DH_S)
        ys, ks_, vs_, Cs, ns, ms = decoder_layer(ys, c_sample, k_past, v_past, state_mlstm_C[l],
                                                 state_mlstm_n[l], state_mlstm_m[l], past_len, *lw)
        kp_l.append(kp.astype(cache_sb_k.dtype)); vp_l.append(vp.astype(cache_sb_v.dtype))
        Cp_l.append(Cp); np_l.append(np_); mp_l.append(mp)
        ks_l.append(ks_.astype(cache_sb_k.dtype)); vs_l.append(vs_.astype(cache_sb_v.dtype))
        Cs_l.append(Cs); ns_l.append(ns); ms_l.append(ms)
    y_prompt = yp.astype(x_prompt.dtype)
    y_sample = ys.astype(x_sample.dtype)
    k_prompt = jnp.stack(kp_l)
    v_prompt = jnp.stack(vp_l)
    C_prompt = jnp.stack(Cp_l)
    n_prompt = jnp.stack(np_l)
    m_prompt = jnp.stack(mp_l)
    k_sample = jnp.stack(ks_l)
    v_sample = jnp.stack(vs_l)
    C_sample = jnp.stack(Cs_l)
    n_sample = jnp.stack(ns_l)
    m_sample = jnp.stack(ms_l)
    return (y_prompt, y_sample, k_prompt, v_prompt, C_prompt, n_prompt, m_prompt,
            k_sample, v_sample, C_sample, n_sample, m_sample)


_drawn_inputs = setup_inputs


def setup_inputs(seed=0):
    import zlib

    import numpy as np

    out = dict(_drawn_inputs(seed))
    spreads = {}
    factors = {'qnorm_g': 25.63,
     'knorm_g': 8.989,
     'mlstm_head_g': 11.286,
     'norm_ffn_g': 3.171,
     'sb_bias': 3.842}
    for name, (base, spread) in spreads.items():
        noise = np.random.default_rng([zlib.crc32(name.encode()), seed]).standard_normal(out[name].shape)
        drawn = base * np.exp(spread * noise) if base else spread * noise
        out[name] = __import__('jax').numpy.asarray(drawn.astype(out[name].dtype))
    for name, factor in factors.items():
        out[name] = (out[name] * factor).astype(out[name].dtype)
    return out
```

```python
from contextlib import ExitStack

import numpy as np
import concourse.bass as bass
from concourse import mybir

ALU = mybir.AluOpType
ACT = mybir.ActivationFunctionType
AX = mybir.AxisListType
F32 = mybir.dt.float32
BF16 = mybir.dt.bfloat16
I32 = mybir.dt.int32
U32 = mybir.dt.uint32
ds = bass.ds

P = 128
D = 1024
KD = D // P
SEQ = 1024
NT = SEQ // P
NB = 8
SQ = 8
NS = NB * SQ
PAST = 1024
PAGE = 128
NPG = PAST // PAGE
HM, DM = 4, 128
HS, DS = 8, 64
WM, WS = HM * DM, HS * DS
NIN = 4 * WM + 2 * HM + 3 * WS
TT = SEQ + NS
CAP = 15.0
EPS = 1e-6
HIDE = -1e30
PH, NK, DK, TK = 8, 128, 128, 16
NE = NK * NK
KX = PH * TK
EXP_LN = "natural_log_exp_and_others"


class Signal:

    def __init__(self, sem, per=1, ahead=0):
        self.sem, self.per, self.ahead = sem, per, ahead

    def at(self, k, n=None):
        return k * self.per + ((self.per if n is None else n) + self.ahead * self.per)

    def ago(self, k, n=None):
        return k * self.per + (self.per if n is None else n)


def build(nc, io):
    ctx = ExitStack()
    with ctx:
        scopes = [(ctx, [])]

        def sem(name):
            scope, held = scopes[-1]
            held.append(scope.enter_context(nc.semaphore(name)))
            return held[-1]

        def pool_dma_sem(name):
            return ctx.enter_context(nc.semaphore(name))

        def phase(run, **kw):
            with ExitStack() as scope:
                scopes.append((scope, []))
                run(**kw)
                _, held = scopes.pop()
                with nc.Block() as block:
                    @block.sync
                    def _(sp):
                        for s in held:
                            sp.sem_clear(s)

        def signal(name, per=1, ahead=0):
            return Signal(sem(name), per, ahead)

        passed = {id(e): sem(f"passed_{n}") for n, e in
                  (("pe", nc.tensor), ("act", nc.scalar), ("dve", nc.vector), ("pool", nc.gpsimd), ("sp", nc.sync))}

        def reached(eng, sig, value):
            s = sig.sem if isinstance(sig, Signal) else sig
            eng.wait_ge(s, value)
            if not isinstance(value, int):
                eng.sem_inc(passed[id(eng)], 1)

        def prime(eng, *sigs):
            for s in sigs:
                eng.sem_inc(s.sem, s.ahead * s.per)

        def dram(name, shape, dt=F32):
            return nc.dram_tensor(name, shape, dt, kind="Internal").ap()

        mod_d = dram("mod_d", (1 + NB, 6 * D))
        mix_d = dram("mix_d", ((NT + 1) * P, 4 * WM))
        sq_d = dram("sq_d", ((NT + 1) * P, WS))
        x1_d = dram("x1_d", ((NT + 1) * P, D))

        shared = dict(nc=nc, pool_dma_sem=pool_dma_sem, io=io, sem=sem, signal=signal, reached=reached, prime=prime,
                      mod_d=mod_d, mix_d=mix_d, sq_d=sq_d, x1_d=x1_d)
        outer = ExitStack()
        with outer:
            def sbo(name, shape, dt=F32):
                return outer.enter_context(nc.sbuf_tensor(name, shape, dt))

            ident = sbo("ident", [P, P])
            gate_rows = sbo("gate_rows", [HM, 2, TT])
            sel_head = sbo("sel_head", [HM, HM, P])
            w_in_loaded = sem("w_in_loaded")
            shared.update(sel_head=sel_head, ident=ident, gate_rows=gate_rows, w_in_loaded=w_in_loaded)
            with nc.sbuf_tensor("w_in_sb", [P, KD, NIN], F32) as w_in_sb:
                shared.update(w_in_sb=w_in_sb)
                phase(modulation, **shared)
                phase(projection, **shared)
            with nc.sbuf_tensor("cols", [P, NT + 1, P], F32) as cols, \
                 nc.sbuf_tensor("bm_rows", [HM, TT], F32) as bm_rows, \
                 nc.sbuf_tensor("carry_all", [P, HM, NT + NB], F32) as carry_all:
                shared.update(cols=cols, bm_rows=bm_rows, carry_all=carry_all)
                phase(gates, **shared)
                phase(prompt_mix, **shared)
                with nc.sbuf_tensor("hcat_s", [P, D], F32) as hcat_s:
                    phase(sample_mlstm, hcat_s=hcat_s, **shared)
                    phase(sample_attention, hcat_s=hcat_s, **shared)
        phase(experts, **shared)


def modulation(nc, io, sem, pool_dma_sem, signal, reached, prime, mod_d, ident, w_in_sb, w_in_loaded, **_):
    NC_, CH = 6 * D // 512, 512
    NBUF = 3
    with ExitStack() as ctx:
        sb = lambda n, s, d=F32: ctx.enter_context(nc.sbuf_tensor(n, s, d))
        ps = lambda n, s, d=F32: ctx.enter_context(nc.psum_tensor(n, s, d))
        R = 1 + NB
        c_rows = sb("c_rows", [R, D])
        e_rows = sb("e_rows", [R, D])
        silu_c = sb("silu_c", [R, D])
        c_cols = sb("c_cols", [P, KD, R])
        w_ada = sb("w_ada", [P, NBUF, KD, CH])
        b_rows = sb("b_rows", [R, 2, CH])
        g_rows = sb("g_rows", [R, 2, CH])
        mod_rows = sb("mod_rows", [R, 2, CH])
        ps_c = ps("ps_c", [P, KD, 16])
        ps_m = ps("ps_m", [P, 2, CH])
        c_in, w_in = sem("c_in"), [sem(f"w_ada_in{i}") for i in range(NBUF)]
        b_in = [pool_dma_sem(f"b_ada_in{i}") for i in range(2)]
        ident_done, silu_step, c_turned, c_copied = sem("ident_done"), sem("silu_step"), sem("c_turned"), sem("c_copied")
        mod_summed, mod_added, mod_stored = sem("mod_summed"), sem("mod_added"), [pool_dma_sem(f"mod_stored{i}") for i in range(2)]

        gains = {2: io["norm_mix_g"], 3: io["norm_mix_g"], 8: io["norm_ffn_g"], 9: io["norm_ffn_g"]}
        block = ctx.enter_context(nc.Block())

        @block.sync
        def _(sp):
            sp.dma_start(c_rows[0:1, :], io["c_prompt"]).then_inc(c_in, 16)
            sp.dma_start(c_rows[1:R, :], io["c_sample"]).then_inc(c_in, 16)
            for n in range(NC_):
                if n >= NBUF:
                    sp.wait_ge(mod_summed, n - NBUF + 1)
                sp.dma_start(w_ada[:, n % NBUF], io["w_ada"][0, :, n * CH:(n + 1) * CH]
                             .rearrange("(k p) n -> p k n", p=P)).then_inc(w_in[n % NBUF], 16)
            sp.dma_start(w_in_sb[:, :, :], io["w_in"][0].rearrange("(k p) n -> p k n", p=P)).then_inc(w_in_loaded, 16)

        def store_mod(eng, n):
            eng.wait_ge(mod_added, n + 1)
            eng.dma_start(mod_d[:, n * CH:(n + 1) * CH], mod_rows[:, n % 2, :]).then_inc(mod_stored[n % 2], 16)

        @block.gpsimd
        def _(pool):
            pool.memset(ident[:, :], 0.0).then_inc(ident_done, 1)
            pool.wait_ge(ident_done, 1)
            pool.affine_select(out=ident[:, :], in_=ident[:, :], compare_op=ALU.not_equal, fill=1.0, base=0,
                               pattern=[[-1, P]], channel_multiplier=1).then_inc(ident_done, 1)
            for n in range(NC_):
                if n >= 2:
                    pool.wait_ge(mod_added, n - 1)
                bias = io["b_ada"][0:1, n * CH:(n + 1) * CH].broadcast_to([R, CH])
                pool.dma_start(b_rows[:, n % 2, :], bias).then_inc(b_in[n % 2], 16)
                if n in gains:
                    c0 = (n % 2) * CH
                    pool.dma_start(g_rows[:, n % 2, :], gains[n][0:1, c0:c0 + CH].broadcast_to([R, CH])).then_inc(b_in[n % 2], 16)
                if n >= 1:
                    store_mod(pool, n - 1)
            store_mod(pool, NC_ - 1)
            pool.wait_ge(mod_stored[0], 16 * NC_ // 2)
            pool.wait_ge(mod_stored[1], 16 * NC_ // 2)

        @block.scalar
        def _(act):
            act.preload_act_table_set(EXP_LN)
            act.wait_ge(silu_step, 1)
            act.activation(e_rows[:, :], silu_c[:, :], ACT.Exp, scale=-1.0).then_inc(silu_step, 1)

        @block.vector
        def _(dve):
            dve.wait_ge(c_in, 32)
            dve.tensor_scalar(silu_c[:, :], c_rows[:, :], -80.0, None, ALU.max).then_inc(silu_step, 1)
            dve.wait_ge(silu_step, 2)
            dve.tensor_scalar(e_rows[:, :], e_rows[:, :], 1.0, None, ALU.add)
            dve.drain()
            dve.reciprocal(e_rows[:, :], e_rows[:, :])
            dve.drain()
            dve.tensor_tensor(silu_c[:, :], c_rows[:, :], e_rows[:, :], ALU.mult).then_inc(silu_step, 1)
            dve.wait_ge(c_turned, 1)
            dve.tensor_copy(c_cols[:, :, :], ps_c[:, :, 0:R]).then_inc(c_copied, 1)
            rows_in = [0, 0]
            for n in range(NC_):
                rows_in[n % 2] += 16 + 16 * (n in gains)
                dve.wait_ge(b_in[n % 2], rows_in[n % 2])
                dve.wait_ge(mod_summed, n + 1)
                if n >= 2:
                    dve.wait_ge(mod_stored[n % 2], 16 * (n // 2))
                out = mod_rows[:, n % 2, :]
                ins = dve.tensor_tensor(out, ps_m[0:R, n % 2, :], b_rows[:, n % 2, :], ALU.add)
                if n in gains:
                    dve.drain()
                    ins = dve.scalar_tensor_tensor(out=out, in0=out, scalar=1.0, in1=g_rows[:, n % 2, :],
                                                   op0=ALU.add, op1=ALU.mult)
                ins.then_inc(mod_added, 1)

        @block.tensor
        def _(pe):
            pe.wait_ge(ident_done, 2)
            pe.wait_ge(silu_step, 3)
            for k in range(KD):
                t = pe.transpose(ps_c[:, k, 0:R], silu_c[:, k * P:(k + 1) * P], ident[0:R, 0:R])
            t.then_inc(c_turned, 1)
            pe.wait_ge(c_copied, 1)
            for n in range(NC_):
                pe.wait_ge(w_in[n % NBUF], 16 * (n // NBUF + 1))
                if n >= 2:
                    pe.wait_ge(mod_added, n - 1)
                for k in range(KD):
                    m = pe.matmul(ps_m[0:R, n % 2, :], c_cols[:, k, :], w_ada[:, n % NBUF, k, :], start=k == 0, stop=k == KD - 1)
                m.then_inc(mod_summed, 1)


def load_rows(eng, dst, mod_d, col, sample):
    if sample:
        src = mod_d[1:1 + NB, col:col + D].unsqueeze(1).broadcast_to([NB, SQ, D])
    else:
        src = mod_d[0:1, col:col + D].broadcast_to([P, D])
    return eng.dma_start(dst, src)


def projection(nc, io, sem, signal, reached, prime, mod_d, mix_d, sq_d, ident, w_in_sb, w_in_loaded, gate_rows, **_):
    with ExitStack() as ctx:
        sb = lambda n, s, d=F32: ctx.enter_context(nc.sbuf_tensor(n, s, d))
        ps = lambda n, s, d=F32: ctx.enter_context(nc.psum_tensor(n, s, d))
        x = sb("x", [P, D])
        gain, shift = sb("gain", [P, D]), sb("shift", [P, D])
        h = sb("h", [P, D])
        hT = sb("hT", [P, KD, P])
        stage = sb("stage", [P, 7, 512])
        sq_g, sk_g, hm_g = sb("sq_g", [P, WS]), sb("sk_g", [P, WS]), sb("hm_g", [P, WM])
        b_gate = sb("b_gate", [P, 2 * HM])
        square = sb("square", [P, 2, 512])
        og = sb("og", [P, 512])
        ssq, ssh = sb("ssq", [P, 1]), sb("ssh", [P, 2, HS])
        rstd, rsh = sb("rstd", [P, 1]), sb("rsh", [P, 2, HS])
        gt = sb("gt", [P, 4, 2 * HM])
        ps_t = ps("ps_t", [P, KD, P])
        ps_p = [ps(f"ps_p{i}", [P, 512]) for i in range(4)]
        ps_g = ps("ps_g", [P, 512])
        ps_r = ps("ps_r", [HM, 2, P])

        S0 = 4 * WM + 2 * HM
        starts = [S0, S0 + WS, S0 + 2 * WS, 0, WM, 2 * WM, 3 * WM]
        consts_in, mods_in = sem("consts_in"), sem("mods_in")
        x_in, x_free = signal("x_in", 16), signal("x_free", 1, 1)
        ssq_done, rstd_done, h_done = signal("ssq_done"), signal("rstd_done"), signal("h_done")
        h_turned, hT_act, hT_dve = signal("h_turned"), signal("hT_act"), signal("hT_dve")
        proj = signal("proj", 8, 1)
        read_act, read_dve = signal("read_act", 4, 1), signal("read_dve", 3, 1)
        gate_a, gate_v, gate_t, gate_c = signal("gate_a", 2), signal("gate_v", 3), signal("gate_t"), signal("gate_c")
        head_a, head_v = signal("head_a", 4), signal("head_v", 2)
        og_v, og_a = signal("og_v"), signal("og_a")
        staged_dve = signal("staged_dve", 3)
        stored = signal("stored", 16 * 7, 1)
        block = ctx.enter_context(nc.Block())

        @block.sync
        def _(sp):
            prime(sp, stored)
            for dst, src, w in ((sq_g, "qnorm_g", WS), (sk_g, "knorm_g", WS), (hm_g, "mlstm_head_g", WM)):
                sp.dma_start(dst[:, :], io[src].rearrange("a h d -> a (h d)").broadcast_to([P, w])).then_inc(consts_in, 16)
            sp.dma_start(b_gate[:, :], io["b_gates"].broadcast_to([P, 2 * HM])).then_inc(consts_in, 16)
            load_rows(sp, gain[:, :], mod_d, D, False).then_inc(mods_in, 16)
            load_rows(sp, shift[:, :], mod_d, 0, False).then_inc(mods_in, 16)

            def load(k, sample):
                reached(sp, x_free, x_free.ago(k))
                if sample:
                    load_rows(sp, gain[0:NS, :], mod_d, D, True).then_inc(mods_in, 16)
                    load_rows(sp, shift[0:NS, :], mod_d, 0, True).then_inc(mods_in, 16)
                    sp.dma_start(x[0:NS, :], io["x_sample"].rearrange("b q d -> (b q) d")).then_inc(x_in.sem, 16)
                else:
                    sp.dma_start(x[:, :], io["x_prompt"][0, ds(k * P, P), :]).then_inc(x_in.sem, 16)

            def store(k, sample):
                rows = NS if sample else P
                flat = lambda a: a.rearrange("a b t h d -> (a b t) (h d)")
                out_at, here = (ds(0, rows) if sample else ds(k * P, rows)), ds(k * P, rows)
                dst = [sq_d[here, :], flat(io["k_sample" if sample else "k_prompt"])[out_at, :],
                       flat(io["v_sample" if sample else "v_prompt"])[out_at, :]]
                dst += [mix_d[here, j * WM:(j + 1) * WM] for j in range(4)]
                for n, (sig, rise) in enumerate([(staged_dve, 1), (staged_dve, 2), (read_act, 1), (read_act, 2),
                                                 (read_act, 3), (read_act, 4), (staged_dve, 3)]):
                    reached(sp, sig, sig.at(k, rise))
                    sp.dma_start(dst[n], stage[0:rows, n, :]).then_inc(stored.sem, 16)

            load(0, False)
            with sp.Fori(0, NT - 1) as k:
                load(k + 1, False)
                store(k, False)
            load(NT, True)
            store(NT - 1, False)
            store(NT, True)
            sp.wait_ge(stored.sem, stored.at(NT))

        @block.tensor
        def _(pe):
            prime(pe, proj)
            pe.wait_ge(w_in_loaded, 16)

            def tile(k):
                reached(pe, h_done, h_done.at(k))
                for j in range(KD):
                    t = pe.transpose(ps_t[:, j, :], h[:, j * P:(j + 1) * P], ident[:, :])
                t.then_inc(h_turned.sem, 1)
                reached(pe, hT_act, hT_act.at(k))
                reached(pe, hT_dve, hT_dve.at(k))
                for j in range(KD):
                    m = pe.matmul(ps_g[:, 0:2 * HM], hT[:, j, :], w_in_sb[:, j, 4 * WM:4 * WM + 2 * HM], start=j == 0, stop=j == KD - 1)
                m.then_inc(proj.sem, 1)
                bank_free = [(read_act, read_act.ago(k, 3)), (read_act, read_act.ago(k, 4)),
                             (read_dve, read_dve.ago(k, 3)), (read_act, read_act.ago(k, 2)),
                             (read_dve, read_dve.at(k, 1)), (read_dve, read_dve.at(k, 2)), (read_act, read_act.at(k, 1))]
                for n, c0 in enumerate(starts):
                    reached(pe, *bank_free[n])
                    for j in range(KD):
                        m = pe.matmul(ps_p[n % 4][:, :], hT[:, j, :], w_in_sb[:, j, c0:c0 + 512], start=j == 0, stop=j == KD - 1)
                    m.then_inc(proj.sem, 1)
                    if n == 0:
                        reached(pe, gate_v, gate_v.at(k, 3))
                        for r in range(2):
                            t = pe.transpose(ps_r[:, r, :], gt[:, 3, r * HM:(r + 1) * HM], ident[:, :])
                        t.then_inc(gate_t.sem, 1)

            with pe.Fori(0, NT) as k:
                tile(k)
            tile(NT)

        @block.scalar
        def _(act):
            act.preload_act_table_set(EXP_LN)
            prime(act, read_act)

            def norm(k):
                reached(act, ssq_done, ssq_done.at(k))
                act.activation(rstd[:, :], ssq[:, :], ACT.Ln, scale=1.0 / D, bias=EPS)
                act.drain()
                act.activation(rstd[:, :], rstd[:, :], ACT.Exp, scale=-0.5).then_inc(rstd_done.sem, 1)

            def head_norm(k, w):
                reached(act, proj, proj.at(k, 2 + w))
                act.activation(square[:, w, :], ps_p[w][:, :], ACT.Square).then_inc(head_a.sem, 1)
                reached(act, head_v, head_v.at(k, w + 1))
                act.activation(rsh[:, w, :], ssh[:, w, :], ACT.Ln, scale=1.0 / DS, bias=EPS)
                act.drain()
                act.activation(rsh[:, w, :], rsh[:, w, :], ACT.Exp, scale=-0.5).then_inc(head_a.sem, 1)

            def tile(k, more):
                reached(act, h_turned, h_turned.at(k))
                reached(act, proj, proj.ago(k))
                act.activation(hT[:, 0:KD // 2, :], ps_t[:, 0:KD // 2, :], ACT.Copy).then_inc(hT_act.sem, 1)
                reached(act, gate_v, gate_v.at(k, 1))
                act.activation(gt[:, 1, :], gt[:, 0, :], ACT.Exp, scale=2.0 / CAP).then_inc(gate_a.sem, 1)
                reached(act, gate_v, gate_v.at(k, 2))
                act.activation(gt[:, 1, :], gt[:, 2, :], ACT.Exp, scale=-1.0)
                act.drain()
                act.activation(gt[:, 1, :], gt[:, 1, :], ACT.Ln, bias=1.0).then_inc(gate_a.sem, 1)
                head_norm(k, 0)
                head_norm(k, 1)
                if more:
                    norm(k + 1)
                reached(act, stored, stored.ago(k))
                for n in (2, 3, 4, 5):
                    reached(act, proj, proj.at(k, 2 + n))
                    scale = DM ** -0.5 if n == 4 else 1.0
                    act.activation(stage[:, n, :], ps_p[n % 4][:, :], ACT.Copy, scale=scale).then_inc(read_act.sem, 1)
                reached(act, og_v, og_v.at(k))
                act.activation(og[:, :], og[:, :], ACT.Exp, scale=-1.0).then_inc(og_a.sem, 1)

            norm(0)
            with act.Fori(0, NT) as k:
                tile(k, True)
            tile(NT, False)

        @block.vector
        def _(dve):
            prime(dve, x_free, read_dve)
            dve.wait_ge(consts_in, 64)

            def norm(k, mods):
                reached(dve, x_in, x_in.at(k))
                dve.wait_ge(mods_in, mods)
                dve.tensor_tensor_reduce(h[:, :], x[:, :], x[:, :], 1.0, 0.0, ALU.mult, ALU.add, ssq[:, :]).then_inc(ssq_done.sem, 1)
                reached(dve, rstd_done, rstd_done.at(k))
                dve.drain()
                dve.scalar_tensor_tensor(out=h[:, :], in0=x[:, :], scalar=rstd[:, 0:1], in1=gain[:, :], op0=ALU.mult, op1=ALU.mult)
                dve.drain()
                dve.tensor_tensor(h[:, :], h[:, :], shift[:, :], ALU.add).then_inc(h_done.sem, 1)
                dve.drain()
                dve.sem_inc(x_free.sem, 1)

            def head_norm(k, w, g):
                reached(dve, head_a, head_a.at(k, 2 * w + 1))
                dve.tensor_reduce(ssh[:, w, :], square[:, w, :].rearrange("p (h d) -> p h d", h=HS), AX.X, ALU.add).then_inc(head_v.sem, 1)
                reached(dve, head_a, head_a.at(k, 2 * w + 2))
                v = stage[:, w, :].rearrange("p (h d) -> p h d", h=HS)
                dve.tensor_tensor(v, ps_p[w][:, :].rearrange("p (h d) -> p h d", h=HS),
                                  rsh[:, w, :].unsqueeze(2).broadcast_to([P, HS, DS]), ALU.mult).then_inc(read_dve.sem, 1)
                dve.drain()
                dve.tensor_tensor(stage[:, w, :], stage[:, w, :], g[:, :], ALU.mult).then_inc(staged_dve.sem, 1)

            def tile(k, mods):
                reached(dve, h_turned, h_turned.at(k))
                reached(dve, proj, proj.ago(k))
                dve.tensor_copy(hT[:, KD // 2:KD, :], ps_t[:, KD // 2:KD, :]).then_inc(hT_dve.sem, 1)
                reached(dve, proj, proj.at(k, 1))
                dve.tensor_tensor(gt[:, 0, :], ps_g[:, 0:2 * HM], b_gate[:, :], ALU.add)
                dve.drain()
                dve.tensor_scalar(gt[:, 0, :], gt[:, 0, :], -30.0 * CAP, 30.0 * CAP, ALU.max, ALU.min).then_inc(gate_v.sem, 1)
                reached(dve, gate_a, gate_a.at(k, 1))
                dve.tensor_scalar(gt[:, 2, :], gt[:, 1, :], 1.0, None, ALU.add)
                dve.drain()
                dve.reciprocal(gt[:, 2, :], gt[:, 2, :])
                dve.drain()
                dve.tensor_scalar(gt[:, 2, :], gt[:, 2, :], -2.0 * CAP, CAP, ALU.mult, ALU.add).then_inc(gate_v.sem, 1)
                reached(dve, gate_a, gate_a.at(k, 2))
                dve.drain()
                dve.tensor_copy(gt[:, 3, 0:HM], gt[:, 2, 0:HM])
                dve.tensor_scalar(gt[:, 3, HM:2 * HM], gt[:, 1, HM:2 * HM], -1.0, None, ALU.mult)
                dve.drain()
                dve.sem_inc(gate_v.sem, 1)
                reached(dve, stored, stored.ago(k))
                head_norm(k, 0, sq_g)
                head_norm(k, 1, sk_g)
                reached(dve, gate_t, gate_t.at(k))
                width = P if mods else NS
                dve.tensor_copy(gate_rows[:, :, ds(k * P, width)], ps_r[:, :, 0:width]).then_inc(gate_c.sem, 1)
                if mods:
                    norm(k + 1, mods)
                reached(dve, proj, proj.at(k, 8))
                dve.tensor_scalar(og[:, :], ps_p[6 % 4][:, :], -80.0, None, ALU.max).then_inc(og_v.sem, 1)
                dve.drain()
                dve.sem_inc(read_dve.sem, 1)
                reached(dve, og_a, og_a.at(k))
                dve.tensor_scalar(og[:, :], og[:, :], 1.0, None, ALU.add)
                dve.drain()
                dve.reciprocal(og[:, :], og[:, :])
                dve.drain()
                dve.tensor_tensor(stage[:, 6, :], og[:, :], hm_g[:, :], ALU.mult).then_inc(staged_dve.sem, 1)
                dve.drain()

            norm(0, 32)
            with dve.Fori(0, NT - 1) as k:
                tile(k, 32)
            tile(NT - 1, 64)
            tile(NT, 0)


def gates(nc, io, sem, signal, reached, ident, gate_rows, cols, bm_rows, carry_all, sel_head, **_):
    NCH = NT + NB
    with ExitStack() as ctx:
        sb = lambda n, s, d=F32: ctx.enter_context(nc.sbuf_tensor(n, s, d))
        ps = lambda n, s, d=F32: ctx.enter_context(nc.psum_tensor(n, s, d))
        go_on = sb("go_on", [HM, TT])
        b_row, m_row = sb("b_row", [HM, TT]), sb("m_row", [HM, TT])
        m_start = sb("m_start", [HM, NB])
        m_before, bm_end, carry = sb("m_before", [HM, NCH]), sb("bm_end", [HM, NCH]), sb("carry", [HM, NCH])
        fi = sb("fi", [HM, 2, NS])
        kinds = sb("kinds", [P, TT])
        ps_k = [ps(f"ps_k{i}", [P, 4, P]) for i in range(3)]
        ps_y = ps("ps_y", [P, HM, NCH])
        ready, m_in, rows_out, sel_made = sem("g_ready"), sem("m_in"), sem("rows_out"), sem("sel_made")
        stepped, exped, turned, m_out = sem("g_stepped"), sem("g_exped"), sem("g_turned"), sem("m_out")
        prompt = lambda a: a[:, 0:SEQ].rearrange("p (c t) -> p c t", t=P)
        sample = lambda a: a[:, SEQ:TT].rearrange("p (c t) -> p c t", t=SQ)
        block = ctx.enter_context(nc.Block())

        @block.sync
        def _(sp):
            sp.dma_start(m_start[:, :], io["state_mlstm_m"].rearrange("a b h -> h (a b)"), allow_slow_non_contiguous=True).then_inc(m_in, 16)
            sp.wait_ge(stepped, 1)
            sp.dma_start(io["m_prompt"].rearrange("a b h -> h (a b)"), m_row[:, SEQ - 1:SEQ], allow_slow_non_contiguous=True).then_inc(m_out, 16)
            sp.dma_start(io["m_sample"].rearrange("a b h -> h (a b)"), sample(m_row)[:, :, SQ - 1], allow_slow_non_contiguous=True).then_inc(m_out, 16)
            sp.wait_ge(m_out, 32)

        @block.gpsimd
        def _(pool):
            pool.memset(sel_head[:, :, :], 0.0).then_inc(sel_made, 1)
            pool.wait_ge(sel_made, 1)
            pool.affine_select(out=sel_head[:, :, :], in_=sel_head[:, :, :], compare_op=ALU.not_equal, fill=1.0, base=0,
                               pattern=[[-1, HM], [0, P]], channel_multiplier=1).then_inc(sel_made, 1)

        @block.vector
        def _(dve):
            i_row, f_row = gate_rows[:, 0, :], gate_rows[:, 1, :]
            dve.memset(kinds[:, :], 0.0)
            dve.memset(go_on[:, :], 1.0)
            dve.memset(m_before[:, 0:1], 0.0)
            dve.drain()
            dve.memset(prompt(go_on)[:, :, 0], 0.0)
            dve.memset(sample(go_on)[:, :, 0], 0.0)
            dve.drain()
            dve.tensor_tensor_scan(b_row[:, :], go_on[:, :], f_row, 0.0, ALU.mult, ALU.add)
            dve.tensor_tensor_scan(m_row[:, 0:SEQ], f_row[:, 0:SEQ], i_row[:, 0:SEQ], 0.0, ALU.add, ALU.max)
            dve.tensor_copy(fi[:, :, :], gate_rows[:, :, SEQ:TT])
            dve.drain()
            dve.wait_ge(m_in, 16)
            first = lambda r: fi[:, r, :].rearrange("p (c t) -> p c t", t=SQ)[:, :, 0]
            dve.tensor_tensor(first(0), first(1), m_start[:, :], ALU.add)
            dve.drain()
            dve.tensor_tensor(first(0), first(0), sample(gate_rows[:, 0, :])[:, :, 0], ALU.max)
            dve.memset(first(1), HIDE)
            dve.drain()
            dve.tensor_tensor_scan(m_row[:, SEQ:TT], fi[:, 1, :], fi[:, 0, :], 0.0, ALU.add, ALU.max)
            dve.drain()
            dve.tensor_tensor(bm_rows[:, :], b_row[:, :], m_row[:, :], ALU.subtract).then_inc(stepped, 1)
            dve.tensor_tensor(kinds[0:HM, :], i_row, b_row[:, :], ALU.subtract)
            dve.tensor_copy(m_before[:, 1:NT], prompt(m_row)[:, 0:NT - 1, P - 1])
            dve.tensor_copy(m_before[:, NT:NCH], m_start[:, :])
            dve.drain()
            dve.tensor_copy(bm_end[:, 0:NT], prompt(bm_rows)[:, :, P - 1])
            dve.tensor_copy(bm_end[:, NT:NCH], sample(bm_rows)[:, :, SQ - 1])
            dve.drain()
            dve.tensor_tensor(carry[:, :], bm_end[:, :], m_before[:, :], ALU.add)
            for view, c0, c1, t in ((prompt, 0, NT, P), (sample, NT, NCH, SQ)):
                wide = lambda a: a[:, c0:c1].unsqueeze(2).broadcast_to([HM, c1 - c0, t])
                dve.tensor_tensor(view(kinds[32:32 + HM, :]), view(bm_rows), wide(m_before), ALU.add)
                dve.tensor_tensor(view(kinds[96:96 + HM, :]), view(kinds[0:HM, :]), wide(bm_end), ALU.add)
            dve.drain()
            dve.sem_inc(stepped, 1)
            dve.wait_ge(turned, 1)
            for n in range(3):
                w, r = (4, P) if n < 2 else (1, NS)
                dve.tensor_copy(cols[0:r, 4 * n:4 * n + w, :], ps_k[n][0:r, 0:w, :])
            dve.tensor_copy(carry_all[:, :, :], ps_y[:, :, :])

        @block.scalar
        def _(act):
            act.preload_act_table_set(EXP_LN)
            act.wait_ge(stepped, 2)
            act.activation(kinds[32:32 + HM, :], kinds[32:32 + HM, :], ACT.Exp)
            act.activation(kinds[64:64 + HM, :], m_row[:, :], ACT.Exp, scale=-1.0)
            act.activation(kinds[96:96 + HM, :], kinds[96:96 + HM, :], ACT.Exp)
            act.activation(carry[:, :], carry[:, :], ACT.Exp)
            act.drain()
            act.sem_inc(exped, 1)

        @block.tensor
        def _(pe):
            pe.wait_ge(exped, 1)
            pe.wait_ge(sel_made, 2)
            for n in range(NT + 1):
                w = P if n < NT else NS
                pe.transpose(ps_k[n // 4][0:w, n % 4, :], kinds[:, n * P:n * P + w], ident[:, :])
            for h in range(HM):
                t = pe.matmul(ps_y[:, h, :], sel_head[:, h, :], carry[:, :], start=True, stop=True)
            t.then_inc(turned, 1)


def prompt_mix(nc, io, sem, signal, reached, prime, mod_d, mix_d, sq_d, x1_d, ident, cols, bm_rows, carry_all,
               sel_head, **_):
    V1 = DM + 1
    with ExitStack() as ctx:
        sb = lambda n, s, d=F32: ctx.enter_context(nc.sbuf_tensor(n, s, d))
        ps = lambda n, s, d=F32: ctx.enter_context(nc.psum_tensor(n, s, d))
        w_out = sb("w_out_sb", [P, KD, D])
        gate_a = sb("gate_a_rows", [P, D])
        sb_bias = sb("sb_bias_sb", [P, HS])
        ident_h = sb("ident_h", [P, P], BF16)
        hide = sb("hide", [P, 2 * SEQ], BF16)
        after = sb("after", [P, P])
        KT = sb("KT", [P, HS // 2, SEQ])
        V = sb("V", [P, NT, WS])
        mx = sb("mx", [P, 4, WM])
        v1 = sb("v1", [P, HM, V1])
        vd = sb("vd", [P, HM, V1])
        sq = sb("sq", [P, WS])
        qkT = sb("qkT", [P, 2 * HM, P])
        QT = sb("QT", [P, HS // 2, P])
        colt, carry_t = sb("colt", [P, P]), sb("carry_t", [P, HM])
        wt, sw = sb("wt", [P, HM, P]), sb("sw", [P, HM, P])
        intra, num = sb("intra", [P, HM, V1]), sb("num", [P, HM, V1])
        Cn = sb("Cn", [P, HM, V1])
        den, ssq, fac = sb("den", [P, 2, HM]), sb("m_ssq", [P, HM]), sb("fac", [P, HM])
        junk = sb("junk", [P, P])
        lz, zb, cum = sb("lz", [P, SEQ]), sb("zb", [P, SEQ]), sb("cum", [P, SEQ])
        dd = sb("dd", [P, 2, SEQ])
        A, AT = sb("A", [P, SEQ]), sb("AT", [P, NT, P])
        hcat, hcT = sb("hcat", [P, D]), sb("hcT", [P, KD, P])
        xr = sb("xr", [P, D])
        one = sb("one", [P, 1])
        psZ, psA, psC = ps("psZ", [P, SEQ]), ps("psA", [P, SEQ]), ps("psC", [P, SEQ])
        psO, psE = ps("psO", [P, 512]), ps("psE", [P, 512])
        v1_of = lambda a, h: a[:, (h // 2) * 512 + (h % 2) * V1:(h // 2) * 512 + (h % 2) * V1 + V1]

        wo_in, const_in, kv_in = sem("wo_in"), sem("mix_const_in"), sem("kv_in")
        masks, k_turned, k_copied, zeroed = sem("masks"), sem("k_turned"), sem("k_copied"), sem("zeroed")
        mix_in, mix_free = signal("mix_in", 64), signal("mix_free", 1, 1)
        colt_set = signal("colt_set")
        t_qk, c_qk_a, c_qk_v = signal("t_qk"), signal("c_qk_a"), signal("c_qk_v")
        t_sq, c_sq = signal("t_sq"), signal("c_sq")
        bm_out, w_sum, w_exp = signal("bm_out"), signal("w_sum"), signal("w_exp")
        s_out, s_w = signal("s_out"), signal("s_w")
        intra_out, intra_copied, inter_out = signal("intra_out"), signal("intra_copied"), signal("inter_out")
        num_done, den_done, sq_done, rs_done = signal("num_done"), signal("den_done"), signal("sq_done"), signal("rs_done")
        hm_done, vd_done, up_out, state_done = signal("hm_done"), signal("vd_done"), signal("up_out"), signal("state_done", 1, 1)
        z_out, z_lin, l_done, l_used = (signal("z_out", HS), signal("z_lin", HS), signal("l_done", HS),
                                        signal("l_used", HS, 1))
        d_done, a_done, at_out, at_act, at_dve, av_out = (signal("d_done", HS), signal("a_done", HS), signal("at_out", HS),
                                                          signal("at_act", HS), signal("at_dve", HS), signal("av_out", HS))
        hs_done, t_hc, hc_act, hc_dve = signal("hs_done"), signal("t_hc"), signal("hc_act"), signal("hc_dve")
        y_out, x1_done, x1_stored = signal("y_out"), signal("x1_done", 1, 1), signal("x1_stored", 16, 1)
        c_turned, c_ready, state_stored = sem("C_turned"), sem("C_ready"), sem("state_stored")
        block = ctx.enter_context(nc.Block())
        flat = lambda a: a.rearrange("a b t h d -> (a b t) (h d)")

        @block.sync
        def _(sp):
            prime(sp, x1_stored)
            sp.dma_start(V[:, :, :], flat(io["v_prompt"]).rearrange("(j p) n -> p j n", p=P)).then_inc(kv_in, 16)
            for n, buf in enumerate((lz, zb, cum, A)):
                sp.dma_start(buf[:, :].rearrange("p (j n) -> p j n", j=2),
                             flat(io["k_prompt"])[n * 2 * P:(n + 1) * 2 * P, :].rearrange("(j p) n -> p j n", p=P)).then_inc(kv_in, 16)
            load_rows(sp, gate_a[:, :], mod_d, 2 * D, False).then_inc(const_in, 16)
            sp.dma_start(sb_bias[:, :], io["sb_bias"].broadcast_to([P, HS])).then_inc(const_in, 16)

            def load(k):
                reached(sp, mix_free, mix_free.ago(k))
                sp.dma_start(mx[:, :, :], mix_d[ds(k * P, P), :].rearrange("p (j n) -> p j n", j=4)).then_inc(mix_in.sem, 16)
                sp.dma_start(sq[:, :], sq_d[ds(k * P, P), :]).then_inc(mix_in.sem, 16)
                sp.dma_start(v1[:, :, 0:DM], mix_d[ds(k * P, P), 2 * WM:3 * WM].rearrange("p (h n) -> p h n", h=HM)).then_inc(mix_in.sem, 16)
                reached(sp, x1_stored, x1_stored.ago(k))
                sp.dma_start(xr[:, :], io["x_prompt"][0, ds(k * P, P), :]).then_inc(mix_in.sem, 16)

            def store(k):
                reached(sp, x1_done, x1_done.at(k))
                sp.dma_start(x1_d[ds(k * P, P), :], xr[:, :]).then_inc(x1_stored.sem, 16)

            sp.wait_ge(zeroed, 1)
            load(0)
            sp.dma_start(w_out[:, :, :], io["w_out"][0].rearrange("(k p) n -> p k n", p=P)).then_inc(wo_in, 16)
            with sp.Fori(0, NT - 1) as k:
                store(k)
                load(k + 1)
            store(NT - 1)
            sp.wait_ge(c_ready, 1)
            sp.dma_start(io["C_prompt"].rearrange("a b h v k -> v (a b h) k"), wt[:, :, :]).then_inc(state_stored, 16)
            sp.dma_start(io["n_prompt"].rearrange("a b h k -> k (a b h)"), Cn[:, :, DM], allow_slow_non_contiguous=True).then_inc(state_stored, 16)
            sp.wait_ge(state_stored, 32)
            sp.wait_ge(x1_stored.sem, x1_stored.at(NT - 1))

        @block.gpsimd
        def _(pool):
            pool.memset(hide[:, :], 0.0)
            pool.memset(after[:, :], 0.0)
            pool.memset(ident_h[:, :], 0.0).then_inc(masks, 1)
            pool.drain()
            pool.affine_select(out=hide[:, :], in_=hide[:, :], compare_op=ALU.is_gt, fill=HIDE, base=SEQ,
                               pattern=[[-1, 2 * SEQ]], channel_multiplier=1)
            pool.affine_select(out=after[:, :], in_=after[:, :], compare_op=ALU.is_ge, fill=HIDE, base=0,
                               pattern=[[1, P]], channel_multiplier=-1)
            pool.affine_select(out=ident_h[:, :], in_=ident_h[:, :], compare_op=ALU.not_equal, fill=1.0, base=0,
                               pattern=[[-1, P]], channel_multiplier=1)
            pool.drain()
            pool.sem_inc(masks, 1)

        @block.tensor
        def _(pe):
            pe.wait_ge(kv_in, 80)
            pe.wait_ge(masks, 2)
            banks = (psZ[:, 0:512], psZ[:, 512:1024], psA[:, 0:512], psA[:, 512:1024])
            n = 0
            for pair in range(HS // 2):
                for half in range(2):
                    if n >= 4:
                        pe.wait_ge(k_copied, n - 3)
                    for j in range(4):
                        t = half * 4 + j
                        buf = (lz, zb, cum, A)[t // 2]
                        c0 = (t % 2) * WS + pair * P
                        ins = pe.transpose(banks[n % 4][:, j * P:(j + 1) * P], buf[:, c0:c0 + P], ident[:, :])
                    ins.then_inc(k_turned, 1)
                    n += 1
            pe.wait_ge(k_copied, 8)
            pe.wait_ge(zeroed, 1)

            def mlstm(k):
                reached(pe, mix_in, mix_in.at(k))
                for j in range(2 * HM):
                    t = pe.transpose(psC[:, j * P:(j + 1) * P], mx[:, j // HM, (j % HM) * DM:(j % HM + 1) * DM], ident[:, :])
                t.then_inc(t_qk.sem, 1)
                for j in range(HS // 2):
                    t = pe.transpose(psE[:, j * P:(j + 1) * P], sq[:, j * P:(j + 1) * P], ident[:, :])
                t.then_inc(t_sq.sem, 1)
                reached(pe, c_sq, c_sq.at(k))
                for h in range(HM):
                    m = pe.matmul(psE[:, h * P:(h + 1) * P], sel_head[:, h, :], bm_rows[:, ds(k * P, P)], start=True, stop=True)
                m.then_inc(bm_out.sem, 1)
                reached(pe, c_qk_a, c_qk_a.at(k))
                reached(pe, c_qk_v, c_qk_v.at(k))
                reached(pe, state_done, state_done.ago(k))
                for h in range(HM):
                    m = pe.matmul(v1_of(psA, h), qkT[:, h, :], Cn[:, h, :], start=True, stop=True)
                m.then_inc(inter_out.sem, 1)
                reached(pe, w_sum, w_sum.at(k))
                for h in range(HM):
                    m = pe.matmul(psE[:, h * P:(h + 1) * P], qkT[:, HM + h, :], qkT[:, h, :], start=True, stop=True)
                m.then_inc(s_out.sem, 1)
                reached(pe, s_w, s_w.at(k))
                for h in range(HM):
                    m = pe.matmul(v1_of(psC, h), sw[:, h, :], v1[:, h, :], start=True, stop=True)
                m.then_inc(intra_out.sem, 1)
                reached(pe, intra_copied, intra_copied.at(k))
                reached(pe, vd_done, vd_done.at(k))
                for h in range(HM):
                    m = pe.matmul(v1_of(psC, h), mx[:, 1, h * DM:(h + 1) * DM], vd[:, h, :], start=True, stop=True)
                m.then_inc(up_out.sem, 1)

            def attention(k):
                for s in range(HS + 2):
                    if s < HS:
                        if s > 0:
                            reached(pe, z_lin, z_lin.at(k, s))
                        at = slice((s % 2) * DS, (s % 2 + 1) * DS)
                        for c in range(2):
                            zc = psZ[:, c * 512:(c + 1) * 512]
                            pe.matmul(zc, ident_h[:, :], hide[:, ds(SEQ - k * P + c * 512, 512)], start=True, stop=False)
                            m = pe.matmul(zc, QT[at, s // 2, :], KT[at, s // 2, c * 512:(c + 1) * 512], start=False, stop=True)
                        m.then_inc(z_out.sem, 1)
                    if 1 <= s <= HS:
                        if s == 1:
                            reached(pe, num_done, num_done.at(k))
                        else:
                            reached(pe, at_act, at_act.at(k, s - 1))
                            reached(pe, at_dve, at_dve.at(k, s - 1))
                        reached(pe, a_done, a_done.at(k, s))
                        for j in range(NT):
                            t = pe.transpose(psA[:, j * P:(j + 1) * P], A[:, j * P:(j + 1) * P], ident[:, :])
                        t.then_inc(at_out.sem, 1)
                    if s >= 2:
                        h = s - 2
                        reached(pe, at_act, at_act.at(k, h + 1))
                        reached(pe, at_dve, at_dve.at(k, h + 1))
                        for j in range(NT):
                            m = pe.matmul(psO[:, h * DS:(h + 1) * DS], AT[:, j, :], V[:, j, h * DS:(h + 1) * DS], start=j == 0, stop=j == NT - 1)
                        m.then_inc(av_out.sem, 1)

            def project(k):
                reached(pe, hm_done, hm_done.at(k))
                reached(pe, hs_done, hs_done.at(k))
                reached(pe, state_done, state_done.at(k))
                for j in range(KD):
                    t = pe.transpose(psC[:, j * P:(j + 1) * P], hcat[:, j * P:(j + 1) * P], ident[:, :])
                t.then_inc(t_hc.sem, 1)
                reached(pe, hc_act, hc_act.at(k))
                reached(pe, hc_dve, hc_dve.at(k))
                for c in range(2):
                    for j in range(KD):
                        m = pe.matmul(psZ[:, c * 512:(c + 1) * 512], hcT[:, j, :], w_out[:, j, c * 512:(c + 1) * 512], start=j == 0, stop=j == KD - 1)
                m.then_inc(y_out.sem, 1)
                reached(pe, x1_done, x1_done.at(k))

            def tile(k):
                mlstm(k)
                attention(k)
                project(k)

            pe.wait_ge(wo_in, 16)
            with pe.Fori(0, NT) as k:
                tile(k)
            for h in range(HM):
                t = pe.transpose(psE[:, h * P:(h + 1) * P], Cn[:, h, 0:DM], ident[:, :])
            t.then_inc(c_turned, 1)

        @block.scalar
        def _(act):
            act.preload_act_table_set(EXP_LN)
            act.wait_ge(const_in, 32)

            def mlstm(k):
                reached(act, t_qk, t_qk.at(k))
                act.activation(qkT[:, 0:HM, :], psC[:, 0:512].rearrange("p (h t) -> p h t", h=HM), ACT.Copy).then_inc(c_qk_a.sem, 1)
                reached(act, t_sq, t_sq.at(k))
                act.activation(QT[:, :, :], psE[:, :].rearrange("p (h t) -> p h t", h=HM), ACT.Copy).then_inc(c_sq.sem, 1)
                reached(act, w_sum, w_sum.at(k))
                act.activation(wt[:, :, :], wt[:, :, :], ACT.Exp).then_inc(w_exp.sem, 1)
                reached(act, intra_out, intra_out.at(k))
                for g in range(2):
                    c = act.activation(intra[:, 2 * g:2 * g + 2, :], psC[:, g * 512:g * 512 + 2 * V1].rearrange("p (h t) -> p h t", h=2), ACT.Copy)
                c.then_inc(intra_copied.sem, 1)
                reached(act, den_done, den_done.at(k))
                for h in range(HM):
                    act.activation(junk[:, :], num[:, h, 0:DM], ACT.Square, scale=den[:, 1, h:h + 1], accum_out=ssq[:, h:h + 1])
                    act.drain()
                act.activation(ssq[:, :], ssq[:, :], ACT.Ln, scale=1.0 / DM, bias=EPS)
                act.drain()
                act.activation(ssq[:, :], ssq[:, :], ACT.Exp, scale=-0.5).then_inc(rs_done.sem, 1)

            def attention(k):
                for s in range(HS + 2):
                    if s >= 2:
                        h = s - 2
                        reached(act, at_out, at_out.at(k, h + 1))
                        if h > 0:
                            reached(act, av_out, av_out.at(k, h))
                        act.activation(AT[:, 0:NT // 2, :], psA[:, 0:512].rearrange("p (j t) -> p j t", t=P), ACT.Copy).then_inc(at_act.sem, 1)
                    if 1 <= s <= HS:
                        reached(act, d_done, d_done.at(k, s))
                        act.activation(A[:, :], dd[:, (s - 1) % 2, :], ACT.Exp).then_inc(a_done.sem, 1)
                    if s < HS:
                        reached(act, z_lin, z_lin.at(k, s + 1))
                        reached(act, l_used, l_used.at(k, s + 1) - 1)
                        act.activation(lz[:, :], zb[:, :], ACT.Abs)
                        act.drain()
                        act.activation(lz[:, :], lz[:, :], ACT.Exp, scale=-1.0)
                        act.drain()
                        act.activation(lz[:, :], lz[:, :], ACT.Ln, bias=1.0).then_inc(l_done.sem, 1)

            def project(k):
                reached(act, av_out, av_out.at(k))
                act.activation(hcat[:, WM:D], psO[:, :], ACT.Copy).then_inc(hs_done.sem, 1)
                reached(act, t_hc, t_hc.at(k))
                act.activation(hcT[:, 0:KD // 2, :], psC[:, 0:512].rearrange("p (j t) -> p j t", t=P), ACT.Copy).then_inc(hc_act.sem, 1)

            def tile(k):
                mlstm(k)
                attention(k)
                project(k)

            with act.Fori(0, NT) as k:
                tile(k)
            act.wait_ge(c_turned, 1)
            act.activation(wt[:, :, :], psE[:, :].rearrange("p (h t) -> p h t", h=HM), ACT.Copy).then_inc(c_ready, 1)

        @block.vector
        def _(dve):
            prime(dve, mix_free, l_used, x1_done, state_done)
            for n in range(8):
                dve.wait_ge(k_turned, n + 1)
                bank = (psZ[:, 0:512], psZ[:, 512:1024], psA[:, 0:512], psA[:, 512:1024])[n % 4]
                dve.tensor_copy(KT[:, n // 2, (n % 2) * 512:(n % 2 + 1) * 512], bank).then_inc(k_copied, 1)
            dve.memset(Cn[:, :, :], 0.0)
            dve.memset(v1[:, :, :], 1.0)
            dve.drain()
            dve.sem_inc(zeroed, 1)
            dve.wait_ge(const_in, 32)

            def mlstm(k):
                dve.tensor_copy(colt[:, :], cols[:, ds(k, 1), :].rearrange("p a n -> p (a n)"))
                dve.tensor_copy(carry_t[:, :], carry_all[:, :, ds(k, 1)].rearrange("p h a -> p (h a)"))
                reached(dve, mix_in, mix_in.at(k))
                dve.drain()
                for h in range(HM):
                    v = dve.tensor_scalar(vd[:, h, :], v1[:, h, :], colt[:, 96 + h:97 + h], None, ALU.mult)
                v.then_inc(vd_done.sem, 1)
                reached(dve, t_qk, t_qk.at(k))
                dve.tensor_copy(qkT[:, HM:2 * HM, :], psC[:, 512:1024].rearrange("p (h t) -> p h t", h=HM)).then_inc(c_qk_v.sem, 1)
                reached(dve, bm_out, bm_out.at(k))
                for h in range(HM):
                    w = dve.scalar_tensor_tensor(out=wt[:, h, :], in0=psE[:, h * P:(h + 1) * P], scalar=colt[:, h:h + 1],
                                                 in1=after[:, :], op0=ALU.add, op1=ALU.add)
                w.then_inc(w_sum.sem, 1)
                reached(dve, s_out, s_out.at(k))
                reached(dve, w_exp, w_exp.at(k))
                dve.tensor_tensor(sw[:, :, :], wt[:, :, :], psE[:, :].rearrange("p (h t) -> p h t", h=HM), ALU.mult).then_inc(s_w.sem, 1)
                reached(dve, inter_out, inter_out.at(k))
                reached(dve, intra_copied, intra_copied.at(k))
                for h in range(HM):
                    dve.scalar_tensor_tensor(out=num[:, h, :], in0=v1_of(psA, h), scalar=colt[:, 32 + h:33 + h],
                                             in1=intra[:, h, :], op0=ALU.mult, op1=ALU.add)
                dve.drain()
                dve.sem_inc(num_done.sem, 1)
                dve.tensor_scalar(den[:, 0, :], num[:, :, DM], -1.0, None, ALU.mult)
                dve.drain()
                dve.tensor_tensor(den[:, 0, :], den[:, 0, :], num[:, :, DM], ALU.max)
                dve.drain()
                dve.tensor_tensor(den[:, 0, :], den[:, 0, :], colt[:, 64:64 + HM], ALU.max)
                dve.drain()
                dve.reciprocal(den[:, 1, :], den[:, 0, :]).then_inc(den_done.sem, 1)
                reached(dve, up_out, up_out.at(k))
                for h in range(HM):
                    dve.scalar_tensor_tensor(out=Cn[:, h, :], in0=Cn[:, h, :], scalar=carry_t[:, h:h + 1],
                                             in1=v1_of(psC, h), op0=ALU.mult, op1=ALU.add)
                dve.drain()
                dve.sem_inc(state_done.sem, 1)
                reached(dve, rs_done, rs_done.at(k))
                dve.tensor_tensor(fac[:, :], ssq[:, :], den[:, 1, :], ALU.mult)
                dve.drain()
                for h in range(HM):
                    dve.scalar_tensor_tensor(out=hcat[:, h * DM:(h + 1) * DM], in0=num[:, h, 0:DM], scalar=fac[:, h:h + 1],
                                             in1=mx[:, 3, h * DM:(h + 1) * DM], op0=ALU.mult, op1=ALU.mult)
                dve.drain()
                dve.sem_inc(hm_done.sem, 1)
                dve.sem_inc(mix_free.sem, 1)

            def attention(k):
                for s in range(HS + 2):
                    if s < HS:
                        reached(dve, z_out, z_out.at(k, s + 1))
                        dve.tensor_scalar(zb[:, :], psZ[:, :], DS ** -0.5, sb_bias[:, s:s + 1], ALU.mult, ALU.add).then_inc(z_lin.sem, 1)
                    if s >= 2:
                        h = s - 2
                        reached(dve, at_out, at_out.at(k, h + 1))
                        if h > 0:
                            reached(dve, av_out, av_out.at(k, h))
                        dve.tensor_copy(AT[:, NT // 2:NT, :], psA[:, 512:1024].rearrange("p (j t) -> p j t", t=P)).then_inc(at_dve.sem, 1)
                    if s < HS:
                        reached(dve, l_done, l_done.at(k, s + 1))
                        dve.drain()
                        dve.scalar_tensor_tensor(out=cum[:, :], in0=zb[:, :], scalar=0.0, in1=lz[:, :], op0=ALU.max, op1=ALU.add).then_inc(l_used.sem, 1)
                        dve.drain()
                        back = cum[:, ::-1]
                        dve.tensor_tensor_scan(back, one[:, 0:1].broadcast_to([P, SEQ]), back, 0.0, ALU.mult, ALU.add)
                        dve.drain()
                        if s >= 2:
                            reached(dve, a_done, a_done.at(k, s - 1))
                        dve.tensor_tensor(dd[:, s % 2, :], zb[:, :], cum[:, :], ALU.subtract).then_inc(d_done.sem, 1)
                        dve.drain()

            def project(k):
                reached(dve, t_hc, t_hc.at(k))
                dve.tensor_copy(hcT[:, KD // 2:KD, :], psC[:, 512:1024].rearrange("p (j t) -> p j t", t=P)).then_inc(hc_dve.sem, 1)
                reached(dve, y_out, y_out.at(k))
                dve.tensor_tensor(zb[:, :], psZ[:, :], gate_a[:, :], ALU.mult)
                dve.drain()
                dve.tensor_tensor(xr[:, :], zb[:, :], xr[:, :], ALU.add).then_inc(x1_done.sem, 1)
                dve.drain()

            def tile(k):
                mlstm(k)
                attention(k)
                project(k)

            dve.memset(one[:, :], 1.0)
            with dve.Fori(0, NT) as k:
                tile(k)


def sample_mlstm(nc, io, sem, signal, reached, mix_d, ident, cols, bm_rows, carry_all, sel_head, hcat_s, **_):
    V1, NBH = DM + 1, NB * HM
    with ExitStack() as ctx:
        sb = lambda n, s, d=F32: ctx.enter_context(nc.sbuf_tensor(n, s, d))
        ps = lambda n, s, d=F32: ctx.enter_context(nc.psum_tensor(n, s, d))
        mx = sb("s_mx", [NS, 4, WM])
        v1, vd = sb("s_v1", [NS, HM, V1]), sb("s_vd", [NS, HM, DM])
        vdm = sb("s_vdm", [NS, NB, HM, DM])
        dec = sb("s_dec", [NS, HM, NB])
        qkT = sb("s_qkT", [P, 2 * HM, NS])
        qm = sb("s_qm", [P, HM, NB, NS])
        C = sb("s_C", [P, NBH, DM])
        CT = sb("s_CT", [P, NBH, V1])
        n_in, n_new, n_rows = sb("s_n", [NBH, DM]), sb("s_nn", [P, NB, HM]), sb("s_nr", [NBH, DM])
        own = sb("s_own", [P, NB, NS])
        own_row = sb("s_own_row", [NS, NB])
        see = sb("s_see", [NS, NS])
        wt, sw = sb("s_wt", [NS, HM, NS]), sb("s_sw", [NS, HM, NS])
        intra, num = sb("s_intra", [NS, HM, V1]), sb("s_num", [NS, HM, V1])
        den, ssq, fac, junk = sb("s_den", [NS, 2, HM]), sb("s_ssq", [NS, HM]), sb("s_fac", [NS, HM]), sb("s_junk", [NS, P])
        psQ, psN, psE = ps("s_psQ", [P, 2 * HM, NS]), ps("s_psN", [P, NBH]), ps("s_psE", [P, 512])
        psI, psS = ps("s_psI", [P, 1024]), [ps(f"s_psS{i}", [P, 4, P]) for i in range(2)]
        v1_of = lambda a, h: a[0:NS, (h // 2) * 512 + (h % 2) * V1:(h // 2) * 512 + (h % 2) * V1 + V1]
        loaded, ones_set, masks = sem("s_loaded"), sem("s_ones"), sem("s_masks")
        pe_d, act_d, dve_d = sem("s_pe_done"), sem("s_act_done"), sem("s_dve_done")
        ct_t, ct_c, up_m, up_c, kept = sem("s_ct_t"), sem("s_ct_c"), sem("s_up_m"), sem("s_up_c"), sem("s_kept")
        here = slice(SEQ, SEQ + NS)
        block = ctx.enter_context(nc.Block())

        @block.sync
        def _(sp):
            sp.dma_start(mx[:, :, :], mix_d[here, :].rearrange("p (j n) -> p j n", j=4)).then_inc(loaded, 16)
            sp.dma_start(n_in[:, :], io["state_mlstm_n"].rearrange("a b h k -> (a b h) k")).then_inc(loaded, 16)
            sp.dma_start(C[:, :, :], io["state_mlstm_C"].rearrange("a b h v k -> v (a b h) k")).then_inc(loaded, 16)
            sp.wait_ge(ones_set, 1)
            sp.dma_start(v1[:, :, 0:DM], mix_d[here, 2 * WM:3 * WM].rearrange("p (h n) -> p h n", h=HM)).then_inc(loaded, 16)
            sp.wait_ge(up_c, NB)
            sp.dma_start(io["C_sample"].rearrange("a b h v k -> v (a b h) k"), C[:, :, :]).then_inc(kept, 16)
            sp.wait_ge(act_d, 6)
            sp.dma_start(io["n_sample"].rearrange("a b h k -> (a b h) k"), n_rows[:, :]).then_inc(kept, 16)
            sp.wait_ge(kept, 32)

        @block.gpsimd
        def _(pool):
            pool.memset(own[:, :, :], 1.0)
            pool.memset(own_row[:, :], 1.0)
            pool.memset(see[:, :], 0.0)
            pool.drain()

            def keep(a, pattern, base, cm, fill):
                pool.affine_select(out=a, in_=a, compare_op=ALU.is_ge, fill=fill, base=base, pattern=pattern, channel_multiplier=cm)
                pool.drain()
            keep(own[:, :, :], [[-SQ, NB], [1, NS]], 0, 0, 0.0)
            keep(own[:, :, :], [[SQ, NB], [-1, NS]], SQ - 1, 0, 0.0)
            keep(own_row[:, :], [[-SQ, NB]], 0, 1, 0.0)
            keep(own_row[:, :], [[SQ, NB]], SQ - 1, -1, 0.0)
            see3 = see[:, :].rearrange("p (b q) -> p b q", q=SQ)
            keep(see3, [[-SQ, NB], [0, SQ]], 0, 1, HIDE)
            keep(see3, [[SQ, NB], [0, SQ]], SQ - 1, -1, HIDE)
            keep(see3, [[SQ, NB], [1, SQ]], 0, -1, HIDE)
            pool.sem_inc(masks, 1)

        @block.tensor
        def _(pe):
            pe.wait_ge(loaded, 64)
            for j in range(2 * HM):
                t = pe.transpose(psQ[:, j, :], mx[:, j // HM, (j % HM) * DM:(j % HM + 1) * DM], ident[0:NS, 0:NS])
            t.then_inc(pe_d, 1)
            pe.transpose(psN[:, :], n_in[:, :], ident[0:NBH, 0:NBH]).then_inc(pe_d, 1)
            for h in range(HM):
                m = pe.matmul(psE[0:NS, h * NS:(h + 1) * NS], sel_head[:, h, 0:NS], bm_rows[:, SEQ:TT], start=True, stop=True)
            m.then_inc(pe_d, 1)
            for b in range(NB):
                if b >= 2:
                    pe.wait_ge(ct_c, b - 1)
                for h in range(HM):
                    t = pe.transpose(psS[b % 2][:, h, :], C[:, b * HM + h, :], ident[:, :])
                t.then_inc(ct_t, 1)
            pe.wait_ge(act_d, 1)
            pe.wait_ge(dve_d, 1)
            for h in range(HM):
                m = pe.matmul(psE[0:NS, h * NS:(h + 1) * NS], qkT[:, HM + h, :], qkT[:, h, :], start=True, stop=True)
            m.then_inc(pe_d, 1)
            pe.wait_ge(ct_c, NB + 1)
            pe.wait_ge(dve_d, 2)
            for h in range(HM):
                for b in range(NB):
                    m = pe.matmul(v1_of(psI, h), qm[:, h, b, :], CT[:, b * HM + h, :], start=b == 0, stop=b == NB - 1)
            m.then_inc(pe_d, 1)
            pe.wait_ge(dve_d, 4)
            for h in range(HM):
                m = pe.matmul(psS[h // 2][0:NS, :, :].rearrange("p j t -> p (j t)")[:, (h % 2) * V1:(h % 2 + 1) * V1],
                              sw[:, h, :], v1[:, h, :], start=True, stop=True)
            m.then_inc(pe_d, 1)
            pe.wait_ge(dve_d, 3)
            for h in range(HM):
                m = pe.matmul(psN[:, h * NB:(h + 1) * NB], mx[:, 1, h * DM:(h + 1) * DM], dec[:, h, :], start=True, stop=True)
            m.then_inc(pe_d, 1)
            pe.wait_ge(act_d, 3)
            for b in range(NB):
                if b >= 2:
                    pe.wait_ge(up_c, b - 1)
                for h in range(HM):
                    m = pe.matmul(psS[b % 2][:, h, :], vdm[:, b, h, :], mx[:, 1, h * DM:(h + 1) * DM], start=True, stop=True)
                m.then_inc(up_m, 1)
            pe.wait_ge(dve_d, 6)
            pe.transpose(psE[0:NBH, 0:P], n_new[:, :, :].rearrange("p b h -> p (b h)"), ident[:, :]).then_inc(pe_d, 1)

        @block.scalar
        def _(act):
            act.preload_act_table_set(EXP_LN)
            act.wait_ge(pe_d, 1)
            act.activation(qkT[:, :, :], psQ[:, :, :], ACT.Copy).then_inc(act_d, 1)
            act.wait_ge(dve_d, 1)
            act.activation(wt[:, :, :], wt[:, :, :], ACT.Exp).then_inc(act_d, 1)
            act.wait_ge(pe_d, 6)
            for g in range(2):
                act.activation(intra[:, 2 * g:2 * g + 2, :], psS[g][0:NS, :, :].rearrange("p j t -> p (j t)")[:, 0:2 * V1]
                               .rearrange("p (h t) -> p h t", h=2), ACT.Copy)
            act.drain()
            act.sem_inc(act_d, 1)
            act.wait_ge(dve_d, 5)
            for h in range(HM):
                act.activation(junk[:, :], num[:, h, 0:DM], ACT.Square, scale=den[:, 1, h:h + 1], accum_out=ssq[:, h:h + 1])
                act.drain()
            act.activation(ssq[:, :], ssq[:, :], ACT.Ln, scale=1.0 / DM, bias=EPS)
            act.drain()
            act.activation(ssq[:, :], ssq[:, :], ACT.Exp, scale=-0.5).then_inc(act_d, 2)
            act.wait_ge(pe_d, 8)
            act.activation(n_rows[:, :], psE[0:NBH, 0:P], ACT.Copy).then_inc(act_d, 1)

        @block.vector
        def _(dve):
            dve.memset(v1[:, :, :], 1.0)
            dve.drain()
            dve.sem_inc(ones_set, 1)
            dve.wait_ge(loaded, 64)
            dve.wait_ge(masks, 1)
            dve.wait_ge(pe_d, 3)
            col = cols[0:NS, NT, :]
            for h in range(HM):
                dve.scalar_tensor_tensor(out=wt[:, h, :], in0=psE[0:NS, h * NS:(h + 1) * NS], scalar=col[:, h:h + 1],
                                         in1=see[:, :], op0=ALU.add, op1=ALU.add)
            dve.drain()
            dve.sem_inc(dve_d, 1)
            dve.tensor_copy(CT[:, :, DM], psN[:, :])
            for b in range(NB):
                dve.wait_ge(ct_t, b + 1)
                dve.tensor_copy(CT[:, b * HM:(b + 1) * HM, 0:DM], psS[b % 2][:, :, :]).then_inc(ct_c, 1)
            dve.drain()
            dve.sem_inc(ct_c, 1)
            dve.wait_ge(act_d, 1)
            for h in range(HM):
                dve.tensor_tensor(qm[:, h, :, :], qkT[:, h:h + 1, :].broadcast_to([P, NB, NS]), own[:, :, :], ALU.mult)
            dve.drain()
            dve.sem_inc(dve_d, 1)
            for h in range(HM):
                dve.tensor_scalar(vd[:, h, :], v1[:, h, 0:DM], col[:, 96 + h:97 + h], None, ALU.mult)
                dve.tensor_scalar(dec[:, h, :], own_row[:, :], col[:, 96 + h:97 + h], None, ALU.mult)
            dve.drain()
            for b in range(NB):
                dve.tensor_scalar(vdm[:, b, :, :], vd[:, :, :], own_row[:, b:b + 1], None, ALU.mult)
            dve.drain()
            dve.sem_inc(dve_d, 1)
            dve.wait_ge(act_d, 2)
            dve.wait_ge(pe_d, 4)
            dve.tensor_tensor(sw[:, :, :], wt[:, :, :], psE[0:NS, 0:HM * NS].rearrange("p (h t) -> p h t", h=HM), ALU.mult).then_inc(dve_d, 1)
            dve.wait_ge(act_d, 3)
            dve.wait_ge(pe_d, 5)
            for h in range(HM):
                dve.scalar_tensor_tensor(out=num[:, h, :], in0=v1_of(psI, h), scalar=col[:, 32 + h:33 + h],
                                         in1=intra[:, h, :], op0=ALU.mult, op1=ALU.add)
            dve.drain()
            dve.tensor_scalar(den[:, 0, :], num[:, :, DM], -1.0, None, ALU.mult)
            dve.drain()
            dve.tensor_tensor(den[:, 0, :], den[:, 0, :], num[:, :, DM], ALU.max)
            dve.drain()
            dve.tensor_tensor(den[:, 0, :], den[:, 0, :], col[:, 64:64 + HM], ALU.max)
            dve.drain()
            dve.reciprocal(den[:, 1, :], den[:, 0, :]).then_inc(dve_d, 1)
            keep = carry_all[:, :, NT:NT + NB].rearrange("p h b -> p b h")
            dve.wait_ge(pe_d, 7)
            dve.tensor_tensor(n_new[:, :, :], CT[:, :, DM].rearrange("p (b h) -> p b h", h=HM), keep, ALU.mult)
            dve.drain()
            dve.tensor_tensor(n_new[:, :, :], n_new[:, :, :], psN[:, :].rearrange("p (h b) -> p b h", b=NB), ALU.add).then_inc(dve_d, 1)
            for b in range(NB):
                dve.wait_ge(up_m, b + 1)
                for h in range(HM):
                    dve.scalar_tensor_tensor(out=C[:, b * HM + h, :], in0=C[:, b * HM + h, :],
                                             scalar=carry_all[:, h, NT + b:NT + b + 1], in1=psS[b % 2][:, h, :], op0=ALU.mult, op1=ALU.add)
                dve.drain()
                dve.sem_inc(up_c, 1)
            dve.wait_ge(act_d, 5)
            dve.tensor_tensor(fac[:, :], ssq[:, :], den[:, 1, :], ALU.mult)
            dve.drain()
            for h in range(HM):
                dve.scalar_tensor_tensor(out=hcat_s[0:NS, h * DM:(h + 1) * DM], in0=num[:, h, 0:DM], scalar=fac[:, h:h + 1],
                                         in1=mx[:, 3, h * DM:(h + 1) * DM], op0=ALU.mult, op1=ALU.mult)


def sample_attention(nc, io, sem, pool_dma_sem, signal, reached, prime, mod_d, sq_d, x1_d, ident, hcat_s, **_):
    G, TK_ = NB // 2, PAST + SQ
    with ExitStack() as ctx:
        sb = lambda n, s, d=F32: ctx.enter_context(nc.sbuf_tensor(n, s, d))
        ps = lambda n, s, d=F32: ctx.enter_context(nc.psum_tensor(n, s, d))
        w_out = sb("a_w_out", [P, KD, D])
        gate_a = sb("a_gate", [NS, D])
        xr = sb("a_x", [NS, D])
        Kp, Vp = sb("a_K", [P, 2, NPG, WS]), sb("a_V", [P, 2, NPG, WS])
        Vn = sb("a_Vn", [SQ, 2, WS])
        KT = sb("a_KT", [P, 4, 2, TK_])
        qn, kn = sb("a_qn", [NS, WS]), sb("a_kn", [NS, WS])
        QT, KnT = sb("a_QT", [P, 4, NS]), sb("a_KnT", [P, 4, NS])
        Q0 = sb("a_Q0", [P, 4, 2, P])
        pick = sb("a_pick", [P, 4, 2, 16])
        own = sb("a_own", [P, 16])
        fold4, fold = sb("a_fold4", [P, 2, SQ, HS]), sb("a_fold", [P, 2, SQ])
        vis, hide_f, hide = sb("a_vis", [P, SQ, 16]), sb("a_hide_f", [P, SQ]), sb("a_hide", [P, SQ], BF16)
        ident_h = sb("a_ident_h", [P, P], BF16)
        bias = sb("a_bias", [P, 1])
        one = sb("a_one", [P, 1])
        table, table_f = sb("a_table", [P, NB * NPG], I32), sb("a_table_f", [P, NB * NPG])
        lane, lane_f = sb("a_lane", [P, 1], I32), sb("a_lane_f", [P, 1])
        rows, rows_g = sb("a_rows", [P, NB * NPG], I32), sb("a_rows_g", [P, 2 * NPG], I32)
        zb, lz, cum = sb("a_zb", [P, TK_]), sb("a_lz", [P, TK_]), sb("a_cum", [P, TK_])
        A = sb("a_A", [P, TK_])
        AT, ATn = sb("a_AT", [P, NPG, P]), sb("a_ATn", [SQ, P])
        mo = sb("a_mo", [P, 2, WS])
        hs = sb("a_hs", [16, WS])
        hcT = sb("a_hcT", [P, KD, NS])
        psZ, psT = ps("a_psZ", [P, 3 * 512]), [ps(f"a_psT{i}", [P, 512]) for i in range(2)]
        psO, psX = ps("a_psO", [P, 2, 512]), ps("a_psX", [P, 512])
        const_in, own_in, wo_in, set_up, folded = sem("a_const"), sem("a_own_in"), sem("a_wo"), sem("a_setup"), sem("a_folded")
        idx_done, rows_set = sem("a_idx"), signal("a_rows_set")
        k_in, v_in = (Signal(pool_dma_sem(n), 16 * 2 * NPG) for n in ("a_k_in", "a_v_in"))
        vn_in = signal("a_vn_in", 16)
        free = signal("a_free", 1, 1)
        qk_t, qk_c = sem("a_qk_t"), sem("a_qk_c")
        q0_set, k_t, k_ca, k_cv = signal("a_q0"), signal("a_k_t", 16), signal("a_k_ca", 8), signal("a_k_cv", 8)
        z_out, z_lin, l_done, d_done, a_done = (signal(n) for n in ("a_z", "a_zl", "a_l", "a_d", "a_a"))
        at_t, at_c, o_out, mo_done, hs_out, hs_done, hs_kept = (signal("a_at_t", 3), signal("a_at_c", 3), signal("a_o"), signal("a_mo"),
                                                                signal("a_hs_out"), signal("a_hs"), signal("a_hs_kept", 16))
        fin_t, fin_c, y_out, x1_done, x1_kept = sem("a_fin_t"), sem("a_fin_c"), sem("a_y"), sem("a_x1"), sem("a_x1_kept")
        block = ctx.enter_context(nc.Block())
        pages_k = io["cache_sb_k"].rearrange("a n p h d -> (a n p) (h d)")
        pages_v = io["cache_sb_v"].rearrange("a n p h d -> (a n p) (h d)")
        flat = lambda a: a.rearrange("a b t h d -> (a b t) (h d)")

        @block.sync
        def _(sp):
            sp.dma_start(table[:, :], io["page_table"].rearrange("b j -> (b j)").unsqueeze(0).broadcast_to([P, NB * NPG])).then_inc(idx_done, 16)
            sp.dma_start(qn[:, :], sq_d[SEQ:SEQ + NS, :]).then_inc(own_in, 16)
            sp.dma_start(kn[:, :], flat(io["k_sample"])).then_inc(own_in, 16)
            for b in range(2):
                sp.dma_start(bias[b * 64:(b + 1) * 64, :], io["sb_bias"].rearrange("a h -> h a")
                             .broadcast_to([HS, SQ]), allow_slow_non_contiguous=True).then_inc(const_in, 16)
            load_rows(sp, gate_a[:, :], mod_d, 2 * D, True).then_inc(const_in, 16)
            sp.dma_start(xr[:, :], io["x_sample"].rearrange("b q d -> (b q) d")).then_inc(const_in, 16)
            sp.dma_start(w_out[:, :, :], io["w_out"][0].rearrange("(k p) n -> p k n", p=P)).then_inc(wo_in, 16)
            with sp.Fori(0, G) as g:
                reached(sp, free, free.ago(g))
                sp.dma_start(Vn[:, :, :], flat(io["v_sample"])[ds(g * 16, 16), :].rearrange("(b q) n -> q b n", q=SQ)).then_inc(vn_in.sem, 16)
                reached(sp, hs_done, hs_done.at(g))
                sp.dma_start(sq_d[ds(g * 16 + SEQ + NS, 16), :], hs[:, :]).then_inc(hs_kept.sem, 16)
            sp.wait_ge(hs_kept.sem, hs_kept.at(G - 1))
            sp.dma_start(hcat_s[0:NS, WM:D], sq_d[SEQ + NS:SEQ + 2 * NS, :]).then_inc(const_in, 16)
            sp.wait_ge(x1_done, 1)
            sp.dma_start(x1_d[SEQ:SEQ + NS, :], xr[:, :]).then_inc(x1_kept, 16)
            sp.wait_ge(x1_kept, 16)

        @block.gpsimd
        def _(pool):
            pool.iota(lane[:, :], [[0, 1]], base=0, channel_multiplier=1)
            pool.drain()
            pool.sem_inc(set_up, 1)

            def gather(b, j, pages, dst, sig):
                pool.indirect_dma_start(dst[:, b, j, :], None, pages,
                                        bass.IndirectOffsetOnAxis(rows_g[:, b * NPG + j:b * NPG + j + 1], 0)).then_inc(sig.sem, 16)

            def gathers():
                for pages, dst, sig in ((pages_k, Kp, k_in), (pages_v, Vp, v_in)):
                    for b in range(2):
                        for j in range(NPG):
                            gather(b, j, pages, dst, sig)

            for a, v in ((pick, 1.0), (own, 1.0), (fold4, 1.0), (vis, 1.0), (ident_h, 0.0)):
                pool.memset(a[tuple(slice(None) for _ in a.shape)], v)
            pool.drain()

            def keep(a, pattern, base, cm, op=ALU.is_ge, fill=0.0):
                pool.affine_select(out=a, in_=a, compare_op=op, fill=fill, base=base, pattern=pattern, channel_multiplier=cm)
                pool.drain()
            keep(ident_h[:, :], [[-1, P]], 0, 1, ALU.not_equal, 1.0)
            keep(own[:, :], [[-SQ, 16]], 0, 1)
            keep(fold4[:, :, :, :], [[-64, 2], [-1, SQ], [-SQ, HS]], 0, 1, ALU.is_equal)
            keep(vis[:, :, :], [[-1, SQ], [-SQ, 16]], -1, 1)
            for half in range(2):
                v = pick[half * 64:(half + 1) * 64, :, :, :].rearrange("p c b (e h) -> p c (b e) h", e=2)
                keep(v, [[-2, 4], [0, 4], [1, HS]], -half, 0, ALU.is_equal)
            pool.drain()
            keep(own[:, :], [[SQ, 16]], SQ - 1, -1)
            keep(vis[:, :, :], [[0, SQ], [SQ, 16]], SQ - 1, -1)
            v = pick[:, :, :, :].rearrange("p c b (e h) -> p c b e h", e=2)
            for b in range(2):
                keep(v[:, :, b, :, :], [[0, 4], [1, 2], [0, HS]], -b, 0, ALU.is_equal)
            pool.drain()
            pool.sem_inc(set_up, 1)
            pool.wait_ge(rows_set.sem, rows_set.at(0))
            gathers()
            with pool.Fori(1, G) as g:
                reached(pool, rows_set, rows_set.at(g))
                gathers()

        @block.tensor
        def _(pe):
            pe.wait_ge(own_in, 32)
            for n, a in enumerate((qn, kn)):
                for c in range(4):
                    t = pe.transpose(psT[n][:, c * P:c * P + NS], a[:, c * P:(c + 1) * P], ident[0:NS, 0:NS])
            t.then_inc(qk_t, 1)
            pe.wait_ge(qk_c, 1)

            def pair(g):
                reached(pe, k_in, k_in.at(g))
                for n in range(16):
                    if n >= 2:
                        sig = k_ca if n % 2 == 0 else k_cv
                        reached(pe, sig, sig.at(g, n // 2))
                    for c in range(4):
                        t = pe.transpose(psT[n % 2][:, c * P:(c + 1) * P], Kp[:, n // NPG, n % NPG, c * P:(c + 1) * P], ident[:, :])
                    t.then_inc(k_t.sem, 1)
                reached(pe, k_ca, k_ca.at(g))
                reached(pe, k_cv, k_cv.at(g))
                reached(pe, q0_set, q0_set.at(g))
                for n, (c0, c1) in enumerate(((0, 512), (512, 1024), (1024, TK_))):
                    zc = psZ[:, n * 512:n * 512 + c1 - c0]
                    if n == 2:
                        pe.matmul(zc, ident_h[:, :], hide[:, :], start=True, stop=False)
                    for c in range(4):
                        for b in range(2):
                            m = pe.matmul(zc, Q0[:, c, b, :], KT[:, c, b, c0:c1], start=n < 2 and c == 0 and b == 0, stop=c == 3 and b == 1)
                m.then_inc(z_out.sem, 1)
                reached(pe, a_done, a_done.at(g))
                for n in range(3):
                    if n == 2:
                        reached(pe, at_c, at_c.at(g, 1))
                        t = pe.transpose(psT[0][0:SQ, 0:P], A[:, PAST:TK_], ident[:, :])
                    else:
                        for j in range(4):
                            t = pe.transpose(psT[n][:, j * P:(j + 1) * P], A[:, (n * 4 + j) * P:(n * 4 + j + 1) * P], ident[:, :])
                    t.then_inc(at_t.sem, 1)
                reached(pe, at_c, at_c.at(g))
                reached(pe, v_in, v_in.at(g))
                reached(pe, vn_in, vn_in.at(g))
                for b in range(2):
                    for j in range(NPG):
                        pe.matmul(psO[:, b, :], AT[:, j, :], Vp[:, b, j, :], start=j == 0, stop=False)
                    m = pe.matmul(psO[:, b, :], ATn[:, :], Vn[:, b, :], start=False, stop=True)
                m.then_inc(o_out.sem, 1)
                reached(pe, mo_done, mo_done.at(g))
                pe.matmul(psX[0:16, :], fold[:, :, :].rearrange("p b q -> p (b q)"), mo[:, 0, :], start=True, stop=True).then_inc(hs_out.sem, 1)

            pe.wait_ge(folded, 1)
            with pe.Fori(0, G) as g:
                pair(g)
            pe.wait_ge(const_in, 80)
            pe.wait_ge(hs_done.sem, hs_done.at(G - 1))
            for j in range(KD):
                t = pe.transpose(psX[:, j * NS:(j + 1) * NS], hcat_s[0:NS, j * P:(j + 1) * P], ident[0:NS, 0:NS])
            t.then_inc(fin_t, 1)
            pe.wait_ge(fin_c, 1)
            pe.wait_ge(wo_in, 16)
            for c in range(2):
                for j in range(KD):
                    m = pe.matmul(psO[0:NS, c, :], hcT[:, j, :], w_out[:, j, c * 512:(c + 1) * 512], start=j == 0, stop=j == KD - 1)
            m.then_inc(y_out, 1)

        @block.scalar
        def _(act):
            act.preload_act_table_set(EXP_LN)
            def pair(g):
                for n in range(0, 16, 2):
                    reached(act, k_t, k_t.at(g, n + 1))
                    act.activation(KT[:, :, n // NPG, (n % NPG) * P:(n % NPG + 1) * P],
                                   psT[0][:, :].rearrange("p (c t) -> p c t", c=4), ACT.Copy).then_inc(k_ca.sem, 1)
                reached(act, z_lin, z_lin.at(g))
                act.activation(lz[:, :], zb[:, :], ACT.Abs)
                act.drain()
                act.activation(lz[:, :], lz[:, :], ACT.Exp, scale=-1.0)
                act.drain()
                act.activation(lz[:, :], lz[:, :], ACT.Ln, bias=1.0).then_inc(l_done.sem, 1)
                reached(act, d_done, d_done.at(g))
                act.activation(A[:, :], cum[:, :], ACT.Exp).then_inc(a_done.sem, 1)
                for n in range(3):
                    reached(act, at_t, at_t.at(g, n + 1))
                    if n == 2:
                        c = act.activation(ATn[:, :], psT[0][0:SQ, 0:P], ACT.Copy)
                    else:
                        c = act.activation(AT[:, n * 4:(n + 1) * 4, :], psT[n][:, :].rearrange("p (c t) -> p c t", c=4), ACT.Copy)
                    c.then_inc(at_c.sem, 1)
                reached(act, hs_out, hs_out.at(g))
                act.activation(hs[:, :], psX[0:16, :], ACT.Copy).then_inc(hs_done.sem, 1)

            with act.Fori(0, G) as g:
                pair(g)
                reached(act, hs_kept, hs_kept.at(g))
            act.wait_ge(fin_t, 1)
            act.activation(hcT[:, :, :], psX[:, :].rearrange("p (j t) -> p j t", j=KD), ACT.Copy).then_inc(fin_c, 1)

        @block.vector
        def _(dve):
            dve.memset(one[:, :], 1.0)
            dve.wait_ge(idx_done, 16)
            dve.wait_ge(set_up, 1)
            dve.tensor_copy(table_f[:, :], table[:, :])
            dve.tensor_copy(lane_f[:, :], lane[:, :])
            dve.drain()
            dve.tensor_scalar(rows[:, :], table_f[:, :], float(PAGE), lane_f[:, 0:1], ALU.mult, ALU.add)
            dve.drain()

            def take_rows(g):
                dve.tensor_copy(rows_g[:, :], rows[:, ds(g * 2 * NPG, 2 * NPG)]).then_inc(rows_set.sem, 1)

            take_rows(0)
            dve.wait_ge(set_up, 2)
            dve.tensor_reduce(fold[:, :, :], fold4[:, :, :, :], AX.X, ALU.add)
            dve.tensor_reduce(hide_f[:, :], vis[:, :, :], AX.X, ALU.add)
            dve.drain()
            dve.tensor_scalar(hide[:, :], hide_f[:, :], -HIDE, HIDE, ALU.mult, ALU.add)
            dve.drain()
            dve.sem_inc(folded, 1)
            dve.wait_ge(qk_t, 1)
            dve.tensor_copy(QT[:, :, :], psT[0][:, :].rearrange("p (c t) -> p c t", c=4)[:, :, 0:NS])
            dve.tensor_copy(KnT[:, :, :], psT[1][:, :].rearrange("p (c t) -> p c t", c=4)[:, :, 0:NS])
            dve.drain()
            dve.sem_inc(qk_c, 1)
            prime(dve, free)
            dve.wait_ge(const_in, 64)

            def pair(g):
                q = QT[:, :, ds(g * 16, 16)].rearrange("p c (b q) -> p c b q", q=SQ)
                for c in range(4):
                    dve.tensor_tensor(Q0[:, c, :, :].rearrange("p b (x q) -> p b x q", q=SQ),
                                      q[:, c, :, :].unsqueeze(2).broadcast_to([P, 2, 16, SQ]),
                                      pick[:, c, :, :].unsqueeze(3).broadcast_to([P, 2, 16, SQ]), ALU.mult)
                for b in range(2):
                    dve.tensor_copy(KT[:, :, b, PAST:TK_], KnT[:, :, ds(g * 16 + b * SQ, SQ)])
                dve.drain()
                dve.sem_inc(q0_set.sem, 1)
                for n in range(1, 16, 2):
                    reached(dve, k_t, k_t.at(g, n + 1))
                    dve.tensor_copy(KT[:, :, n // NPG, (n % NPG) * P:(n % NPG + 1) * P],
                                    psT[1][:, :].rearrange("p (c t) -> p c t", c=4)).then_inc(k_cv.sem, 1)
                reached(dve, z_out, z_out.at(g))
                dve.tensor_scalar(zb[:, :], psZ[:, 0:TK_], DS ** -0.5, bias[:, 0:1], ALU.mult, ALU.add).then_inc(z_lin.sem, 1)
                reached(dve, l_done, l_done.at(g))
                dve.drain()
                dve.scalar_tensor_tensor(out=cum[:, :], in0=zb[:, :], scalar=0.0, in1=lz[:, :], op0=ALU.max, op1=ALU.add)
                dve.drain()
                back = cum[:, ::-1]
                dve.tensor_tensor_scan(back, one[:, 0:1].broadcast_to([P, TK_]), back, 0.0, ALU.mult, ALU.add)
                dve.drain()
                dve.tensor_tensor(cum[:, :], zb[:, :], cum[:, :], ALU.subtract).then_inc(d_done.sem, 1)
                reached(dve, o_out, o_out.at(g))
                for b in range(2):
                    dve.tensor_tensor(mo[:, b, :].rearrange("p (h d) -> p h d", h=HS), psO[:, b, :].rearrange("p (h d) -> p h d", h=HS),
                                      own[:, b * HS:(b + 1) * HS].unsqueeze(2).broadcast_to([P, HS, DS]), ALU.mult)
                dve.drain()
                dve.tensor_tensor(mo[:, 0, :], mo[:, 0, :], mo[:, 1, :], ALU.add).then_inc(mo_done.sem, 1)
                reached(dve, hs_out, hs_out.at(g))
                dve.sem_inc(free.sem, 1)

            with dve.Fori(0, G - 1) as g:
                pair(g)
                reached(dve, k_in, k_in.at(g))
                reached(dve, v_in, v_in.at(g))
                take_rows(g + 1)
            pair(G - 1)
            dve.wait_ge(y_out, 1)
            dve.tensor_tensor(gate_a[:, :], psO[0:NS, :, :].rearrange("p a n -> p (a n)"), gate_a[:, :], ALU.mult)
            dve.drain()
            dve.tensor_tensor(xr[:, :], gate_a[:, :], xr[:, :], ALU.add).then_inc(x1_done, 1)



def experts(nc, io, sem, pool_dma_sem, signal, reached, prime, mod_d, x1_d, **_):
    NU, NV, NW, GR, PIECES = 4, 8, 4, 8, 8
    PT = P // PIECES
    LOW = -3e38
    with ExitStack() as ctx:
        sb = lambda n, s, d=F32: ctx.enter_context(nc.sbuf_tensor(n, s, d))
        ps = lambda n, s, d=F32: ctx.enter_context(nc.psum_tensor(n, s, d))
        ident = sb("f_ident", [P, P])
        w_q = sb("w_query_sb", [P, KD, 2 * PH * DK])
        sub = sb("sub_keys_T", [P, 2, NK])
        gain, shift, gate = sb("f_gain", [P, D]), sb("f_shift", [P, D]), sb("f_gate", [P, D])
        xp, hf = sb("f_x", [P, D]), sb("hf", [P, D])
        xo = sb("f_xo", [P, D])
        rest = sb("f_rest", [P, D])
        parts = sb("f_parts", [P, 3, D], BF16)
        x3 = sb("f_x3", [96, 4, D], BF16)
        hfT, qT = sb("hfT", [P, KD, P]), sb("qT", [P, 2 * PH, P])
        sc = sb("scores", [P, 2 * PH, NK])
        va, ia, iaf = sb("va", [P, 2 * PH, TK]), sb("ia", [P, 2 * PH, TK], U32), sb("iaf", [P, 2 * PH, TK])
        s2, cand, cand2 = sb("s2", [P, NK]), sb("cand", [P, TK, TK]), sb("cand2", [P, TK * TK])
        ts, pos = sb("ts", [P, PH, TK]), sb("pos", [P, PH, TK], U32)
        pij, pijf = sb("pij", [P, 2, PH * TK], U32), sb("pijf", [P, 2, PH * TK])
        number, found = sb("number", [P, TK]), sb("found", [P, 2, PH * TK])
        number_i = sb("number_i", [P, TK], I32)
        gates_e, gsum = sb("gates_e", [P, PH, TK]), sb("gsum", [P, PH])
        idx_next, g_next = sb("idx_next", [P, P], I32), sb("g_next", [P, P])
        idx, gT = sb("idx", [P, P], I32), sb("gT", [P, P])
        ssq, rstd = sb("f_ssq", [P, 1]), sb("f_rstd", [P, 1])
        sel3, zero_h = sb("sel3", [96, 32], BF16), sb("zero_h", [96, P], BF16)
        strip = sb("strip", [P, 2 * P])
        ub, vb = sb("ub", [P, NU, D]), sb("vb", [P, NV, D])
        junk = sb("f_junk", [P, D], BF16)
        slot = sb("slot", [P, GR], I32)
        dot, act_o = sb("dot", [P, GR]), sb("act_o", [P, GR])
        W = sb("W", [P, NW, P])
        psX, psY, psP = ps("psX", [P, 2, D]), ps("psY", [P, D]), ps("psP", [P, D])

        wq_in, mods_in, sub_in, set_up = sem("wq_in"), sem("f_mods_in"), sem("sub_in"), sem("f_setup")
        sub_t, sub_c = sem("sub_t"), sem("sub_c")
        x_in, x_free = signal("f_x_in", 16), signal("f_x_free", 1, 1)
        ssq_d, rstd_d, h_d, h_t, hT_a, hT_v = (signal(f"f_{n}") for n in ("ssq_d", "rstd_d", "h_d", "h_t", "hT_a", "hT_v"))
        part_a, part_v, x3_in = signal("part_a", 3), signal("part_v", 2), signal("x3_in", 16 * 12)
        q_out, q_copied, sc_out, sc_copied = signal("q_out", 4), signal("q_copied", 4), signal("sc_out", 4), signal("sc_copied", 4)
        soft_v, soft_a, made, made_t, next_set = signal("soft_v"), signal("soft_a"), signal("made"), signal("made_t", 2), signal("next_set", 1)
        cur_set, idx_taken = signal("cur_set"), signal("idx_taken")
        u_in, v_in = [pool_dma_sem(f"u_in{i}") for i in range(NU)], [pool_dma_sem(f"v_in{i}") for i in range(NV)]
        slot_set = sem("slot_set")
        spread, dotted, acted, weighed, added = sem("spread"), sem("dotted"), sem("acted"), sem("weighed"), sem("added")
        y_read, out_set, out_kept, xo_in = signal("y_read", 1, 1), signal("out_set"), signal("out_kept", 16, 1), signal("xo_in", 16)
        block = ctx.enter_context(nc.Block())

        def rounds(eng, route, spend, boundary):
            for piece in range(PIECES):
                route(0, piece)
            with eng.Fori(0, NT - 1) as r:
                boundary(r)
                for piece in range(PIECES):
                    route(r + 1, piece)
                    with eng.Fori(0, PT // GR) as c:
                        spend(r, piece, c)
                boundary(r, end=True)
            boundary(NT - 1)
            for piece in range(PIECES):
                route(NT, piece)
                with eng.Fori(0, PT // GR) as c:
                    spend(NT - 1, piece, c)
            boundary(NT - 1, end=True)
            boundary(NT)
            for piece in range(NS // PT):
                with eng.Fori(0, PT // GR) as c:
                    spend(NT, piece, c)
            boundary(NT, end=True)

        def group(r, piece, c):
            local = c * GR + piece * PT
            return local, r * P + local

        @block.sync
        def _(sp):
            prime(sp, out_kept)
            load_rows(sp, gain[:, :], mod_d, 4 * D, False).then_inc(mods_in, 16)
            load_rows(sp, shift[:, :], mod_d, 3 * D, False).then_inc(mods_in, 16)
            load_rows(sp, gate[:, :], mod_d, 5 * D, False).then_inc(mods_in, 16)

            def load(k, sample):
                reached(sp, x_free, x_free.ago(k))
                rows = NS if sample else P
                if sample:
                    load_rows(sp, gain[0:NS, :], mod_d, 4 * D, True).then_inc(mods_in, 16)
                    load_rows(sp, shift[0:NS, :], mod_d, 3 * D, True).then_inc(mods_in, 16)
                sp.dma_start(xp[0:rows, :], x1_d[ds(k * P, rows), :]).then_inc(x_in.sem, 16)

            def spread_load(k):
                reached(sp, part_a, part_a.at(k))
                if not (isinstance(k, int) and k == 0):
                    reached(sp, added, k * P + NV)
                for part in range(3):
                    for g in range(4):
                        sp.dma_start(x3[part * 32:(part + 1) * 32, g, :], parts[g * 32:(g + 1) * 32, part, :]).then_inc(x3_in.sem, 16)

            def finish(r, sample):
                rows = NS if sample else P
                if sample:
                    load_rows(sp, gate[0:NS, :], mod_d, 5 * D, True).then_inc(mods_in, 16)
                sp.dma_start(xo[0:rows, :], x1_d[ds(r * P, rows), :]).then_inc(xo_in.sem, 16)
                reached(sp, out_set, out_set.at(r))
                dst = io["y_sample"].rearrange("b q d -> (b q) d") if sample else io["y_prompt"][0, ds(r * P, P), :]
                sp.dma_start(dst, xo[0:rows, :]).then_inc(out_kept.sem, 16)
                reached(sp, out_kept, out_kept.at(r))

            load(0, False)
            for n, name in enumerate(("sub_keys_a", "sub_keys_b")):
                sp.dma_start(s2[:, :] if n == 0 else cand2[:, 0:NK], io[name][0]).then_inc(sub_in, 16)
            sp.dma_start(w_q[:, :, :], io["w_query"][0].rearrange("(k p) n -> p k n", p=P)).then_inc(wq_in, 16)
            spread_load(0)
            with sp.Fori(0, NT - 1) as r:
                load(r + 1, False)
                spread_load(r + 1)
                finish(r, False)
            load(NT, True)
            spread_load(NT)
            finish(NT - 1, False)
            finish(NT, True)

        @block.gpsimd
        def _(pool):
            pool.iota(number_i[:, :], [[1, TK]], base=0, channel_multiplier=0)
            pool.memset(ident[:, :], 0.0)
            pool.memset(sel3[:, :], 0.0)
            pool.memset(zero_h[:, :], 0.0)
            pool.memset(strip[:, :], 0.0)
            pool.drain()
            pool.memset(strip[:, P:P + 1], 1.0)
            pool.affine_select(out=ident[:, :], in_=ident[:, :], compare_op=ALU.not_equal, fill=1.0, base=0,
                               pattern=[[-1, P]], channel_multiplier=1)
            pool.drain()
            for part in range(3):
                pool.affine_select(out=sel3[:, :], in_=sel3[:, :], compare_op=ALU.not_equal, fill=1.0, base=-32 * part,
                                   pattern=[[-1, 32]], channel_multiplier=1)
                pool.drain()
            pool.sem_inc(set_up, 1)

            def spend(r, piece, c):
                local, base = group(r, piece, c)
                for j in range(GR):
                    reached(pool, dotted, base + j + 1)
                    reached(pool, added, base + j + 1)
                    pool.tensor_copy(slot[:, j:j + 1], idx[:, ds(local + j, 1)]).then_inc(slot_set, 1)
                    reached(pool, slot_set, base + j + 1)
                    at = bass.IndirectOffsetOnAxis(slot[:, j:j + 1], 0)
                    pool.indirect_dma_start(ub[:, j % NU, :], None, io["expert_u"][0], at).then_inc(u_in[j % NU], 16)
                    pool.indirect_dma_start(vb[:, j, :], None, io["expert_v"][0], at).then_inc(v_in[j], 16)

            def boundary(r, end=False):
                if end:
                    pool.sem_inc(idx_taken.sem, 1)
                else:
                    reached(pool, cur_set, cur_set.at(r))

            rounds(pool, lambda k, piece: None, spend, boundary)

        @block.tensor
        def _(pe):
            pe.sem_inc(added, NV)
            pe.wait_ge(sub_in, 32)
            pe.wait_ge(set_up, 1)
            pe.transpose(psP[:, 0:NK], s2[:, :], ident[:, :])
            pe.transpose(psP[:, NK:2 * NK], cand2[:, 0:NK], ident[:, :]).then_inc(sub_t, 1)
            pe.wait_ge(sub_c, 1)
            pe.wait_ge(wq_in, 16)

            def query(k, g):
                if g >= 2:
                    reached(pe, q_copied, q_copied.at(k, g - 1))
                for c in range(4):
                    for j in range(KD):
                        m = pe.matmul(psP[:, (g % 2) * 512 + c * P:(g % 2) * 512 + (c + 1) * P],
                                      w_q[:, j, (4 * g + c) * DK:(4 * g + c + 1) * DK], hfT[:, j, :], start=j == 0, stop=j == KD - 1)
                m.then_inc(q_out.sem, 1)

            def score(k, g):
                reached(pe, q_copied, q_copied.at(k, g + 1 if g % 2 else g + 2))
                for c in range(4):
                    m = pe.matmul(psP[:, (g % 2) * 512 + c * P:(g % 2) * 512 + (c + 1) * P], qT[:, 4 * g + c, :], sub[:, c % 2, :],
                                  start=True, stop=True)
                m.then_inc(sc_out.sem, 1)

            def route(k, piece):
                if piece == 0:
                    reached(pe, h_d, h_d.at(k))
                    for j in range(KD):
                        t = pe.transpose(psP[:, j * P:(j + 1) * P], hf[:, j * P:(j + 1) * P], ident[:, :])
                    t.then_inc(h_t.sem, 1)
                if piece in (1, 2):
                    if piece == 1:
                        reached(pe, hT_a, hT_a.at(k))
                        reached(pe, hT_v, hT_v.at(k))
                    else:
                        reached(pe, sc_copied, sc_copied.at(k, 2))
                    for g in (2 * piece - 2, 2 * piece - 1):
                        query(k, g)
                    for g in (2 * piece - 2, 2 * piece - 1):
                        score(k, g)
                if piece == 7:
                    reached(pe, sc_copied, sc_copied.at(k))
                    reached(pe, made, made.at(k))
                    pe.transpose(psP[:, 0:P], found[:, 0, :], ident[:, :]).then_inc(made_t.sem, 1)
                    pe.transpose(psP[:, 512:512 + P], gates_e[:, :, :].rearrange("p h k -> p (h k)"), ident[:, :]).then_inc(made_t.sem, 1)

            def spend(r, piece, c):
                local, base = group(r, piece, c)

                def spread_row(j):
                    reached(pe, dotted, base + j + NU - 1)
                    x0 = (piece % 2) * PT + j
                    pick = sel3[:, ds(c * GR + x0, 1)].broadcast_to([96, P])
                    for half in range(2):
                        m = pe.matmul(psX[:, j % 2, half * 512:(half + 1) * 512], pick,
                                      x3[:, piece * PT // 32, half * 512:(half + 1) * 512], start=True, stop=True)
                    m.then_inc(spread, 1)

                spread_row(0)
                spread_row(1)
                for j in range(GR):
                    if j + 2 < GR:
                        spread_row(j + 2)
                    reached(pe, weighed, base + j + 1)
                    reached(pe, v_in[j], base * 2 + 16)
                    for half in range(2):
                        m = pe.matmul(psY[:, half * 512:(half + 1) * 512], W[:, j % NW, :], vb[:, j, half * 512:(half + 1) * 512],
                                      start=False, stop=False, skip_group_check=True)
                    m.then_inc(added, 1)

            def boundary(r, end=False):
                if end:
                    return
                reached(pe, x3_in, x3_in.at(r))
                reached(pe, y_read, y_read.ago(r))
                for half in range(2):
                    pe.matmul(psY[:, half * 512:(half + 1) * 512], zero_h[:, :], x3[:, 0, half * 512:(half + 1) * 512],
                              start=True, stop=False, skip_group_check=True)

            rounds(pe, route, spend, boundary)

        @block.scalar
        def _(act):
            act.preload_act_table_set(EXP_LN)

            def route(k, piece):
                if piece == 0:
                    reached(act, ssq_d, ssq_d.at(k))
                    act.activation(rstd[:, :], ssq[:, :], ACT.Ln, scale=1.0 / D, bias=EPS)
                    act.drain()
                    act.activation(rstd[:, :], rstd[:, :], ACT.Exp, scale=-0.5).then_inc(rstd_d.sem, 1)
                    reached(act, h_t, h_t.at(k))
                    act.activation(hfT[:, 0:4, :], psP[:, 0:512].rearrange("p (j t) -> p j t", t=P), ACT.Copy).then_inc(hT_a.sem, 1)
                    if not (isinstance(k, int) and k == 0):
                        reached(act, x3_in, x3_in.at(k - 1))
                    act.activation(parts[:, 0, :], hf[:, :], ACT.Copy).then_inc(part_a.sem, 1)
                    reached(act, part_v, part_v.at(k, 1))
                    act.activation(parts[:, 1, :], rest[:, :], ACT.Copy).then_inc(part_a.sem, 1)
                    reached(act, part_v, part_v.at(k, 2))
                    act.activation(parts[:, 2, :], rest[:, :], ACT.Copy).then_inc(part_a.sem, 1)
                if piece in (1, 2):
                    for g in (2 * piece - 2, 2 * piece - 1):
                        reached(act, q_out, q_out.at(k, g + 1))
                        act.activation(qT[:, 4 * g:4 * g + 4, :], psP[:, (g % 2) * 512:(g % 2 + 1) * 512].rearrange("p (j t) -> p j t", t=P),
                                       ACT.Copy).then_inc(q_copied.sem, 1)
                    for g in (2 * piece - 2, 2 * piece - 1):
                        reached(act, sc_out, sc_out.at(k, g + 1))
                        act.activation(sc[:, 4 * g:4 * g + 4, :], psP[:, (g % 2) * 512:(g % 2 + 1) * 512].rearrange("p (j t) -> p j t", t=P),
                                       ACT.Copy).then_inc(sc_copied.sem, 1)
                if piece == 7:
                    reached(act, soft_v, soft_v.at(k))
                    act.activation(gates_e[:, :, :], gates_e[:, :, :], ACT.Exp).then_inc(soft_a.sem, 1)

            def spend(r, piece, c):
                local, base = group(r, piece, c)
                for j in range(GR):
                    reached(act, dotted, base + j + 1 + NU)
                    act.activation(act_o[:, j:j + 1], dot[:, j:j + 1], ACT.Gelu).then_inc(acted, 1)

            rounds(act, route, spend, lambda r, end=False: None)

        @block.vector
        def _(dve):
            prime(dve, x_free, y_read)
            dve.sem_inc(dotted, NU)
            dve.wait_ge(sub_t, 1)
            dve.tensor_copy(sub[:, :, :], psP[:, 0:2 * NK].rearrange("p (a n) -> p a n", a=2)).then_inc(sub_c, 1)
            dve.wait_ge(set_up, 1)
            dve.tensor_copy(number[:, :], number_i[:, :])
            dve.drain()

            def top16(values, spare, top, at):
                dve.max(top[:, 0:8], values)
                dve.drain()
                dve.max_index(at[:, 0:8], top[:, 0:8], values)
                dve.match_replace(spare, top[:, 0:8], values, LOW)
                dve.drain()
                dve.max(top[:, 8:16], spare)
                dve.drain()
                dve.max_index(at[:, 8:16], top[:, 8:16], spare)
                dve.drain()

            def side(k, u):
                if u % 4 == 0:
                    reached(dve, sc_copied, sc_copied.at(k, u // 4 + 1))
                top16(sc[:, u, :], s2[:, :], va[:, u, :], ia[:, u, :])

            def pairs(h):
                dve.tensor_tensor(cand[:, :, :], va[:, 2 * h, :].unsqueeze(2).broadcast_to([P, TK, TK]),
                                  va[:, 2 * h + 1, :].unsqueeze(1).broadcast_to([P, TK, TK]), ALU.add)
                dve.drain()
                top16(cand[:, :, :].rearrange("p a b -> p (a b)"), cand2[:, :], ts[:, h, :], pos[:, h, :])

            def look_up(half):
                H4, w = PH // 2, PH // 2 * TK
                hs = slice(half * H4, (half + 1) * H4)
                cs = slice(half * w, (half + 1) * w)
                flat_pos = pos[:, hs, :].rearrange("p h k -> p (h k)")
                dve.tensor_scalar(pij[:, 0, cs], flat_pos, 4, None, ALU.logical_shift_right)
                dve.tensor_scalar(pij[:, 1, cs], flat_pos, TK - 1, None, ALU.bitwise_and)
                us = slice(half * 2 * H4, (half + 1) * 2 * H4)
                dve.tensor_copy(iaf[:, us, :], ia[:, us, :])
                dve.drain()
                dve.tensor_copy(pijf[:, :, cs], pij[:, :, cs])
                dve.drain()
                hot = sc[:, us, :].rearrange("p u n -> p (u n)").rearrange("p (x k i) -> p x k i", k=TK, i=TK)[:, 0:H4, :, :]
                flat = hot.rearrange("p x k i -> p (x k) i")
                for which in range(2):
                    table = iaf[:, us, :].rearrange("p (h s) i -> p h s i", s=2)[:, :, which, :]
                    dve.tensor_tensor(flat, pijf[:, which, cs].unsqueeze(2).broadcast_to([P, w, TK]),
                                      number[:, :].unsqueeze(1).broadcast_to([P, w, TK]), ALU.is_equal)
                    dve.drain()
                    dve.tensor_tensor(hot, hot, table.unsqueeze(2).broadcast_to([P, H4, TK, TK]), ALU.mult)
                    dve.drain()
                    dve.tensor_reduce(found[:, which, cs], flat, AX.X, ALU.add)
                    dve.drain()
                dve.scalar_tensor_tensor(out=found[:, 0, cs], in0=found[:, 0, cs], scalar=float(NK), in1=found[:, 1, cs],
                                         op0=ALU.mult, op1=ALU.add)
                dve.drain()

            def route(k, piece):
                last = isinstance(k, int) and k == NT
                if piece == 0:
                    reached(dve, x_in, x_in.at(k))
                    dve.wait_ge(mods_in, 16 * (5 if last else 3))
                    dve.tensor_tensor_reduce(hf[:, :], xp[:, :], xp[:, :], 1.0, 0.0, ALU.mult, ALU.add, ssq[:, :]).then_inc(ssq_d.sem, 1)
                    reached(dve, rstd_d, rstd_d.at(k))
                    dve.drain()
                    dve.scalar_tensor_tensor(out=hf[:, :], in0=xp[:, :], scalar=rstd[:, 0:1], in1=gain[:, :], op0=ALU.mult, op1=ALU.mult)
                    dve.drain()
                    dve.tensor_tensor(hf[:, :], hf[:, :], shift[:, :], ALU.add).then_inc(h_d.sem, 1)
                    dve.drain()
                    dve.sem_inc(x_free.sem, 1)
                    reached(dve, h_t, h_t.at(k))
                    dve.tensor_copy(hfT[:, 4:8, :], psP[:, 512:1024].rearrange("p (j t) -> p j t", t=P)).then_inc(hT_v.sem, 1)
                    reached(dve, part_a, part_a.at(k, 1))
                    dve.tensor_tensor(rest[:, :], hf[:, :], parts[:, 0, :], ALU.subtract).then_inc(part_v.sem, 1)
                    reached(dve, part_a, part_a.at(k, 2))
                    dve.drain()
                    dve.tensor_tensor(rest[:, :], rest[:, :], parts[:, 1, :], ALU.subtract).then_inc(part_v.sem, 1)
                for u in {2: range(0, 4), 3: range(4, 10), 4: range(10, 16)}.get(piece, ()):
                    side(k, u)
                for h in {5: (0, 1, 2, 3), 6: (4, 5), 7: (6, 7)}.get(piece, ()):
                    pairs(h)
                if piece == 6:
                    look_up(0)
                if piece == 7:
                    look_up(1)
                    dve.tensor_tensor(gates_e[:, :, :], ts[:, :, :], ts[:, :, 0:1].broadcast_to([P, PH, TK]), ALU.subtract).then_inc(soft_v.sem, 1)
                    reached(dve, soft_a, soft_a.at(k))
                    dve.drain()
                    dve.tensor_reduce(gsum[:, :], gates_e[:, :, :], AX.X, ALU.add)
                    dve.drain()
                    dve.reciprocal(gsum[:, :], gsum[:, :])
                    dve.drain()
                    dve.tensor_tensor(gates_e[:, :, :], gates_e[:, :, :], gsum[:, :].unsqueeze(2).broadcast_to([P, PH, TK]), ALU.mult)
                    dve.drain()
                    dve.sem_inc(made.sem, 1)
                    reached(dve, made_t, made_t.at(k))
                    dve.tensor_copy(idx_next[:, :], psP[:, 0:P])
                    dve.tensor_copy(g_next[:, :], psP[:, 512:512 + P])
                    dve.drain()

            def spend(r, piece, c):
                local, base = group(r, piece, c)

                def weigh(j):
                    reached(dve, acted, base + j + 1)
                    reached(dve, added, base + j + 1 + NV - NW)
                    dve.tensor_scalar(W[:, j % NW, :], strip[:, ds(P - local - j, P)], act_o[:, j:j + 1], gT[:, ds(local + j, 1)],
                                      ALU.mult, ALU.mult).then_inc(weighed, 1)

                for j in range(GR):
                    reached(dve, spread, base + j + 1)
                    reached(dve, u_in[j % NU], base * 4 + 16 * (j // NU + 1))
                    dve.tensor_tensor_reduce(junk[:, :], ub[:, j % NU, :], psX[:, j % 2, :], 1.0, 0.0, ALU.mult, ALU.add,
                                             dot[:, j:j + 1]).then_inc(dotted, 1)
                    if j >= 1:
                        weigh(j - 1)
                    dve.drain()
                weigh(GR - 1)
                dve.drain()

            def boundary(r, end=False):
                if end:
                    last = isinstance(r, int) and r == NT
                    reached(dve, added, (SEQ + NS if last else (r + 1) * P) + NV)
                    reached(dve, xo_in, xo_in.at(r))
                    dve.wait_ge(mods_in, 16 * (6 if last else 3))
                    dve.tensor_tensor(rest[:, :], psY[:, :], gate[:, :], ALU.mult).then_inc(y_read.sem, 1)
                    dve.drain()
                    dve.tensor_tensor(xo[:, :], rest[:, :], xo[:, :], ALU.add).then_inc(out_set.sem, 1)
                    dve.drain()
                    return
                if not (isinstance(r, int) and r == 0):
                    reached(dve, idx_taken, idx_taken.at(r - 1))
                dve.tensor_copy(idx[:, :], idx_next[:, :])
                dve.tensor_copy(gT[:, :], g_next[:, :])
                dve.drain()
                dve.sem_inc(cur_set.sem, 1)

            rounds(dve, route, spend, boundary)


_INS = ["x_prompt", "x_sample", "cache_sb_k", "cache_sb_v", "state_mlstm_C", "state_mlstm_n", "state_mlstm_m",
        "page_table", "c_prompt", "c_sample", "w_ada", "b_ada", "norm_mix_g", "norm_ffn_g", "w_in", "b_gates",
        "qnorm_g", "knorm_g", "sb_bias", "mlstm_head_g", "w_out", "w_query", "sub_keys_a", "sub_keys_b",
        "expert_u", "expert_v"]
_OUTS = [("y_prompt", (1, SEQ, D)), ("y_sample", (NB, SQ, D)),
         ("k_prompt", (1, 1, SEQ, HS, DS)), ("v_prompt", (1, 1, SEQ, HS, DS)),
         ("C_prompt", (1, 1, HM, DM, DM)), ("n_prompt", (1, 1, HM, DM)), ("m_prompt", (1, 1, HM)),
         ("k_sample", (1, NB, SQ, HS, DS)), ("v_sample", (1, NB, SQ, HS, DS)),
         ("C_sample", (1, NB, HM, DM, DM)), ("n_sample", (1, NB, HM, DM)), ("m_sample", (1, NB, HM))]


def kernel(**inputs):
    import concourse.bacc as bacc
    from concourse.bass_utils import run_bass_kernel_spmd as run

    nc = bacc.Bacc("TRN2", target_bir_lowering=False, num_devices=1)
    arrays, io = {}, {}
    for name in _INS:
        a = np.ascontiguousarray(inputs[name])
        arrays[f"in_{name}"] = a
        io[name] = nc.dram_tensor(f"in_{name}", a.shape, mybir.dt.from_np(a.dtype), kind="ExternalInput").ap()
    for name, shape in _OUTS:
        io[name] = nc.dram_tensor(f"out_{name}", shape, F32, kind="ExternalOutput").ap()
    build(nc, io)
    r = run(nc, [arrays], core_ids=[0])
    return tuple(r.results[0][f"out_{name}"] for name, _ in _OUTS)
```

```python
from contextlib import ExitStack

import numpy as np
import concourse.bass as bass
from concourse import mybir

ALU = mybir.AluOpType
ACT = mybir.ActivationFunctionType
AX = mybir.AxisListType
F32 = mybir.dt.float32
BF16 = mybir.dt.bfloat16
I32 = mybir.dt.int32
U32 = mybir.dt.uint32
ds = bass.ds

P = 128
D = 1024
KD = D // P
SEQ = 1024
NT = SEQ // P
NB = 8
SQ = 8
NS = NB * SQ
PAST = 1024
PAGE = 128
NPG = PAST // PAGE
HM, DM = 4, 128
HS, DS = 8, 64
WM, WS = HM * DM, HS * DS
NIN = 4 * WM + 2 * HM + 3 * WS
TT = SEQ + NS
CAP = 15.0
EPS = 1e-6
HIDE = -1e30
PH, NK, DK, TK = 8, 128, 128, 16
NE = NK * NK
KX = PH * TK
EXP_LN = "natural_log_exp_and_others"


class Signal:

    def __init__(self, sem, per=1, ahead=0):
        self.sem, self.per, self.ahead = sem, per, ahead

    def at(self, k, n=None):
        return k * self.per + ((self.per if n is None else n) + self.ahead * self.per)

    def ago(self, k, n=None):
        return k * self.per + (self.per if n is None else n)


def build(nc, io):
    ctx = ExitStack()
    with ctx:
        scopes = [(ctx, [])]

        def sem(name):
            scope, held = scopes[-1]
            held.append(scope.enter_context(nc.semaphore(name)))
            return held[-1]

        def pool_dma_sem(name):
            return ctx.enter_context(nc.semaphore(name))

        def phase(run, **kw):
            with ExitStack() as scope:
                scopes.append((scope, []))
                run(**kw)
                _, held = scopes.pop()
                with nc.Block() as block:
                    @block.sync
                    def _(sp):
                        for s in held:
                            sp.sem_clear(s)

        def signal(name, per=1, ahead=0):
            return Signal(sem(name), per, ahead)

        passed = {id(e): sem(f"passed_{n}") for n, e in
                  (("pe", nc.tensor), ("act", nc.scalar), ("dve", nc.vector), ("pool", nc.gpsimd), ("sp", nc.sync))}

        def reached(eng, sig, value):
            s = sig.sem if isinstance(sig, Signal) else sig
            eng.wait_ge(s, value)
            if not isinstance(value, int):
                eng.sem_inc(passed[id(eng)], 1)

        def prime(eng, *sigs):
            for s in sigs:
                eng.sem_inc(s.sem, s.ahead * s.per)

        def dram(name, shape, dt=F32):
            return nc.dram_tensor(name, shape, dt, kind="Internal").ap()

        mod_d = dram("mod_d", (1 + NB, 6 * D))
        mix_d = dram("mix_d", ((NT + 1) * P, 4 * WM))
        sq_d = dram("sq_d", ((NT + 1) * P, WS))
        x1_d = dram("x1_d", ((NT + 1) * P, D))

        shared = dict(nc=nc, pool_dma_sem=pool_dma_sem, io=io, sem=sem, signal=signal, reached=reached, prime=prime,
                      mod_d=mod_d, mix_d=mix_d, sq_d=sq_d, x1_d=x1_d)
        outer = ExitStack()
        with outer:
            def sbo(name, shape, dt=F32):
                return outer.enter_context(nc.sbuf_tensor(name, shape, dt))

            ident = sbo("ident", [P, P])
            gate_rows = sbo("gate_rows", [HM, 2, TT])
            sel_head = sbo("sel_head", [HM, HM, P])
            w_in_loaded = sem("w_in_loaded")
            shared.update(sel_head=sel_head, ident=ident, gate_rows=gate_rows, w_in_loaded=w_in_loaded)
            with nc.sbuf_tensor("w_in_sb", [P, KD, NIN], F32) as w_in_sb:
                shared.update(w_in_sb=w_in_sb)
                phase(modulation, **shared)
                phase(projection, **shared)
            with nc.sbuf_tensor("cols", [P, NT + 1, P], F32) as cols, \
                 nc.sbuf_tensor("bm_rows", [HM, TT], F32) as bm_rows, \
                 nc.sbuf_tensor("carry_all", [P, HM, NT + NB], F32) as carry_all:
                shared.update(cols=cols, bm_rows=bm_rows, carry_all=carry_all)
                phase(gates, **shared)
                phase(prompt_mix, **shared)
                with nc.sbuf_tensor("hcat_s", [P, D], F32) as hcat_s:
                    phase(sample_mlstm, hcat_s=hcat_s, **shared)
                    phase(sample_attention, hcat_s=hcat_s, **shared)
        phase(experts, **shared)


def modulation(nc, io, sem, pool_dma_sem, signal, reached, prime, mod_d, ident, w_in_sb, w_in_loaded, **_):
    NC_, CH = 6 * D // 512, 512
    NBUF = 3
    with ExitStack() as ctx:
        sb = lambda n, s, d=F32: ctx.enter_context(nc.sbuf_tensor(n, s, d))
        ps = lambda n, s, d=F32: ctx.enter_context(nc.psum_tensor(n, s, d))
        R = 1 + NB
        c_rows = sb("c_rows", [R, D])
        e_rows = sb("e_rows", [R, D])
        silu_c = sb("silu_c", [R, D])
        c_cols = sb("c_cols", [P, KD, R])
        w_ada = sb("w_ada", [P, NBUF, KD, CH])
        b_rows = sb("b_rows", [R, 2, CH])
        g_rows = sb("g_rows", [R, 2, CH])
        mod_rows = sb("mod_rows", [R, 2, CH])
        ps_c = ps("ps_c", [P, KD, 16])
        ps_m = ps("ps_m", [P, 2, CH])
        c_in, w_in = sem("c_in"), [sem(f"w_ada_in{i}") for i in range(NBUF)]
        b_in = [pool_dma_sem(f"b_ada_in{i}") for i in range(2)]
        ident_done, silu_step, c_turned, c_copied = sem("ident_done"), sem("silu_step"), sem("c_turned"), sem("c_copied")
        mod_summed, mod_added, mod_stored = sem("mod_summed"), sem("mod_added"), [pool_dma_sem(f"mod_stored{i}") for i in range(2)]

        gains = {2: io["norm_mix_g"], 3: io["norm_mix_g"], 8: io["norm_ffn_g"], 9: io["norm_ffn_g"]}
        block = ctx.enter_context(nc.Block())

        @block.sync
        def _(sp):
            sp.dma_start(c_rows[0:1, :], io["c_prompt"]).then_inc(c_in, 16)
            sp.dma_start(c_rows[1:R, :], io["c_sample"]).then_inc(c_in, 16)
            for n in range(NC_):
                if n >= NBUF:
                    sp.wait_ge(mod_summed, n - NBUF + 1)
                sp.dma_start(w_ada[:, n % NBUF], io["w_ada"][0, :, n * CH:(n + 1) * CH]
                             .rearrange("(k p) n -> p k n", p=P)).then_inc(w_in[n % NBUF], 16)
            sp.dma_start(w_in_sb[:, :, :], io["w_in"][0].rearrange("(k p) n -> p k n", p=P)).then_inc(w_in_loaded, 16)

        def store_mod(eng, n):
            eng.wait_ge(mod_added, n + 1)
            eng.dma_start(mod_d[:, n * CH:(n + 1) * CH], mod_rows[:, n % 2, :]).then_inc(mod_stored[n % 2], 16)

        @block.gpsimd
        def _(pool):
            pool.memset(ident[:, :], 0.0).then_inc(ident_done, 1)
            pool.wait_ge(ident_done, 1)
            pool.affine_select(out=ident[:, :], in_=ident[:, :], compare_op=ALU.not_equal, fill=1.0, base=0,
                               pattern=[[-1, P]], channel_multiplier=1).then_inc(ident_done, 1)
            for n in range(NC_):
                if n >= 2:
                    pool.wait_ge(mod_added, n - 1)
                bias = io["b_ada"][0:1, n * CH:(n + 1) * CH].broadcast_to([R, CH])
                pool.dma_start(b_rows[:, n % 2, :], bias).then_inc(b_in[n % 2], 16)
                if n in gains:
                    c0 = (n % 2) * CH
                    pool.dma_start(g_rows[:, n % 2, :], gains[n][0:1, c0:c0 + CH].broadcast_to([R, CH])).then_inc(b_in[n % 2], 16)
                if n >= 1:
                    store_mod(pool, n - 1)
            store_mod(pool, NC_ - 1)
            pool.wait_ge(mod_stored[0], 16 * NC_ // 2)
            pool.wait_ge(mod_stored[1], 16 * NC_ // 2)

        @block.scalar
        def _(act):
            act.preload_act_table_set(EXP_LN)
            act.wait_ge(silu_step, 1)
            act.activation(e_rows[:, :], silu_c[:, :], ACT.Exp, scale=-1.0).then_inc(silu_step, 1)

        @block.vector
        def _(dve):
            dve.wait_ge(c_in, 32)
            dve.tensor_scalar(silu_c[:, :], c_rows[:, :], -80.0, None, ALU.max).then_inc(silu_step, 1)
            dve.wait_ge(silu_step, 2)
            dve.tensor_scalar(e_rows[:, :], e_rows[:, :], 1.0, None, ALU.add)
            dve.drain()
            dve.reciprocal(e_rows[:, :], e_rows[:, :])
            dve.drain()
            dve.tensor_tensor(silu_c[:, :], c_rows[:, :], e_rows[:, :], ALU.mult).then_inc(silu_step, 1)
            dve.wait_ge(c_turned, 1)
            dve.tensor_copy(c_cols[:, :, :], ps_c[:, :, 0:R]).then_inc(c_copied, 1)
            rows_in = [0, 0]
            for n in range(NC_):
                rows_in[n % 2] += 16 + 16 * (n in gains)
                dve.wait_ge(b_in[n % 2], rows_in[n % 2])
                dve.wait_ge(mod_summed, n + 1)
                if n >= 2:
                    dve.wait_ge(mod_stored[n % 2], 16 * (n // 2))
                out = mod_rows[:, n % 2, :]
                ins = dve.tensor_tensor(out, ps_m[0:R, n % 2, :], b_rows[:, n % 2, :], ALU.add)
                if n in gains:
                    dve.drain()
                    ins = dve.scalar_tensor_tensor(out=out, in0=out, scalar=1.0, in1=g_rows[:, n % 2, :],
                                                   op0=ALU.add, op1=ALU.mult)
                ins.then_inc(mod_added, 1)

        @block.tensor
        def _(pe):
            pe.wait_ge(ident_done, 2)
            pe.wait_ge(silu_step, 3)
            for k in range(KD):
                t = pe.transpose(ps_c[:, k, 0:R], silu_c[:, k * P:(k + 1) * P], ident[0:R, 0:R])
            t.then_inc(c_turned, 1)
            pe.wait_ge(c_copied, 1)
            for n in range(NC_):
                pe.wait_ge(w_in[n % NBUF], 16 * (n // NBUF + 1))
                if n >= 2:
                    pe.wait_ge(mod_added, n - 1)
                for k in range(KD):
                    m = pe.matmul(ps_m[0:R, n % 2, :], c_cols[:, k, :], w_ada[:, n % NBUF, k, :], start=k == 0, stop=k == KD - 1)
                m.then_inc(mod_summed, 1)


def load_rows(eng, dst, mod_d, col, sample):
    if sample:
        src = mod_d[1:1 + NB, col:col + D].unsqueeze(1).broadcast_to([NB, SQ, D])
    else:
        src = mod_d[0:1, col:col + D].broadcast_to([P, D])
    return eng.dma_start(dst, src)


def projection(nc, io, sem, signal, reached, prime, mod_d, mix_d, sq_d, ident, w_in_sb, w_in_loaded, gate_rows, **_):
    with ExitStack() as ctx:
        sb = lambda n, s, d=F32: ctx.enter_context(nc.sbuf_tensor(n, s, d))
        ps = lambda n, s, d=F32: ctx.enter_context(nc.psum_tensor(n, s, d))
        x = sb("x", [P, D])
        gain, shift = sb("gain", [P, D]), sb("shift", [P, D])
        h = sb("h", [P, D])
        hT = sb("hT", [P, 2, KD, P])
        stage = sb("stage", [P, 7, 512])
        sq_g, sk_g, hm_g = sb("sq_g", [P, WS]), sb("sk_g", [P, WS]), sb("hm_g", [P, WM])
        b_gate = sb("b_gate", [P, 2 * HM])
        square = sb("square", [P, 2, 512])
        og = sb("og", [P, 512])
        ssq, ssh = sb("ssq", [P, 1]), sb("ssh", [P, 2, HS])
        rstd, rsh = sb("rstd", [P, 1]), sb("rsh", [P, 2, HS])
        gt = sb("gt", [P, 4, 2 * HM])
        ps_t = ps("ps_t", [P, KD, P])
        ps_p = [ps(f"ps_p{i}", [P, 512]) for i in range(4)]
        ps_g = ps("ps_g", [P, 512])
        ps_r = ps("ps_r", [HM, 2, P])

        S0 = 4 * WM + 2 * HM
        starts = [S0, S0 + WS, S0 + 2 * WS, 0, WM, 2 * WM, 3 * WM]
        consts_in, mods_in = sem("consts_in"), sem("mods_in")
        x_in, x_free = signal("x_in", 16), signal("x_free", 1, 1)
        ssq_done, rstd_done, h_done = signal("ssq_done"), signal("rstd_done"), signal("h_done")
        h_turned, hT_act, hT_dve = signal("h_turned"), signal("hT_act"), signal("hT_dve")
        proj = signal("proj", 8, 1)
        read_act, read_dve = signal("read_act", 4, 1), signal("read_dve", 3, 1)
        gate_a, gate_v, gate_t, gate_c = signal("gate_a", 2), signal("gate_v", 3), signal("gate_t"), signal("gate_c")
        head_a, head_v = signal("head_a", 4), signal("head_v", 2)
        og_v, og_a = signal("og_v"), signal("og_a")
        staged_dve = signal("staged_dve", 3)
        stored = signal("stored", 16 * 7, 1)
        block = ctx.enter_context(nc.Block())

        def tiles(eng, tile):
            with eng.Fori(0, NT // 2) as pair:
                tile(pair * 2, 0)
                tile(pair * 2 + 1, 1)
            tile(NT, 0, more=False)

        @block.sync
        def _(sp):
            prime(sp, stored)
            for dst, src, w in ((sq_g, "qnorm_g", WS), (sk_g, "knorm_g", WS), (hm_g, "mlstm_head_g", WM)):
                sp.dma_start(dst[:, :], io[src].rearrange("a h d -> a (h d)").broadcast_to([P, w])).then_inc(consts_in, 16)
            sp.dma_start(b_gate[:, :], io["b_gates"].broadcast_to([P, 2 * HM])).then_inc(consts_in, 16)
            load_rows(sp, gain[:, :], mod_d, D, False).then_inc(mods_in, 16)
            load_rows(sp, shift[:, :], mod_d, 0, False).then_inc(mods_in, 16)

            def load(k, sample):
                reached(sp, x_free, x_free.ago(k))
                if sample:
                    load_rows(sp, gain[0:NS, :], mod_d, D, True).then_inc(mods_in, 16)
                    load_rows(sp, shift[0:NS, :], mod_d, 0, True).then_inc(mods_in, 16)
                    sp.wait_ge(mods_in, 64)
                    sp.dma_start(x[0:NS, :], io["x_sample"].rearrange("b q d -> (b q) d")).then_inc(x_in.sem, 16)
                else:
                    sp.dma_start(x[:, :], io["x_prompt"][0, ds(k * P, P), :]).then_inc(x_in.sem, 16)

            def store(k, sample):
                rows = NS if sample else P
                flat = lambda a: a.rearrange("a b t h d -> (a b t) (h d)")
                out_at, here = (ds(0, rows) if sample else ds(k * P, rows)), ds(k * P, rows)
                dst = [sq_d[here, :], flat(io["k_sample" if sample else "k_prompt"])[out_at, :],
                       flat(io["v_sample" if sample else "v_prompt"])[out_at, :]]
                dst += [mix_d[here, j * WM:(j + 1) * WM] for j in range(4)]
                for n, (sig, rise) in enumerate([(staged_dve, 1), (staged_dve, 2), (read_act, 1), (read_act, 2),
                                                 (read_act, 3), (read_act, 4), (staged_dve, 3)]):
                    reached(sp, sig, sig.at(k, rise))
                    sp.dma_start(dst[n], stage[0:rows, n, :]).then_inc(stored.sem, 16)

            load(0, False)
            with sp.Fori(0, NT - 1) as k:
                load(k + 1, False)
                store(k, False)
            load(NT, True)
            store(NT - 1, False)
            store(NT, True)
            sp.wait_ge(stored.sem, stored.at(NT))

        @block.tensor
        def _(pe):
            prime(pe, proj)
            pe.wait_ge(w_in_loaded, 16)

            def turn(k):
                reached(pe, h_done, h_done.at(k))
                for j in range(KD):
                    t = pe.transpose(ps_t[:, j, :], h[:, j * P:(j + 1) * P], ident[:, :])
                t.then_inc(h_turned.sem, 1)

            def tile(k, b, more=True):
                reached(pe, hT_act, hT_act.at(k))
                reached(pe, hT_dve, hT_dve.at(k))
                for j in range(KD):
                    m = pe.matmul(ps_g[:, 0:2 * HM], hT[:, b, j, :], w_in_sb[:, j, 4 * WM:4 * WM + 2 * HM], start=j == 0, stop=j == KD - 1)
                m.then_inc(proj.sem, 1)
                bank_free = [(read_act, read_act.ago(k, 3)), (read_act, read_act.ago(k, 4)),
                             (read_dve, read_dve.ago(k, 3)), (read_act, read_act.ago(k, 2)),
                             (read_dve, read_dve.at(k, 1)), (read_dve, read_dve.at(k, 2)), (read_act, read_act.at(k, 1))]
                for n, c0 in enumerate(starts):
                    reached(pe, *bank_free[n])
                    for j in range(KD):
                        m = pe.matmul(ps_p[n % 4][:, :], hT[:, b, j, :], w_in_sb[:, j, c0:c0 + 512], start=j == 0, stop=j == KD - 1)
                    m.then_inc(proj.sem, 1)
                    if n == 0:
                        reached(pe, gate_v, gate_v.at(k, 3))
                        for r in range(2):
                            t = pe.transpose(ps_r[:, r, :], gt[:, 3, r * HM:(r + 1) * HM], ident[:, :])
                        t.then_inc(gate_t.sem, 1)
                    if n == 4 and more:
                        turn(k + 1)

            turn(0)
            tiles(pe, tile)

        @block.scalar
        def _(act):
            act.preload_act_table_set(EXP_LN)
            prime(act, read_act)

            def norm(k):
                reached(act, ssq_done, ssq_done.at(k))
                act.activation(rstd[:, :], ssq[:, :], ACT.Ln, scale=1.0 / D, bias=EPS)
                act.drain()
                act.activation(rstd[:, :], rstd[:, :], ACT.Exp, scale=-0.5).then_inc(rstd_done.sem, 1)

            def head_norm(k, w):
                reached(act, proj, proj.at(k, 2 + w))
                act.activation(square[:, w, :], ps_p[w][:, :], ACT.Square).then_inc(head_a.sem, 1)
                reached(act, head_v, head_v.at(k, w + 1))
                act.activation(rsh[:, w, :], ssh[:, w, :], ACT.Ln, scale=1.0 / DS, bias=EPS)
                act.drain()
                act.activation(rsh[:, w, :], rsh[:, w, :], ACT.Exp, scale=-0.5).then_inc(head_a.sem, 1)

            def keep_turned(k, b):
                reached(act, h_turned, h_turned.at(k))
                act.activation(hT[:, b, 0:KD // 2, :], ps_t[:, 0:KD // 2, :], ACT.Copy).then_inc(hT_act.sem, 1)

            def tile(k, b, more=True):
                reached(act, gate_v, gate_v.at(k, 1))
                act.activation(gt[:, 1, :], gt[:, 0, :], ACT.Exp, scale=2.0 / CAP).then_inc(gate_a.sem, 1)
                reached(act, gate_v, gate_v.at(k, 2))
                act.activation(gt[:, 1, :], gt[:, 2, :], ACT.Exp, scale=-1.0)
                act.drain()
                act.activation(gt[:, 1, :], gt[:, 1, :], ACT.Ln, bias=1.0).then_inc(gate_a.sem, 1)
                head_norm(k, 0)
                head_norm(k, 1)
                if more:
                    norm(k + 1)
                reached(act, stored, stored.ago(k))
                for n in (2, 3, 4, 5):
                    reached(act, proj, proj.at(k, 2 + n))
                    scale = DM ** -0.5 if n == 4 else 1.0
                    act.activation(stage[:, n, :], ps_p[n % 4][:, :], ACT.Copy, scale=scale).then_inc(read_act.sem, 1)
                    if n == 4 and more:
                        keep_turned(k + 1, 1 - b)
                reached(act, og_v, og_v.at(k))
                act.activation(og[:, :], og[:, :], ACT.Exp, scale=-1.0).then_inc(og_a.sem, 1)

            norm(0)
            keep_turned(0, 0)
            tiles(act, tile)

        @block.vector
        def _(dve):
            prime(dve, x_free, read_dve)
            dve.wait_ge(consts_in, 64)

            def norm(k):
                reached(dve, x_in, x_in.at(k))
                dve.wait_ge(mods_in, 32)
                dve.tensor_tensor_reduce(h[:, :], x[:, :], x[:, :], 1.0, 0.0, ALU.mult, ALU.add, ssq[:, :]).then_inc(ssq_done.sem, 1)
                reached(dve, rstd_done, rstd_done.at(k))
                dve.drain()
                dve.scalar_tensor_tensor(out=h[:, :], in0=x[:, :], scalar=rstd[:, 0:1], in1=gain[:, :], op0=ALU.mult, op1=ALU.mult)
                dve.drain()
                dve.tensor_tensor(h[:, :], h[:, :], shift[:, :], ALU.add).then_inc(h_done.sem, 1)
                dve.drain()
                dve.sem_inc(x_free.sem, 1)

            def head_norm(k, w, g):
                reached(dve, head_a, head_a.at(k, 2 * w + 1))
                dve.tensor_reduce(ssh[:, w, :], square[:, w, :].rearrange("p (h d) -> p h d", h=HS), AX.X, ALU.add).then_inc(head_v.sem, 1)
                reached(dve, head_a, head_a.at(k, 2 * w + 2))
                v = stage[:, w, :].rearrange("p (h d) -> p h d", h=HS)
                dve.tensor_tensor(v, ps_p[w][:, :].rearrange("p (h d) -> p h d", h=HS),
                                  rsh[:, w, :].unsqueeze(2).broadcast_to([P, HS, DS]), ALU.mult).then_inc(read_dve.sem, 1)
                dve.drain()
                dve.tensor_tensor(stage[:, w, :], stage[:, w, :], g[:, :], ALU.mult).then_inc(staged_dve.sem, 1)

            def keep_turned(k, b):
                reached(dve, h_turned, h_turned.at(k))
                dve.tensor_copy(hT[:, b, KD // 2:KD, :], ps_t[:, KD // 2:KD, :]).then_inc(hT_dve.sem, 1)

            def tile(k, b, more=True):
                reached(dve, proj, proj.at(k, 1))
                dve.tensor_tensor(gt[:, 0, :], ps_g[:, 0:2 * HM], b_gate[:, :], ALU.add)
                dve.drain()
                dve.tensor_scalar(gt[:, 0, :], gt[:, 0, :], -30.0 * CAP, 30.0 * CAP, ALU.max, ALU.min).then_inc(gate_v.sem, 1)
                reached(dve, gate_a, gate_a.at(k, 1))
                dve.tensor_scalar(gt[:, 2, :], gt[:, 1, :], 1.0, None, ALU.add)
                dve.drain()
                dve.reciprocal(gt[:, 2, :], gt[:, 2, :])
                dve.drain()
                dve.tensor_scalar(gt[:, 2, :], gt[:, 2, :], -2.0 * CAP, CAP, ALU.mult, ALU.add).then_inc(gate_v.sem, 1)
                reached(dve, gate_a, gate_a.at(k, 2))
                dve.drain()
                dve.tensor_copy(gt[:, 3, 0:HM], gt[:, 2, 0:HM])
                dve.tensor_scalar(gt[:, 3, HM:2 * HM], gt[:, 1, HM:2 * HM], -1.0, None, ALU.mult)
                dve.drain()
                dve.sem_inc(gate_v.sem, 1)
                reached(dve, stored, stored.ago(k))
                head_norm(k, 0, sq_g)
                head_norm(k, 1, sk_g)
                reached(dve, gate_t, gate_t.at(k))
                width = P if more else NS
                dve.tensor_copy(gate_rows[:, :, ds(k * P, width)], ps_r[:, :, 0:width]).then_inc(gate_c.sem, 1)
                if more:
                    norm(k + 1)
                    keep_turned(k + 1, 1 - b)
                reached(dve, proj, proj.at(k, 8))
                dve.tensor_scalar(og[:, :], ps_p[6 % 4][:, :], -80.0, None, ALU.max).then_inc(og_v.sem, 1)
                dve.drain()
                dve.sem_inc(read_dve.sem, 1)
                reached(dve, og_a, og_a.at(k))
                dve.tensor_scalar(og[:, :], og[:, :], 1.0, None, ALU.add)
                dve.drain()
                dve.reciprocal(og[:, :], og[:, :])
                dve.drain()
                dve.tensor_tensor(stage[:, 6, :], og[:, :], hm_g[:, :], ALU.mult).then_inc(staged_dve.sem, 1)
                dve.drain()

            norm(0)
            keep_turned(0, 0)
            tiles(dve, tile)


def gates(nc, io, sem, signal, reached, ident, gate_rows, cols, bm_rows, carry_all, sel_head, **_):
    NCH = NT + NB
    with ExitStack() as ctx:
        sb = lambda n, s, d=F32: ctx.enter_context(nc.sbuf_tensor(n, s, d))
        ps = lambda n, s, d=F32: ctx.enter_context(nc.psum_tensor(n, s, d))
        go_on = sb("go_on", [HM, TT])
        b_row, m_row = sb("b_row", [HM, TT]), sb("m_row", [HM, TT])
        m_start = sb("m_start", [HM, NB])
        m_before, bm_end, carry = sb("m_before", [HM, NCH]), sb("bm_end", [HM, NCH]), sb("carry", [HM, NCH])
        fi = sb("fi", [HM, 2, NS])
        kinds = sb("kinds", [P, TT])
        ps_k = [ps(f"ps_k{i}", [P, 4, P]) for i in range(3)]
        ps_y = ps("ps_y", [P, HM, NCH])
        ready, m_in, rows_out, sel_made = sem("g_ready"), sem("m_in"), sem("rows_out"), sem("sel_made")
        stepped, exped, turned, m_out = sem("g_stepped"), sem("g_exped"), sem("g_turned"), sem("m_out")
        prompt = lambda a: a[:, 0:SEQ].rearrange("p (c t) -> p c t", t=P)
        sample = lambda a: a[:, SEQ:TT].rearrange("p (c t) -> p c t", t=SQ)
        block = ctx.enter_context(nc.Block())

        @block.sync
        def _(sp):
            sp.dma_start(m_start[:, :], io["state_mlstm_m"].rearrange("a b h -> h (a b)"), allow_slow_non_contiguous=True).then_inc(m_in, 16)
            sp.wait_ge(stepped, 1)
            sp.dma_start(io["m_prompt"].rearrange("a b h -> h (a b)"), m_row[:, SEQ - 1:SEQ], allow_slow_non_contiguous=True).then_inc(m_out, 16)
            sp.dma_start(io["m_sample"].rearrange("a b h -> h (a b)"), sample(m_row)[:, :, SQ - 1], allow_slow_non_contiguous=True).then_inc(m_out, 16)
            sp.wait_ge(m_out, 32)

        @block.gpsimd
        def _(pool):
            pool.memset(sel_head[:, :, :], 0.0).then_inc(sel_made, 1)
            pool.wait_ge(sel_made, 1)
            pool.affine_select(out=sel_head[:, :, :], in_=sel_head[:, :, :], compare_op=ALU.not_equal, fill=1.0, base=0,
                               pattern=[[-1, HM], [0, P]], channel_multiplier=1).then_inc(sel_made, 1)

        @block.vector
        def _(dve):
            i_row, f_row = gate_rows[:, 0, :], gate_rows[:, 1, :]
            dve.memset(kinds[:, :], 0.0)
            dve.memset(go_on[:, :], 1.0)
            dve.memset(m_before[:, 0:1], 0.0)
            dve.drain()
            dve.memset(prompt(go_on)[:, :, 0], 0.0)
            dve.memset(sample(go_on)[:, :, 0], 0.0)
            dve.drain()
            dve.tensor_tensor_scan(b_row[:, :], go_on[:, :], f_row, 0.0, ALU.mult, ALU.add)
            dve.tensor_tensor_scan(m_row[:, 0:SEQ], f_row[:, 0:SEQ], i_row[:, 0:SEQ], 0.0, ALU.add, ALU.max)
            dve.tensor_copy(fi[:, :, :], gate_rows[:, :, SEQ:TT])
            dve.drain()
            dve.wait_ge(m_in, 16)
            first = lambda r: fi[:, r, :].rearrange("p (c t) -> p c t", t=SQ)[:, :, 0]
            dve.tensor_tensor(first(0), first(1), m_start[:, :], ALU.add)
            dve.drain()
            dve.tensor_tensor(first(0), first(0), sample(gate_rows[:, 0, :])[:, :, 0], ALU.max)
            dve.memset(first(1), HIDE)
            dve.drain()
            dve.tensor_tensor_scan(m_row[:, SEQ:TT], fi[:, 1, :], fi[:, 0, :], 0.0, ALU.add, ALU.max)
            dve.drain()
            dve.tensor_tensor(bm_rows[:, :], b_row[:, :], m_row[:, :], ALU.subtract).then_inc(stepped, 1)
            dve.tensor_tensor(kinds[0:HM, :], i_row, b_row[:, :], ALU.subtract)
            dve.tensor_copy(m_before[:, 1:NT], prompt(m_row)[:, 0:NT - 1, P - 1])
            dve.tensor_copy(m_before[:, NT:NCH], m_start[:, :])
            dve.drain()
            dve.tensor_copy(bm_end[:, 0:NT], prompt(bm_rows)[:, :, P - 1])
            dve.tensor_copy(bm_end[:, NT:NCH], sample(bm_rows)[:, :, SQ - 1])
            dve.drain()
            dve.tensor_tensor(carry[:, :], bm_end[:, :], m_before[:, :], ALU.add)
            for view, c0, c1, t in ((prompt, 0, NT, P), (sample, NT, NCH, SQ)):
                wide = lambda a: a[:, c0:c1].unsqueeze(2).broadcast_to([HM, c1 - c0, t])
                dve.tensor_tensor(view(kinds[32:32 + HM, :]), view(bm_rows), wide(m_before), ALU.add)
                dve.tensor_tensor(view(kinds[96:96 + HM, :]), view(kinds[0:HM, :]), wide(bm_end), ALU.add)
            dve.drain()
            dve.sem_inc(stepped, 1)
            dve.wait_ge(turned, 1)
            for n in range(3):
                w, r = (4, P) if n < 2 else (1, NS)
                dve.tensor_copy(cols[0:r, 4 * n:4 * n + w, :], ps_k[n][0:r, 0:w, :])
            dve.tensor_copy(carry_all[:, :, :], ps_y[:, :, :])

        @block.scalar
        def _(act):
            act.preload_act_table_set(EXP_LN)
            act.wait_ge(stepped, 2)
            act.activation(kinds[32:32 + HM, :], kinds[32:32 + HM, :], ACT.Exp)
            act.activation(kinds[64:64 + HM, :], m_row[:, :], ACT.Exp, scale=-1.0)
            act.activation(kinds[96:96 + HM, :], kinds[96:96 + HM, :], ACT.Exp)
            act.activation(carry[:, :], carry[:, :], ACT.Exp)
            act.drain()
            act.sem_inc(exped, 1)

        @block.tensor
        def _(pe):
            pe.wait_ge(exped, 1)
            pe.wait_ge(sel_made, 2)
            for n in range(NT + 1):
                w = P if n < NT else NS
                pe.transpose(ps_k[n // 4][0:w, n % 4, :], kinds[:, n * P:n * P + w], ident[:, :])
            for h in range(HM):
                t = pe.matmul(ps_y[:, h, :], sel_head[:, h, :], carry[:, :], start=True, stop=True)
            t.then_inc(turned, 1)


def prompt_mix(nc, io, sem, signal, reached, prime, mod_d, mix_d, sq_d, x1_d, ident, cols, bm_rows, carry_all,
               sel_head, **_):
    V1 = DM + 1
    with ExitStack() as ctx:
        sb = lambda n, s, d=F32: ctx.enter_context(nc.sbuf_tensor(n, s, d))
        ps = lambda n, s, d=F32: ctx.enter_context(nc.psum_tensor(n, s, d))
        w_out = sb("w_out_sb", [P, KD, D])
        gate_a = sb("gate_a_rows", [P, D])
        sb_bias = sb("sb_bias_sb", [P, HS])
        ident_h = sb("ident_h", [P, P], BF16)
        hide = sb("hide", [P, 3 * P], BF16)
        after = sb("after", [P, P])
        KT = sb("KT", [P, HS // 2, SEQ])
        V = sb("V", [P, NT, WS])
        mx = sb("mx", [P, 4, WM])
        v1 = sb("v1", [P, HM, V1])
        vd = sb("vd", [P, HM, V1])
        sq = sb("sq", [P, WS])
        qkT = sb("qkT", [P, 2 * HM, P])
        QT = sb("QT", [P, HS // 2, P])
        colt, carry_t = sb("colt", [P, P]), sb("carry_t", [P, HM])
        wt, sw = sb("wt", [P, HM, P]), sb("sw", [P, HM, P])
        num = sb("num", [P, HM, V1])
        Cn = sb("Cn", [P, HM, V1])
        den, ssq, fac = sb("den", [P, 2, HM]), sb("m_ssq", [P, HM]), sb("fac", [P, HM])
        junk = sb("junk", [P, P])
        lz, zb, cum = sb("lz", [P, 2, SEQ]), sb("zb", [P, 2, SEQ]), sb("cum", [P, SEQ])
        A, AT = sb("A", [P, 2, SEQ]), sb("AT", [P, 2, NT, P])
        hcat, hcT = sb("hcat", [P, D]), sb("hcT", [P, KD, P])
        xr, xy = sb("xr", [P, D]), sb("xy", [P, D])
        one = sb("one", [P, 1])
        psZ, psA, psC = ps("psZ", [P, SEQ]), ps("psA", [P, SEQ]), ps("psC", [P, SEQ])
        psO, psE = ps("psO", [P, 512]), ps("psE", [P, 512])
        v1_of = lambda a, h: a[:, (h // 2) * 512 + (h % 2) * V1:(h // 2) * 512 + (h % 2) * V1 + V1]

        wo_in, const_in, kv_in = sem("wo_in"), sem("mix_const_in"), sem("kv_in")
        masks, k_turned, k_copied, zeroed = sem("masks"), sem("k_turned"), sem("k_copied"), sem("zeroed")
        mix_in, mix_free = signal("mix_in", 48), signal("mix_free", 1, 1)
        colt_set = signal("colt_set")
        t_qk, c_qk_a, c_qk_v = signal("t_qk"), signal("c_qk_a"), signal("c_qk_v")
        t_sq, c_sq = signal("t_sq"), signal("c_sq")
        bm_out, w_sum, w_exp = signal("bm_out"), signal("w_sum"), signal("w_exp")
        s_out, s_w = signal("s_out"), signal("s_w")
        inter_out, inter_used, intra_out = signal("inter_out"), signal("inter_used"), signal("intra_out")
        num_done, den_done, sq_done, rs_done = signal("num_done"), signal("den_done"), signal("sq_done"), signal("rs_done")
        hm_done, vd_done, up_out, state_done = signal("hm_done"), signal("vd_done"), signal("up_out"), signal("state_done", 1, 1)
        z_out, z_lin, l_done, l_used = (signal("z_out", HS), signal("z_lin", HS), signal("l_done", HS),
                                        signal("l_used", HS, 1))
        xr_in = signal("xr_in", 16)
        d_done, a_done, at_out, at_act, at_dve, av_out = (signal("d_done", HS), signal("a_done", HS), signal("at_out", HS),
                                                          signal("at_act", HS), signal("at_dve", HS), signal("av_out", HS))
        hs_done, t_hc, hc_act, hc_dve = signal("hs_done"), signal("t_hc"), signal("hc_act"), signal("hc_dve")
        y_out, x1_done, x1_stored = signal("y_out"), signal("x1_done", 1, 1), signal("x1_stored", 16, 1)
        c_turned, c_ready, state_stored = sem("C_turned"), sem("C_ready"), sem("state_stored")
        block = ctx.enter_context(nc.Block())
        flat = lambda a: a.rearrange("a b t h d -> (a b t) (h d)")
        key_bufs = (lz[:, 0, :], lz[:, 1, :], zb[:, 0, :], zb[:, 1, :])

        def tiles(eng, tile, project):
            tile(0, P, True)
            tile(1, 2 * P, False)
            for k in range(2, NT, 2):
                with eng.Fori(k, k + 2) as kk:
                    tile(kk, (k + 2) * P, False)
            for slot in range(4, 8):
                project(NT - 1, slot)

        @block.sync
        def _(sp):
            prime(sp, x1_stored)
            sp.dma_start(V[:, :, :], flat(io["v_prompt"]).rearrange("(j p) n -> p j n", p=P)).then_inc(kv_in, 16)
            for n, buf in enumerate(key_bufs):
                sp.dma_start(buf.rearrange("p (j n) -> p j n", j=2),
                             flat(io["k_prompt"])[n * 2 * P:(n + 1) * 2 * P, :].rearrange("(j p) n -> p j n", p=P)).then_inc(kv_in, 16)
            load_rows(sp, gate_a[:, :], mod_d, 2 * D, False).then_inc(const_in, 16)
            sp.dma_start(sb_bias[:, :], io["sb_bias"].broadcast_to([P, HS])).then_inc(const_in, 16)

            def load(k):
                reached(sp, mix_free, mix_free.ago(k))
                sp.dma_start(mx[:, :, :], mix_d[ds(k * P, P), :].rearrange("p (j n) -> p j n", j=4)).then_inc(mix_in.sem, 16)
                sp.dma_start(sq[:, :], sq_d[ds(k * P, P), :]).then_inc(mix_in.sem, 16)
                sp.dma_start(v1[:, :, 0:DM], mix_d[ds(k * P, P), 2 * WM:3 * WM].rearrange("p (h n) -> p h n", h=HM)).then_inc(mix_in.sem, 16)

            def load_x(k):
                reached(sp, x1_stored, x1_stored.ago(k))
                sp.dma_start(xr[:, :], io["x_prompt"][0, ds(k * P, P), :]).then_inc(xr_in.sem, 16)

            def store(k):
                reached(sp, x1_done, x1_done.at(k))
                sp.dma_start(x1_d[ds(k * P, P), :], xr[:, :]).then_inc(x1_stored.sem, 16)

            sp.wait_ge(zeroed, 1)
            load(0)
            sp.dma_start(w_out[:, :, :], io["w_out"][0].rearrange("(k p) n -> p k n", p=P)).then_inc(wo_in, 16)
            load(1)
            load_x(0)
            with sp.Fori(1, NT - 1) as k:
                load(k + 1)
                store(k - 1)
                load_x(k)
            store(NT - 2)
            load_x(NT - 1)
            store(NT - 1)
            sp.wait_ge(c_ready, 1)
            sp.dma_start(io["C_prompt"].rearrange("a b h v k -> v (a b h) k"), wt[:, :, :]).then_inc(state_stored, 16)
            sp.dma_start(io["n_prompt"].rearrange("a b h k -> k (a b h)"), Cn[:, :, DM], allow_slow_non_contiguous=True).then_inc(state_stored, 16)
            sp.wait_ge(state_stored, 32)
            sp.wait_ge(x1_stored.sem, x1_stored.at(NT - 1))

        @block.gpsimd
        def _(pool):
            pool.memset(hide[:, :], 0.0)
            pool.memset(after[:, :], 0.0)
            pool.memset(ident_h[:, :], 0.0).then_inc(masks, 1)
            pool.drain()
            pool.affine_select(out=hide[:, :], in_=hide[:, :], compare_op=ALU.is_gt, fill=HIDE, base=P,
                               pattern=[[-1, 3 * P]], channel_multiplier=1)
            pool.affine_select(out=after[:, :], in_=after[:, :], compare_op=ALU.is_ge, fill=HIDE, base=0,
                               pattern=[[1, P]], channel_multiplier=-1)
            pool.affine_select(out=ident_h[:, :], in_=ident_h[:, :], compare_op=ALU.not_equal, fill=1.0, base=0,
                               pattern=[[-1, P]], channel_multiplier=1)
            pool.drain()
            pool.sem_inc(masks, 1)

        @block.tensor
        def _(pe):
            pe.wait_ge(kv_in, 80)
            pe.wait_ge(masks, 2)
            banks = (psZ[:, 0:512], psZ[:, 512:1024], psA[:, 0:512], psA[:, 512:1024])
            n = 0
            for pair in range(HS // 2):
                for half in range(2):
                    if n >= 4:
                        pe.wait_ge(k_copied, n - 3)
                    for j in range(4):
                        t = half * 4 + j
                        buf = key_bufs[t // 2]
                        c0 = (t % 2) * WS + pair * P
                        ins = pe.transpose(banks[n % 4][:, j * P:(j + 1) * P], buf[:, c0:c0 + P], ident[:, :])
                    ins.then_inc(k_turned, 1)
                    n += 1
            pe.wait_ge(k_copied, 8)
            pe.wait_ge(zeroed, 1)

            def queries(k):
                reached(pe, mix_in, mix_in.at(k))
                for j in range(HS // 2):
                    t = pe.transpose(psE[:, j * P:(j + 1) * P], sq[:, j * P:(j + 1) * P], ident[:, :])
                t.then_inc(t_sq.sem, 1)

            def mlstm(k, slot):
                if slot == 0:
                    for j in range(2 * HM):
                        t = pe.transpose(psC[:, j * P:(j + 1) * P], mx[:, j // HM, (j % HM) * DM:(j % HM + 1) * DM], ident[:, :])
                    t.then_inc(t_qk.sem, 1)
                    for h in range(HM):
                        m = pe.matmul(psE[:, h * P:(h + 1) * P], sel_head[:, h, :], bm_rows[:, ds(k * P, P)], start=True, stop=True)
                    m.then_inc(bm_out.sem, 1)
                if slot == 1:
                    reached(pe, c_qk_a, c_qk_a.at(k))
                    reached(pe, c_qk_v, c_qk_v.at(k))
                    for h in range(HM):
                        m = pe.matmul(v1_of(psC, h), qkT[:, h, :], Cn[:, h, :], start=True, stop=True)
                    m.then_inc(inter_out.sem, 1)
                    reached(pe, w_sum, w_sum.at(k))
                    for h in range(HM):
                        m = pe.matmul(psE[:, h * P:(h + 1) * P], qkT[:, HM + h, :], qkT[:, h, :], start=True, stop=True)
                    m.then_inc(s_out.sem, 1)
                if slot == 2:
                    reached(pe, inter_used, inter_used.at(k))
                    reached(pe, s_w, s_w.at(k))
                    for h in range(HM):
                        m = pe.matmul(v1_of(psC, h), sw[:, h, :], v1[:, h, :], start=True, stop=True)
                    m.then_inc(intra_out.sem, 1)
                if slot == 3:
                    reached(pe, num_done, num_done.at(k))
                    reached(pe, vd_done, vd_done.at(k))
                    for h in range(HM):
                        m = pe.matmul(v1_of(psC, h), mx[:, 1, h * DM:(h + 1) * DM], vd[:, h, :], start=True, stop=True)
                    m.then_inc(up_out.sem, 1)

            def logits(k, w, h):
                at = slice((h % 2) * DS, (h % 2 + 1) * DS)
                if h == 0:
                    reached(pe, c_sq, c_sq.at(k))
                else:
                    reached(pe, z_lin, z_lin.at(k, h))
                near = max(w - 2 * P, 0)
                for c0 in range(0, w, 512):
                    c1 = min(c0 + 512, w)
                    m = pe.matmul(psZ[:, c0:c1], QT[at, h // 2, :], KT[at, h // 2, c0:c1], start=True, stop=near >= c1, skip_group_check=True)
                    if near < c1:
                        m = pe.matmul(psZ[:, near:w], ident_h[:, :], hide[:, ds(P + near - k * P, w - near)], start=False, stop=True,
                                      skip_group_check=True)
                m.then_inc(z_out.sem, 1)

            def turn(k, w, h):
                if h > 0:
                    reached(pe, at_act, at_act.at(k, h))
                    reached(pe, at_dve, at_dve.at(k, h))
                reached(pe, a_done, a_done.at(k, h + 1))
                for j in range(w // P):
                    t = pe.transpose(psA[:, j * P:(j + 1) * P], A[:, h % 2, j * P:(j + 1) * P], ident[:, :])
                t.then_inc(at_out.sem, 1)

            def weigh(k, w, h, first):
                reached(pe, at_act, at_act.at(k, h + 1))
                reached(pe, at_dve, at_dve.at(k, h + 1))
                if h == 0 and not first:
                    reached(pe, hs_done, hs_done.at(k - 1))
                for j in range(w // P):
                    m = pe.matmul(psO[:, h * DS:(h + 1) * DS], AT[:, h % 2, j, :], V[:, j, h * DS:(h + 1) * DS], start=j == 0, stop=j == w // P - 1)
                m.then_inc(av_out.sem, 1)

            def project(k, slot):
                if slot == 4:
                    reached(pe, x1_done, x1_done.at(k - 1))
                    reached(pe, hm_done, hm_done.at(k))
                    reached(pe, hs_done, hs_done.at(k))
                    for j in range(KD):
                        t = pe.transpose(psC[:, j * P:(j + 1) * P], hcat[:, j * P:(j + 1) * P], ident[:, :])
                    t.then_inc(t_hc.sem, 1)
                if slot in (5, 6):
                    pe.wait_ge(wo_in, 16)
                    reached(pe, hc_act, hc_act.at(k))
                    reached(pe, hc_dve, hc_dve.at(k))
                    c = slot - 5
                    for j in range(KD):
                        m = pe.matmul(psC[:, c * 512:(c + 1) * 512], hcT[:, j, :], w_out[:, j, c * 512:(c + 1) * 512], start=j == 0, stop=j == KD - 1)
                    if c == 1:
                        m.then_inc(y_out.sem, 1)

            def tile(k, w, first):
                queries(k)
                if not first:
                    reached(pe, x1_done, x1_done.at(k - 2))
                for s in range(HS + 3):
                    if s < HS:
                        logits(k, w, s)
                    mlstm(k, s)
                    if s == 4:
                        reached(pe, state_done, state_done.at(k))
                    if not first:
                        project(k - 1, s)
                    if 2 <= s < HS + 2:
                        turn(k, w, s - 2)
                    if s >= 3:
                        weigh(k, w, s - 3, first)

            tiles(pe, tile, project)
            for h in range(HM):
                t = pe.transpose(psE[:, h * P:(h + 1) * P], Cn[:, h, 0:DM], ident[:, :])
            t.then_inc(c_turned, 1)

        @block.scalar
        def _(act):
            act.preload_act_table_set(EXP_LN)
            act.wait_ge(const_in, 32)

            def mlstm(k, slot):
                if slot == 0:
                    reached(act, t_qk, t_qk.at(k))
                    act.activation(qkT[:, 0:HM, :], psC[:, 0:512].rearrange("p (h t) -> p h t", h=HM), ACT.Copy).then_inc(c_qk_a.sem, 1)
                if slot == 1:
                    reached(act, w_sum, w_sum.at(k))
                    act.activation(wt[:, :, :], wt[:, :, :], ACT.Exp).then_inc(w_exp.sem, 1)
                if slot == 4:
                    reached(act, den_done, den_done.at(k))
                    for h in range(HM):
                        act.activation(junk[:, :], num[:, h, 0:DM], ACT.Square, scale=den[:, 1, h:h + 1], accum_out=ssq[:, h:h + 1])
                        act.drain()
                    act.activation(ssq[:, :], ssq[:, :], ACT.Ln, scale=1.0 / DM, bias=EPS)
                    act.drain()
                    act.activation(ssq[:, :], ssq[:, :], ACT.Exp, scale=-0.5).then_inc(rs_done.sem, 1)

            def softplus(k, w, h):
                l = lz[:, h % 2, 0:w]
                reached(act, z_lin, z_lin.at(k, h + 1))
                reached(act, l_used, l_used.at(k, h + 1) - 2)
                act.activation(l, zb[:, h % 2, 0:w], ACT.Abs)
                act.drain()
                act.activation(l, l, ACT.Exp, scale=-1.0)
                act.drain()
                act.activation(l, l, ACT.Ln, bias=1.0).then_inc(l_done.sem, 1)

            def project(k, slot):
                if slot == 4:
                    reached(act, t_hc, t_hc.at(k))
                    act.activation(hcT[:, 0:KD // 2, :], psC[:, 0:512].rearrange("p (j t) -> p j t", t=P), ACT.Copy).then_inc(hc_act.sem, 1)

            def tile(k, w, first):
                reached(act, t_sq, t_sq.at(k))
                act.activation(QT[:, :, :], psE[:, :].rearrange("p (h t) -> p h t", h=HM), ACT.Copy).then_inc(c_sq.sem, 1)
                for s in range(HS + 3):
                    if s < HS:
                        softplus(k, w, s)
                    if 1 <= s <= HS:
                        a = A[:, (s - 1) % 2, 0:w]
                        reached(act, d_done, d_done.at(k, s))
                        act.activation(a, a, ACT.Exp).then_inc(a_done.sem, 1)
                    mlstm(k, s)
                    if not first:
                        project(k - 1, s)
                    if 2 <= s < HS + 2:
                        h, n = s - 2, min(w // P, 4)
                        reached(act, at_out, at_out.at(k, h + 1))
                        act.activation(AT[:, h % 2, 0:n, :], psA[:, 0:n * P].rearrange("p (j t) -> p j t", t=P), ACT.Copy).then_inc(at_act.sem, 1)
                reached(act, av_out, av_out.at(k))
                if not first:
                    reached(act, t_hc, t_hc.at(k - 1))
                act.activation(hcat[:, WM:D], psO[:, :], ACT.Copy).then_inc(hs_done.sem, 1)

            tiles(act, tile, project)
            act.wait_ge(c_turned, 1)
            act.activation(wt[:, :, :], psE[:, :].rearrange("p (h t) -> p h t", h=HM), ACT.Copy).then_inc(c_ready, 1)

        @block.vector
        def _(dve):
            prime(dve, mix_free, l_used, x1_done, state_done)
            for n in range(8):
                dve.wait_ge(k_turned, n + 1)
                bank = (psZ[:, 0:512], psZ[:, 512:1024], psA[:, 0:512], psA[:, 512:1024])[n % 4]
                dve.tensor_copy(KT[:, n // 2, (n % 2) * 512:(n % 2 + 1) * 512], bank).then_inc(k_copied, 1)
            dve.memset(Cn[:, :, :], 0.0)
            dve.memset(v1[:, :, :], 1.0)
            dve.drain()
            dve.sem_inc(zeroed, 1)
            dve.wait_ge(const_in, 32)

            def mlstm(k, slot):
                if slot == 0:
                    dve.tensor_copy(colt[:, :], cols[:, ds(k, 1), :].rearrange("p a n -> p (a n)"))
                    dve.tensor_copy(carry_t[:, :], carry_all[:, :, ds(k, 1)].rearrange("p h a -> p (h a)"))
                    dve.drain()
                    for h in range(HM):
                        v = dve.tensor_scalar(vd[:, h, :], v1[:, h, :], colt[:, 96 + h:97 + h], None, ALU.mult)
                    v.then_inc(vd_done.sem, 1)
                    reached(dve, t_qk, t_qk.at(k))
                    dve.tensor_copy(qkT[:, HM:2 * HM, :], psC[:, 512:1024].rearrange("p (h t) -> p h t", h=HM)).then_inc(c_qk_v.sem, 1)
                    reached(dve, bm_out, bm_out.at(k))
                    for h in range(HM):
                        w = dve.scalar_tensor_tensor(out=wt[:, h, :], in0=psE[:, h * P:(h + 1) * P], scalar=colt[:, h:h + 1],
                                                     in1=after[:, :], op0=ALU.add, op1=ALU.add)
                    w.then_inc(w_sum.sem, 1)
                if slot == 1:
                    reached(dve, inter_out, inter_out.at(k))
                    for h in range(HM):
                        v = dve.tensor_scalar(num[:, h, :], v1_of(psC, h), colt[:, 32 + h:33 + h], None, ALU.mult)
                    v.then_inc(inter_used.sem, 1)
                    reached(dve, s_out, s_out.at(k))
                    reached(dve, w_exp, w_exp.at(k))
                    dve.tensor_tensor(sw[:, :, :], wt[:, :, :], psE[:, :].rearrange("p (h t) -> p h t", h=HM), ALU.mult).then_inc(s_w.sem, 1)
                if slot == 2:
                    reached(dve, intra_out, intra_out.at(k))
                    dve.drain()
                    for h in range(HM):
                        dve.tensor_tensor(num[:, h, :], num[:, h, :], v1_of(psC, h), ALU.add)
                    dve.drain()
                    dve.sem_inc(num_done.sem, 1)
                    dve.tensor_scalar(den[:, 0, :], num[:, :, DM], -1.0, None, ALU.mult)
                    dve.drain()
                    dve.tensor_tensor(den[:, 0, :], den[:, 0, :], num[:, :, DM], ALU.max)
                    dve.drain()
                    dve.tensor_tensor(den[:, 0, :], den[:, 0, :], colt[:, 64:64 + HM], ALU.max)
                    dve.drain()
                    dve.reciprocal(den[:, 1, :], den[:, 0, :]).then_inc(den_done.sem, 1)
                if slot == 3:
                    reached(dve, up_out, up_out.at(k))
                    for h in range(HM):
                        dve.scalar_tensor_tensor(out=Cn[:, h, :], in0=Cn[:, h, :], scalar=carry_t[:, h:h + 1],
                                                 in1=v1_of(psC, h), op0=ALU.mult, op1=ALU.add)
                    dve.drain()
                    dve.sem_inc(state_done.sem, 1)

            def mlstm_out(k, first):
                reached(dve, rs_done, rs_done.at(k))
                dve.tensor_tensor(fac[:, :], ssq[:, :], den[:, 1, :], ALU.mult)
                dve.drain()
                if not first:
                    reached(dve, t_hc, t_hc.at(k - 1))
                for h in range(HM):
                    dve.scalar_tensor_tensor(out=hcat[:, h * DM:(h + 1) * DM], in0=num[:, h, 0:DM], scalar=fac[:, h:h + 1],
                                             in1=mx[:, 3, h * DM:(h + 1) * DM], op0=ALU.mult, op1=ALU.mult)
                dve.drain()
                dve.sem_inc(hm_done.sem, 1)
                dve.sem_inc(mix_free.sem, 1)

            def sums(k, w, h):
                z = zb[:, h % 2, 0:w]
                reached(dve, l_done, l_done.at(k, h + 1))
                dve.scalar_tensor_tensor(out=cum[:, 0:w], in0=z, scalar=0.0, in1=lz[:, h % 2, 0:w], op0=ALU.max, op1=ALU.add).then_inc(l_used.sem, 1)
                dve.drain()
                back = cum[:, 0:w][:, ::-1]
                dve.tensor_tensor_scan(back, one[:, 0:1].broadcast_to([P, w]), back, 0.0, ALU.mult, ALU.add)
                dve.drain()
                if h >= 2:
                    reached(dve, at_out, at_out.at(k, h - 1))
                dve.tensor_tensor(A[:, h % 2, 0:w], z, cum[:, 0:w], ALU.subtract).then_inc(d_done.sem, 1)
                dve.drain()

            def project(k, slot):
                if slot == 4:
                    reached(dve, t_hc, t_hc.at(k))
                    dve.tensor_copy(hcT[:, KD // 2:KD, :], psC[:, 512:1024].rearrange("p (j t) -> p j t", t=P)).then_inc(hc_dve.sem, 1)
                if slot == 7:
                    reached(dve, y_out, y_out.at(k))
                    reached(dve, xr_in, xr_in.at(k))
                    dve.tensor_tensor(xy[:, :], psC[:, :], gate_a[:, :], ALU.mult)
                    dve.drain()
                    dve.tensor_tensor(xr[:, :], xy[:, :], xr[:, :], ALU.add).then_inc(x1_done.sem, 1)

            def tile(k, w, first):
                reached(dve, mix_in, mix_in.at(k))
                for s in range(HS + 3):
                    if s < HS:
                        reached(dve, z_out, z_out.at(k, s + 1))
                        dve.tensor_scalar(zb[:, s % 2, 0:w], psZ[:, 0:w], DS ** -0.5, sb_bias[:, s:s + 1], ALU.mult, ALU.add).then_inc(z_lin.sem, 1)
                    if 1 <= s <= HS:
                        sums(k, w, s - 1)
                    mlstm(k, s)
                    if s == 5:
                        mlstm_out(k, first)
                    if not first:
                        project(k - 1, s)
                    if 2 <= s < HS + 2:
                        h, n = s - 2, 4
                        reached(dve, at_out, at_out.at(k, h + 1))
                        if w > n * P:
                            dve.tensor_copy(AT[:, h % 2, n:w // P, :], psA[:, n * P:w].rearrange("p (j t) -> p j t", t=P))
                            dve.drain()
                        dve.sem_inc(at_dve.sem, 1)

            dve.memset(one[:, :], 1.0)
            dve.drain()
            tiles(dve, tile, project)


def sample_mlstm(nc, io, sem, signal, reached, mix_d, ident, cols, bm_rows, carry_all, sel_head, hcat_s, **_):
    V1, NBH = DM + 1, NB * HM
    with ExitStack() as ctx:
        sb = lambda n, s, d=F32: ctx.enter_context(nc.sbuf_tensor(n, s, d))
        ps = lambda n, s, d=F32: ctx.enter_context(nc.psum_tensor(n, s, d))
        mx = sb("s_mx", [NS, 4, WM])
        v1, vd = sb("s_v1", [NS, HM, V1]), sb("s_vd", [NS, HM, DM])
        vdm = sb("s_vdm", [NS, NB, HM, DM])
        dec = sb("s_dec", [NS, HM, NB])
        qkT = sb("s_qkT", [P, 2 * HM, NS])
        qm = sb("s_qm", [P, HM, NB, NS])
        C = sb("s_C", [P, NBH, DM])
        CT = sb("s_CT", [P, NBH, V1])
        n_in, n_new, n_rows = sb("s_n", [NBH, DM]), sb("s_nn", [P, NB, HM]), sb("s_nr", [NBH, DM])
        own = sb("s_own", [P, NB, NS])
        own_row = sb("s_own_row", [NS, NB])
        see = sb("s_see", [NS, NS])
        wt, sw = sb("s_wt", [NS, HM, NS]), sb("s_sw", [NS, HM, NS])
        intra, num = sb("s_intra", [NS, HM, V1]), sb("s_num", [NS, HM, V1])
        den, ssq, fac, junk = sb("s_den", [NS, 2, HM]), sb("s_ssq", [NS, HM]), sb("s_fac", [NS, HM]), sb("s_junk", [NS, P])
        psQ, psN, psE = ps("s_psQ", [P, 2 * HM, NS]), ps("s_psN", [P, NBH]), ps("s_psE", [P, 512])
        psI, psS = ps("s_psI", [P, 1024]), [ps(f"s_psS{i}", [P, 4, P]) for i in range(2)]
        v1_of = lambda a, h: a[0:NS, (h // 2) * 512 + (h % 2) * V1:(h // 2) * 512 + (h % 2) * V1 + V1]
        loaded, ones_set, masks = sem("s_loaded"), sem("s_ones"), sem("s_masks")
        pe_d, act_d, dve_d = sem("s_pe_done"), sem("s_act_done"), sem("s_dve_done")
        ct_t, ct_c, up_m, up_c, kept = sem("s_ct_t"), sem("s_ct_c"), sem("s_up_m"), sem("s_up_c"), sem("s_kept")
        here = slice(SEQ, SEQ + NS)
        block = ctx.enter_context(nc.Block())

        @block.sync
        def _(sp):
            sp.dma_start(mx[:, :, :], mix_d[here, :].rearrange("p (j n) -> p j n", j=4)).then_inc(loaded, 16)
            sp.dma_start(n_in[:, :], io["state_mlstm_n"].rearrange("a b h k -> (a b h) k")).then_inc(loaded, 16)
            sp.dma_start(C[:, :, :], io["state_mlstm_C"].rearrange("a b h v k -> v (a b h) k")).then_inc(loaded, 16)
            sp.wait_ge(ones_set, 1)
            sp.dma_start(v1[:, :, 0:DM], mix_d[here, 2 * WM:3 * WM].rearrange("p (h n) -> p h n", h=HM)).then_inc(loaded, 16)
            sp.wait_ge(up_c, NB)
            sp.dma_start(io["C_sample"].rearrange("a b h v k -> v (a b h) k"), C[:, :, :]).then_inc(kept, 16)
            sp.wait_ge(act_d, 6)
            sp.dma_start(io["n_sample"].rearrange("a b h k -> (a b h) k"), n_rows[:, :]).then_inc(kept, 16)
            sp.wait_ge(kept, 32)

        @block.gpsimd
        def _(pool):
            pool.memset(own[:, :, :], 1.0)
            pool.memset(own_row[:, :], 1.0)
            pool.memset(see[:, :], 0.0)
            pool.drain()

            def keep(a, pattern, base, cm, fill):
                pool.affine_select(out=a, in_=a, compare_op=ALU.is_ge, fill=fill, base=base, pattern=pattern, channel_multiplier=cm)
                pool.drain()
            keep(own[:, :, :], [[-SQ, NB], [1, NS]], 0, 0, 0.0)
            keep(own[:, :, :], [[SQ, NB], [-1, NS]], SQ - 1, 0, 0.0)
            keep(own_row[:, :], [[-SQ, NB]], 0, 1, 0.0)
            keep(own_row[:, :], [[SQ, NB]], SQ - 1, -1, 0.0)
            see3 = see[:, :].rearrange("p (b q) -> p b q", q=SQ)
            keep(see3, [[-SQ, NB], [0, SQ]], 0, 1, HIDE)
            keep(see3, [[SQ, NB], [0, SQ]], SQ - 1, -1, HIDE)
            keep(see3, [[SQ, NB], [1, SQ]], 0, -1, HIDE)
            pool.sem_inc(masks, 1)

        @block.tensor
        def _(pe):
            pe.wait_ge(loaded, 64)
            for j in range(2 * HM):
                t = pe.transpose(psQ[:, j, :], mx[:, j // HM, (j % HM) * DM:(j % HM + 1) * DM], ident[0:NS, 0:NS])
            t.then_inc(pe_d, 1)
            pe.transpose(psN[:, :], n_in[:, :], ident[0:NBH, 0:NBH]).then_inc(pe_d, 1)
            for h in range(HM):
                m = pe.matmul(psE[0:NS, h * NS:(h + 1) * NS], sel_head[:, h, 0:NS], bm_rows[:, SEQ:TT], start=True, stop=True)
            m.then_inc(pe_d, 1)
            for b in range(NB):
                if b >= 2:
                    pe.wait_ge(ct_c, b - 1)
                for h in range(HM):
                    t = pe.transpose(psS[b % 2][:, h, :], C[:, b * HM + h, :], ident[:, :])
                t.then_inc(ct_t, 1)
            pe.wait_ge(act_d, 1)
            pe.wait_ge(dve_d, 1)
            for h in range(HM):
                m = pe.matmul(psE[0:NS, h * NS:(h + 1) * NS], qkT[:, HM + h, :], qkT[:, h, :], start=True, stop=True)
            m.then_inc(pe_d, 1)
            pe.wait_ge(ct_c, NB + 1)
            pe.wait_ge(dve_d, 2)
            for h in range(HM):
                for b in range(NB):
                    m = pe.matmul(v1_of(psI, h), qm[:, h, b, :], CT[:, b * HM + h, :], start=b == 0, stop=b == NB - 1)
            m.then_inc(pe_d, 1)
            pe.wait_ge(dve_d, 4)
            for h in range(HM):
                m = pe.matmul(psS[h // 2][0:NS, :, :].rearrange("p j t -> p (j t)")[:, (h % 2) * V1:(h % 2 + 1) * V1],
                              sw[:, h, :], v1[:, h, :], start=True, stop=True)
            m.then_inc(pe_d, 1)
            pe.wait_ge(dve_d, 3)
            for h in range(HM):
                m = pe.matmul(psN[:, h * NB:(h + 1) * NB], mx[:, 1, h * DM:(h + 1) * DM], dec[:, h, :], start=True, stop=True)
            m.then_inc(pe_d, 1)
            pe.wait_ge(act_d, 3)
            for b in range(NB):
                if b >= 2:
                    pe.wait_ge(up_c, b - 1)
                for h in range(HM):
                    m = pe.matmul(psS[b % 2][:, h, :], vdm[:, b, h, :], mx[:, 1, h * DM:(h + 1) * DM], start=True, stop=True)
                m.then_inc(up_m, 1)
            pe.wait_ge(dve_d, 6)
            pe.transpose(psE[0:NBH, 0:P], n_new[:, :, :].rearrange("p b h -> p (b h)"), ident[:, :]).then_inc(pe_d, 1)

        @block.scalar
        def _(act):
            act.preload_act_table_set(EXP_LN)
            act.wait_ge(pe_d, 1)
            act.activation(qkT[:, :, :], psQ[:, :, :], ACT.Copy).then_inc(act_d, 1)
            act.wait_ge(dve_d, 1)
            act.activation(wt[:, :, :], wt[:, :, :], ACT.Exp).then_inc(act_d, 1)
            act.wait_ge(pe_d, 6)
            for g in range(2):
                act.activation(intra[:, 2 * g:2 * g + 2, :], psS[g][0:NS, :, :].rearrange("p j t -> p (j t)")[:, 0:2 * V1]
                               .rearrange("p (h t) -> p h t", h=2), ACT.Copy)
            act.drain()
            act.sem_inc(act_d, 1)
            act.wait_ge(dve_d, 5)
            for h in range(HM):
                act.activation(junk[:, :], num[:, h, 0:DM], ACT.Square, scale=den[:, 1, h:h + 1], accum_out=ssq[:, h:h + 1])
                act.drain()
            act.activation(ssq[:, :], ssq[:, :], ACT.Ln, scale=1.0 / DM, bias=EPS)
            act.drain()
            act.activation(ssq[:, :], ssq[:, :], ACT.Exp, scale=-0.5).then_inc(act_d, 2)
            act.wait_ge(pe_d, 8)
            act.activation(n_rows[:, :], psE[0:NBH, 0:P], ACT.Copy).then_inc(act_d, 1)

        @block.vector
        def _(dve):
            dve.memset(v1[:, :, :], 1.0)
            dve.drain()
            dve.sem_inc(ones_set, 1)
            dve.wait_ge(loaded, 64)
            dve.wait_ge(masks, 1)
            dve.wait_ge(pe_d, 3)
            col = cols[0:NS, NT, :]
            for h in range(HM):
                dve.scalar_tensor_tensor(out=wt[:, h, :], in0=psE[0:NS, h * NS:(h + 1) * NS], scalar=col[:, h:h + 1],
                                         in1=see[:, :], op0=ALU.add, op1=ALU.add)
            dve.drain()
            dve.sem_inc(dve_d, 1)
            dve.tensor_copy(CT[:, :, DM], psN[:, :])
            for b in range(NB):
                dve.wait_ge(ct_t, b + 1)
                dve.tensor_copy(CT[:, b * HM:(b + 1) * HM, 0:DM], psS[b % 2][:, :, :]).then_inc(ct_c, 1)
            dve.drain()
            dve.sem_inc(ct_c, 1)
            dve.wait_ge(act_d, 1)
            for h in range(HM):
                dve.tensor_tensor(qm[:, h, :, :], qkT[:, h:h + 1, :].broadcast_to([P, NB, NS]), own[:, :, :], ALU.mult)
            dve.drain()
            dve.sem_inc(dve_d, 1)
            for h in range(HM):
                dve.tensor_scalar(vd[:, h, :], v1[:, h, 0:DM], col[:, 96 + h:97 + h], None, ALU.mult)
                dve.tensor_scalar(dec[:, h, :], own_row[:, :], col[:, 96 + h:97 + h], None, ALU.mult)
            dve.drain()
            for b in range(NB):
                dve.tensor_scalar(vdm[:, b, :, :], vd[:, :, :], own_row[:, b:b + 1], None, ALU.mult)
            dve.drain()
            dve.sem_inc(dve_d, 1)
            dve.wait_ge(act_d, 2)
            dve.wait_ge(pe_d, 4)
            dve.tensor_tensor(sw[:, :, :], wt[:, :, :], psE[0:NS, 0:HM * NS].rearrange("p (h t) -> p h t", h=HM), ALU.mult).then_inc(dve_d, 1)
            dve.wait_ge(act_d, 3)
            dve.wait_ge(pe_d, 5)
            for h in range(HM):
                dve.scalar_tensor_tensor(out=num[:, h, :], in0=v1_of(psI, h), scalar=col[:, 32 + h:33 + h],
                                         in1=intra[:, h, :], op0=ALU.mult, op1=ALU.add)
            dve.drain()
            dve.tensor_scalar(den[:, 0, :], num[:, :, DM], -1.0, None, ALU.mult)
            dve.drain()
            dve.tensor_tensor(den[:, 0, :], den[:, 0, :], num[:, :, DM], ALU.max)
            dve.drain()
            dve.tensor_tensor(den[:, 0, :], den[:, 0, :], col[:, 64:64 + HM], ALU.max)
            dve.drain()
            dve.reciprocal(den[:, 1, :], den[:, 0, :]).then_inc(dve_d, 1)
            keep = carry_all[:, :, NT:NT + NB].rearrange("p h b -> p b h")
            dve.wait_ge(pe_d, 7)
            dve.tensor_tensor(n_new[:, :, :], CT[:, :, DM].rearrange("p (b h) -> p b h", h=HM), keep, ALU.mult)
            dve.drain()
            dve.tensor_tensor(n_new[:, :, :], n_new[:, :, :], psN[:, :].rearrange("p (h b) -> p b h", b=NB), ALU.add).then_inc(dve_d, 1)
            for b in range(NB):
                dve.wait_ge(up_m, b + 1)
                for h in range(HM):
                    dve.scalar_tensor_tensor(out=C[:, b * HM + h, :], in0=C[:, b * HM + h, :],
                                             scalar=carry_all[:, h, NT + b:NT + b + 1], in1=psS[b % 2][:, h, :], op0=ALU.mult, op1=ALU.add)
                dve.drain()
                dve.sem_inc(up_c, 1)
            dve.wait_ge(act_d, 5)
            dve.tensor_tensor(fac[:, :], ssq[:, :], den[:, 1, :], ALU.mult)
            dve.drain()
            for h in range(HM):
                dve.scalar_tensor_tensor(out=hcat_s[0:NS, h * DM:(h + 1) * DM], in0=num[:, h, 0:DM], scalar=fac[:, h:h + 1],
                                         in1=mx[:, 3, h * DM:(h + 1) * DM], op0=ALU.mult, op1=ALU.mult)


def sample_attention(nc, io, sem, pool_dma_sem, signal, reached, prime, mod_d, sq_d, x1_d, ident, hcat_s, **_):
    G, TK_ = NB // 2, PAST + SQ
    with ExitStack() as ctx:
        sb = lambda n, s, d=F32: ctx.enter_context(nc.sbuf_tensor(n, s, d))
        ps = lambda n, s, d=F32: ctx.enter_context(nc.psum_tensor(n, s, d))
        w_out = sb("a_w_out", [P, KD, D])
        gate_a = sb("a_gate", [NS, D])
        xr = sb("a_x", [NS, D])
        Kp, Vp = sb("a_K", [P, 2, NPG, WS]), sb("a_V", [P, 2, NPG, WS])
        Vn = sb("a_Vn", [SQ, 2, WS])
        KT = sb("a_KT", [P, 4, 2, TK_])
        qn, kn = sb("a_qn", [NS, WS]), sb("a_kn", [NS, WS])
        QT, KnT = sb("a_QT", [P, 4, NS]), sb("a_KnT", [P, 4, NS])
        Q0 = sb("a_Q0", [P, 4, 2, P])
        pick = sb("a_pick", [P, 4, 2, 16])
        own = sb("a_own", [P, 16])
        fold4, fold = sb("a_fold4", [P, 2, SQ, HS]), sb("a_fold", [P, 2, SQ])
        vis, hide_f, hide = sb("a_vis", [P, SQ, 16]), sb("a_hide_f", [P, SQ]), sb("a_hide", [P, SQ], BF16)
        ident_h = sb("a_ident_h", [P, P], BF16)
        bias = sb("a_bias", [P, 1])
        one = sb("a_one", [P, 1])
        table, table_f = sb("a_table", [P, NB * NPG], I32), sb("a_table_f", [P, NB * NPG])
        lane, lane_f = sb("a_lane", [P, 1], I32), sb("a_lane_f", [P, 1])
        rows, rows_g = sb("a_rows", [P, NB * NPG], I32), sb("a_rows_g", [P, 2, 2 * NPG], I32)
        zb, lz, cum = sb("a_zb", [P, TK_]), sb("a_lz", [P, TK_]), sb("a_cum", [P, TK_])
        A = sb("a_A", [P, TK_])
        AT, ATn = sb("a_AT", [P, NPG, P]), sb("a_ATn", [SQ, P])
        mo = sb("a_mo", [P, 2, WS])
        hs = sb("a_hs", [16, WS])
        hcT = sb("a_hcT", [P, KD, NS])
        psZ, psT = ps("a_psZ", [P, 3 * 512]), [ps(f"a_psT{i}", [P, 512]) for i in range(2)]
        psO, psX = ps("a_psO", [P, 2, 512]), ps("a_psX", [P, 512])
        const_in, own_in, wo_in, set_up, folded = sem("a_const"), sem("a_own_in"), sem("a_wo"), sem("a_setup"), sem("a_folded")
        idx_done, rows_set = sem("a_idx"), signal("a_rows_set", 2)
        k_in, v_in = (Signal(pool_dma_sem(n), 16 * 2 * NPG) for n in ("a_k_in", "a_v_in"))
        vn_in = signal("a_vn_in", 16)
        free = signal("a_free", 1, 1)
        qk_t, qk_c = sem("a_qk_t"), sem("a_qk_c")
        q0_set, k_t, k_ca, k_cv = signal("a_q0"), signal("a_k_t", 16), signal("a_k_ca", 8), signal("a_k_cv", 8)
        z_out, z_lin, l_done, d_done, a_done = (signal(n) for n in ("a_z", "a_zl", "a_l", "a_d", "a_a"))
        at_t, at_c, o_out, mo_done, hs_out, hs_done, hs_kept = (signal("a_at_t", 3), signal("a_at_c", 3), signal("a_o"), signal("a_mo"),
                                                                signal("a_hs_out"), signal("a_hs"), signal("a_hs_kept", 16))
        fin_t, fin_c, y_out, x1_done, x1_kept = sem("a_fin_t"), sem("a_fin_c"), sem("a_y"), sem("a_x1"), sem("a_x1_kept")
        block = ctx.enter_context(nc.Block())
        pages_k = io["cache_sb_k"].rearrange("a n p h d -> (a n p) (h d)")
        pages_v = io["cache_sb_v"].rearrange("a n p h d -> (a n p) (h d)")
        flat = lambda a: a.rearrange("a b t h d -> (a b t) (h d)")

        @block.sync
        def _(sp):
            sp.dma_start(table[:, :], io["page_table"].rearrange("b j -> (b j)").unsqueeze(0).broadcast_to([P, NB * NPG])).then_inc(idx_done, 16)
            sp.dma_start(qn[:, :], sq_d[SEQ:SEQ + NS, :]).then_inc(own_in, 16)
            sp.dma_start(kn[:, :], flat(io["k_sample"])).then_inc(own_in, 16)
            for b in range(2):
                sp.dma_start(bias[b * 64:(b + 1) * 64, :], io["sb_bias"].rearrange("a h -> h a")
                             .broadcast_to([HS, SQ]), allow_slow_non_contiguous=True).then_inc(const_in, 16)
            load_rows(sp, gate_a[:, :], mod_d, 2 * D, True).then_inc(const_in, 16)
            sp.dma_start(xr[:, :], io["x_sample"].rearrange("b q d -> (b q) d")).then_inc(const_in, 16)
            sp.dma_start(w_out[:, :, :], io["w_out"][0].rearrange("(k p) n -> p k n", p=P)).then_inc(wo_in, 16)
            with sp.Fori(0, G) as g:
                reached(sp, free, free.ago(g))
                sp.dma_start(Vn[:, :, :], flat(io["v_sample"])[ds(g * 16, 16), :].rearrange("(b q) n -> q b n", q=SQ)).then_inc(vn_in.sem, 16)
                reached(sp, hs_done, hs_done.at(g))
                sp.dma_start(sq_d[ds(g * 16 + SEQ + NS, 16), :], hs[:, :]).then_inc(hs_kept.sem, 16)
            sp.wait_ge(hs_kept.sem, hs_kept.at(G - 1))
            sp.dma_start(hcat_s[0:NS, WM:D], sq_d[SEQ + NS:SEQ + 2 * NS, :]).then_inc(const_in, 16)
            sp.wait_ge(x1_done, 1)
            sp.dma_start(x1_d[SEQ:SEQ + NS, :], xr[:, :]).then_inc(x1_kept, 16)
            sp.wait_ge(x1_kept, 16)

        @block.gpsimd
        def _(pool):
            pool.iota(lane[:, :], [[0, 1]], base=0, channel_multiplier=1)
            pool.drain()
            pool.sem_inc(set_up, 1)

            def gather(which):
                pages, dst, sig = ((pages_k, Kp, k_in), (pages_v, Vp, v_in))[which]
                for b in range(2):
                    for j in range(NPG):
                        at = bass.IndirectOffsetOnAxis(rows_g[:, which, b * NPG + j:b * NPG + j + 1], 0)
                        pool.indirect_dma_start(dst[:, b, j, :], None, pages, at).then_inc(sig.sem, 16)

            for a, v in ((pick, 1.0), (own, 1.0), (fold4, 1.0), (vis, 1.0), (ident_h, 0.0)):
                pool.memset(a[tuple(slice(None) for _ in a.shape)], v)
            pool.drain()

            def keep(a, pattern, base, cm, op=ALU.is_ge, fill=0.0):
                pool.affine_select(out=a, in_=a, compare_op=op, fill=fill, base=base, pattern=pattern, channel_multiplier=cm)
                pool.drain()
            keep(ident_h[:, :], [[-1, P]], 0, 1, ALU.not_equal, 1.0)
            keep(own[:, :], [[-SQ, 16]], 0, 1)
            keep(fold4[:, :, :, :], [[-64, 2], [-1, SQ], [-SQ, HS]], 0, 1, ALU.is_equal)
            keep(vis[:, :, :], [[-1, SQ], [-SQ, 16]], -1, 1)
            for half in range(2):
                v = pick[half * 64:(half + 1) * 64, :, :, :].rearrange("p c b (e h) -> p c (b e) h", e=2)
                keep(v, [[-2, 4], [0, 4], [1, HS]], -half, 0, ALU.is_equal)
            pool.drain()
            keep(own[:, :], [[SQ, 16]], SQ - 1, -1)
            keep(vis[:, :, :], [[0, SQ], [SQ, 16]], SQ - 1, -1)
            v = pick[:, :, :, :].rearrange("p c b (e h) -> p c b e h", e=2)
            for b in range(2):
                keep(v[:, :, b, :, :], [[0, 4], [1, 2], [0, HS]], -b, 0, ALU.is_equal)
            pool.drain()
            pool.sem_inc(set_up, 1)
            with pool.Fori(0, G) as g:
                for which in range(2):
                    reached(pool, rows_set, rows_set.at(g, which + 1))
                    gather(which)

        @block.tensor
        def _(pe):
            pe.wait_ge(own_in, 32)
            for n, a in enumerate((qn, kn)):
                for c in range(4):
                    t = pe.transpose(psT[n][:, c * P:c * P + NS], a[:, c * P:(c + 1) * P], ident[0:NS, 0:NS])
            t.then_inc(qk_t, 1)
            pe.wait_ge(qk_c, 1)

            def pair(g):
                reached(pe, k_in, k_in.at(g))
                for n in range(16):
                    if n >= 2:
                        sig = k_ca if n % 2 == 0 else k_cv
                        reached(pe, sig, sig.at(g, n // 2))
                    for c in range(4):
                        t = pe.transpose(psT[n % 2][:, c * P:(c + 1) * P], Kp[:, n // NPG, n % NPG, c * P:(c + 1) * P], ident[:, :])
                    t.then_inc(k_t.sem, 1)
                reached(pe, k_ca, k_ca.at(g))
                reached(pe, k_cv, k_cv.at(g))
                reached(pe, q0_set, q0_set.at(g))
                for n, (c0, c1) in enumerate(((0, 512), (512, 1024), (1024, TK_))):
                    zc = psZ[:, n * 512:n * 512 + c1 - c0]
                    if n == 2:
                        pe.matmul(zc, ident_h[:, :], hide[:, :], start=True, stop=False)
                    for c in range(4):
                        for b in range(2):
                            m = pe.matmul(zc, Q0[:, c, b, :], KT[:, c, b, c0:c1], start=n < 2 and c == 0 and b == 0, stop=c == 3 and b == 1)
                m.then_inc(z_out.sem, 1)
                reached(pe, a_done, a_done.at(g))
                for n in range(3):
                    if n == 2:
                        reached(pe, at_c, at_c.at(g, 1))
                        t = pe.transpose(psT[0][0:SQ, 0:P], A[:, PAST:TK_], ident[:, :])
                    else:
                        for j in range(4):
                            t = pe.transpose(psT[n][:, j * P:(j + 1) * P], A[:, (n * 4 + j) * P:(n * 4 + j + 1) * P], ident[:, :])
                    t.then_inc(at_t.sem, 1)
                reached(pe, at_c, at_c.at(g))
                reached(pe, v_in, v_in.at(g))
                reached(pe, vn_in, vn_in.at(g))
                for b in range(2):
                    for j in range(NPG):
                        pe.matmul(psO[:, b, :], AT[:, j, :], Vp[:, b, j, :], start=j == 0, stop=False)
                    m = pe.matmul(psO[:, b, :], ATn[:, :], Vn[:, b, :], start=False, stop=True)
                m.then_inc(o_out.sem, 1)
                reached(pe, mo_done, mo_done.at(g))
                pe.matmul(psX[0:16, :], fold[:, :, :].rearrange("p b q -> p (b q)"), mo[:, 0, :], start=True, stop=True).then_inc(hs_out.sem, 1)

            pe.wait_ge(folded, 1)
            with pe.Fori(0, G) as g:
                pair(g)
            pe.wait_ge(const_in, 80)
            pe.wait_ge(hs_done.sem, hs_done.at(G - 1))
            for j in range(KD):
                t = pe.transpose(psX[:, j * NS:(j + 1) * NS], hcat_s[0:NS, j * P:(j + 1) * P], ident[0:NS, 0:NS])
            t.then_inc(fin_t, 1)
            pe.wait_ge(fin_c, 1)
            pe.wait_ge(wo_in, 16)
            for c in range(2):
                for j in range(KD):
                    m = pe.matmul(psO[0:NS, c, :], hcT[:, j, :], w_out[:, j, c * 512:(c + 1) * 512], start=j == 0, stop=j == KD - 1)
            m.then_inc(y_out, 1)

        @block.scalar
        def _(act):
            act.preload_act_table_set(EXP_LN)
            def pair(g):
                for n in range(0, 16, 2):
                    reached(act, k_t, k_t.at(g, n + 1))
                    act.activation(KT[:, :, n // NPG, (n % NPG) * P:(n % NPG + 1) * P],
                                   psT[0][:, :].rearrange("p (c t) -> p c t", c=4), ACT.Copy).then_inc(k_ca.sem, 1)
                reached(act, z_lin, z_lin.at(g))
                act.activation(lz[:, :], zb[:, :], ACT.Abs)
                act.drain()
                act.activation(lz[:, :], lz[:, :], ACT.Exp, scale=-1.0)
                act.drain()
                act.activation(lz[:, :], lz[:, :], ACT.Ln, bias=1.0).then_inc(l_done.sem, 1)
                reached(act, d_done, d_done.at(g))
                act.activation(A[:, :], cum[:, :], ACT.Exp).then_inc(a_done.sem, 1)
                for n in range(3):
                    reached(act, at_t, at_t.at(g, n + 1))
                    if n == 2:
                        c = act.activation(ATn[:, :], psT[0][0:SQ, 0:P], ACT.Copy)
                    else:
                        c = act.activation(AT[:, n * 4:(n + 1) * 4, :], psT[n][:, :].rearrange("p (c t) -> p c t", c=4), ACT.Copy)
                    c.then_inc(at_c.sem, 1)
                reached(act, hs_out, hs_out.at(g))
                act.activation(hs[:, :], psX[0:16, :], ACT.Copy).then_inc(hs_done.sem, 1)

            with act.Fori(0, G) as g:
                pair(g)
                reached(act, hs_kept, hs_kept.at(g))
            act.wait_ge(fin_t, 1)
            act.activation(hcT[:, :, :], psX[:, :].rearrange("p (j t) -> p j t", j=KD), ACT.Copy).then_inc(fin_c, 1)

        @block.vector
        def _(dve):
            dve.memset(one[:, :], 1.0)
            dve.wait_ge(idx_done, 16)
            dve.wait_ge(set_up, 1)
            dve.tensor_copy(table_f[:, :], table[:, :])
            dve.tensor_copy(lane_f[:, :], lane[:, :])
            dve.drain()
            dve.tensor_scalar(rows[:, :], table_f[:, :], float(PAGE), lane_f[:, 0:1], ALU.mult, ALU.add)
            dve.drain()

            def take_rows(g, which):
                dve.tensor_copy(rows_g[:, which, :], rows[:, ds(g * 2 * NPG, 2 * NPG)]).then_inc(rows_set.sem, 1)

            take_rows(0, 0)
            take_rows(0, 1)
            dve.wait_ge(set_up, 2)
            dve.tensor_reduce(fold[:, :, :], fold4[:, :, :, :], AX.X, ALU.add)
            dve.tensor_reduce(hide_f[:, :], vis[:, :, :], AX.X, ALU.add)
            dve.drain()
            dve.tensor_scalar(hide[:, :], hide_f[:, :], -HIDE, HIDE, ALU.mult, ALU.add)
            dve.drain()
            dve.sem_inc(folded, 1)
            dve.wait_ge(qk_t, 1)
            dve.tensor_copy(QT[:, :, :], psT[0][:, :].rearrange("p (c t) -> p c t", c=4)[:, :, 0:NS])
            dve.tensor_copy(KnT[:, :, :], psT[1][:, :].rearrange("p (c t) -> p c t", c=4)[:, :, 0:NS])
            dve.drain()
            dve.sem_inc(qk_c, 1)
            prime(dve, free)
            dve.wait_ge(const_in, 64)

            def pair(g, more=True):
                q = QT[:, :, ds(g * 16, 16)].rearrange("p c (b q) -> p c b q", q=SQ)
                for c in range(4):
                    dve.tensor_tensor(Q0[:, c, :, :].rearrange("p b (x q) -> p b x q", q=SQ),
                                      q[:, c, :, :].unsqueeze(2).broadcast_to([P, 2, 16, SQ]),
                                      pick[:, c, :, :].unsqueeze(3).broadcast_to([P, 2, 16, SQ]), ALU.mult)
                for b in range(2):
                    dve.tensor_copy(KT[:, :, b, PAST:TK_], KnT[:, :, ds(g * 16 + b * SQ, SQ)])
                dve.drain()
                dve.sem_inc(q0_set.sem, 1)
                for n in range(1, 16, 2):
                    reached(dve, k_t, k_t.at(g, n + 1))
                    dve.tensor_copy(KT[:, :, n // NPG, (n % NPG) * P:(n % NPG + 1) * P],
                                    psT[1][:, :].rearrange("p (c t) -> p c t", c=4)).then_inc(k_cv.sem, 1)
                reached(dve, z_out, z_out.at(g))
                if more:
                    reached(dve, k_in, k_in.at(g))
                    take_rows(g + 1, 0)
                dve.tensor_scalar(zb[:, :], psZ[:, 0:TK_], DS ** -0.5, bias[:, 0:1], ALU.mult, ALU.add).then_inc(z_lin.sem, 1)
                reached(dve, l_done, l_done.at(g))
                dve.drain()
                dve.scalar_tensor_tensor(out=cum[:, :], in0=zb[:, :], scalar=0.0, in1=lz[:, :], op0=ALU.max, op1=ALU.add)
                dve.drain()
                back = cum[:, ::-1]
                dve.tensor_tensor_scan(back, one[:, 0:1].broadcast_to([P, TK_]), back, 0.0, ALU.mult, ALU.add)
                dve.drain()
                dve.tensor_tensor(cum[:, :], zb[:, :], cum[:, :], ALU.subtract).then_inc(d_done.sem, 1)
                reached(dve, o_out, o_out.at(g))
                if more:
                    reached(dve, v_in, v_in.at(g))
                    take_rows(g + 1, 1)
                for b in range(2):
                    dve.tensor_tensor(mo[:, b, :].rearrange("p (h d) -> p h d", h=HS), psO[:, b, :].rearrange("p (h d) -> p h d", h=HS),
                                      own[:, b * HS:(b + 1) * HS].unsqueeze(2).broadcast_to([P, HS, DS]), ALU.mult)
                dve.drain()
                dve.tensor_tensor(mo[:, 0, :], mo[:, 0, :], mo[:, 1, :], ALU.add).then_inc(mo_done.sem, 1)
                reached(dve, hs_out, hs_out.at(g))
                dve.sem_inc(free.sem, 1)

            with dve.Fori(0, G - 1) as g:
                pair(g)
            pair(G - 1, more=False)
            dve.wait_ge(y_out, 1)
            dve.tensor_tensor(gate_a[:, :], psO[0:NS, :, :].rearrange("p a n -> p (a n)"), gate_a[:, :], ALU.mult)
            dve.drain()
            dve.tensor_tensor(xr[:, :], gate_a[:, :], xr[:, :], ALU.add).then_inc(x1_done, 1)



def experts(nc, io, sem, pool_dma_sem, signal, reached, prime, mod_d, x1_d, **_):
    NU, NV, NW, PT = 8, 8, 4, 4
    STEPS = P // PT
    NG = 4
    LOW = -3e38
    group_step = {14: 0, 20: 1, 26: 2}
    with ExitStack() as ctx:
        sb = lambda n, s, d=F32: ctx.enter_context(nc.sbuf_tensor(n, s, d))
        ps = lambda n, s, d=F32: ctx.enter_context(nc.psum_tensor(n, s, d))
        ident = sb("f_ident", [P, P])
        w_q = sb("w_query_sb", [P, KD, 2 * PH * DK])
        sub = sb("sub_keys_T", [P, 2, NK])
        gain, shift, gate = sb("f_gain", [P, D]), sb("f_shift", [P, D]), sb("f_gate", [P, D])
        xp, hf = sb("f_x", [P, D]), sb("hf", [P, D])
        rest = sb("f_rest", [P, D])
        parts = sb("f_parts", [P, 3, D], BF16)
        x3 = sb("f_x3", [96, 4, D], BF16)
        hfT, qT = sb("hfT", [P, KD, P]), sb("qT", [P, 8, P])
        sc = sb("scores", [P, 2 * PH, NK])
        va, ia, iaf = sb("va", [P, 2 * PH, TK]), sb("ia", [P, 2 * PH, TK], U32), sb("iaf", [P, 2 * PH, TK])
        cand, cand2 = sb("cand", [P, TK, TK]), sb("cand2", [P, TK * TK])
        ts, pos = sb("ts", [P, PH, TK]), sb("pos", [P, PH, TK], U32)
        pij, pijf = sb("pij", [P, 2, PH * TK], U32), sb("pijf", [P, 2, PH * TK])
        number, found = sb("number", [P, TK]), sb("found", [P, 2, PH * TK])
        number_i = sb("number_i", [P, TK], I32)
        gates_e, gsum = sb("gates_e", [P, PH, TK]), sb("gsum", [P, PH])
        idx, gT = sb("idx", [P, (NT + 1) * P], I32), sb("gT", [P, (NT + 1) * P])
        ssq, rstd = sb("f_ssq", [P, 1]), sb("f_rstd", [P, 1])
        sel3, zero_h = sb("sel3", [96, 32], BF16), sb("zero_h", [96, P], BF16)
        strip = sb("strip", [P, 2 * P])
        ub, vb = sb("ub", [P, NU, D]), sb("vb", [P, NV, D])
        junk = sb("f_junk", [P, D], BF16)
        slot = sb("slot", [P, NV], I32)
        dot, act_o = sb("dot", [P, NV]), sb("act_o", [P, NV])
        W = sb("W", [P, NW, P])
        psX, psY, psP = ps("psX", [P, 2, D]), ps("psY", [P, D]), ps("psP", [P, D])

        wq_in, mods_in, sub_in, set_up = sem("wq_in"), sem("f_mods_in"), sem("sub_in"), sem("f_setup")
        sub_t, sub_c = sem("sub_t"), sem("sub_c")
        x_in, x_free = signal("f_x_in", 16), signal("f_x_free", 1, 1)
        ssq_d, rstd_d, h_d, h_t, hT_a, hT_v = (signal(f"f_{n}") for n in ("ssq_d", "rstd_d", "h_d", "h_t", "hT_a", "hT_v"))
        part_a, part_v, x3_in = signal("part_a", 3), signal("part_v", 2), [signal(f"x3_in{g}", 48) for g in range(NG)]
        q_out, q_copied, sc_out, sc_copied = signal("q_out", 4), signal("q_copied", 4), signal("sc_out", 4), signal("sc_copied", 4)
        taken = signal("taken", 4, 1)
        soft_v, soft_a, made, made_t, routed = signal("soft_v"), signal("soft_a"), signal("made"), signal("made_t", 2), signal("routed")
        u_in, v_in = [pool_dma_sem(f"u_in{i}") for i in range(NU)], [pool_dma_sem(f"v_in{i}") for i in range(NV)]
        slot_set = sem("slot_set")
        spread, dotted, acted, weighed, added = sem("spread"), sem("dotted"), sem("acted"), sem("weighed"), sem("added")
        y_read, out_set, out_kept, xo_in = signal("y_read", 1, 1), signal("out_set"), signal("out_kept", 16, 1), signal("xo_in", 16)
        block = ctx.enter_context(nc.Block())

        def rounds(eng, ask, choose, spend, boundary):
            for step in range(STEPS):
                ask(0, step)
            for step in range(STEPS):
                choose(0, step)
                ask(1, step)
            with eng.Fori(0, NT - 1) as r:
                boundary(r)
                for step in range(STEPS):
                    choose(r + 1, step)
                    ask(r + 2, step)
                    spend(r, step)
                boundary(r, end=True)
            boundary(NT - 1)
            for step in range(STEPS):
                choose(NT, step, more=False)
                spend(NT - 1, step)
            boundary(NT - 1, end=True)
            boundary(NT)
            for step in range(NS // PT):
                spend(NT, step, last=step == NS // PT - 1)
            boundary(NT, end=True)

        @block.sync
        def _(sp):
            prime(sp, out_kept)
            load_rows(sp, gain[:, :], mod_d, 4 * D, False).then_inc(mods_in, 16)
            load_rows(sp, shift[:, :], mod_d, 3 * D, False).then_inc(mods_in, 16)
            load_rows(sp, gate[:, :], mod_d, 5 * D, False).then_inc(mods_in, 16)

            def load(k, sample):
                reached(sp, x_free, x_free.ago(k))
                rows = NS if sample else P
                if sample:
                    load_rows(sp, gain[0:NS, :], mod_d, 4 * D, True).then_inc(mods_in, 16)
                    load_rows(sp, shift[0:NS, :], mod_d, 3 * D, True).then_inc(mods_in, 16)
                    sp.wait_ge(mods_in, 16 * 5)
                sp.dma_start(xp[0:rows, :], x1_d[ds(k * P, rows), :]).then_inc(x_in.sem, 16)

            def spread_load(k, g):
                for part in range(3):
                    sp.dma_start(x3[part * 32:(part + 1) * 32, g, :], parts[g * 32:(g + 1) * 32, part, :]).then_inc(x3_in[g].sem, 16)

            def finish(r, sample, more=0):
                rows = NS if sample else P
                if more:
                    load(r + 2, more == "sample")
                if sample:
                    load_rows(sp, gate[0:NS, :], mod_d, 5 * D, True).then_inc(mods_in, 16)
                    sp.wait_ge(mods_in, 16 * 6)
                reached(sp, x_free, x_free.at(r + 2 if more else NT))
                sp.dma_start(xp[0:rows, :], x1_d[ds(r * P, rows), :]).then_inc(xo_in.sem, 16)
                if not sample:
                    reached(sp, part_a, part_a.at(r + 1))
                    for g in range(NG):
                        reached(sp, added, r * P + 32 * (g + 1) + NV)
                        spread_load(r + 1, g)
                reached(sp, out_set, out_set.at(r))
                dst = io["y_sample"].rearrange("b q d -> (b q) d") if sample else io["y_prompt"][0, ds(r * P, P), :]
                sp.dma_start(dst, xp[0:rows, :]).then_inc(out_kept.sem, 16)
                reached(sp, out_kept, out_kept.at(r))

            load(0, False)
            for n, name in enumerate(("sub_keys_a", "sub_keys_b")):
                sp.dma_start(cand2[:, n * NK:(n + 1) * NK], io[name][0]).then_inc(sub_in, 16)
            sp.dma_start(w_q[:, :, :], io["w_query"][0].rearrange("(k p) n -> p k n", p=P)).then_inc(wq_in, 16)
            load(1, False)
            sp.wait_ge(part_a.sem, part_a.at(0))
            for g in range(NG):
                spread_load(0, g)
            with sp.Fori(0, NT - 2) as r:
                finish(r, False, more="prompt")
            finish(NT - 2, False, more="sample")
            finish(NT - 1, False)
            finish(NT, True)

        @block.gpsimd
        def _(pool):
            pool.iota(number_i[:, :], [[1, TK]], base=0, channel_multiplier=0)
            pool.memset(ident[:, :], 0.0)
            pool.memset(sel3[:, :], 0.0)
            pool.memset(zero_h[:, :], 0.0)
            pool.memset(strip[:, :], 0.0)
            pool.drain()
            pool.memset(strip[:, P:P + 1], 1.0)
            pool.affine_select(out=ident[:, :], in_=ident[:, :], compare_op=ALU.not_equal, fill=1.0, base=0,
                               pattern=[[-1, P]], channel_multiplier=1)
            pool.drain()
            for part in range(3):
                pool.affine_select(out=sel3[:, :], in_=sel3[:, :], compare_op=ALU.not_equal, fill=1.0, base=-32 * part,
                                   pattern=[[-1, 32]], channel_multiplier=1)
                pool.drain()
            pool.sem_inc(set_up, 1)

            def spend(r, step, last=False):
                for local in range(step * PT, (step + 1) * PT):
                    t, u, v = r * P + local, local % NU, local % NV
                    reached(pool, dotted, t + 1)
                    reached(pool, added, t + 1)
                    pool.tensor_copy(slot[:, v:v + 1], idx[:, ds(t, 1)]).then_inc(slot_set, 1)
                    reached(pool, slot_set, t + 1)
                    at = bass.IndirectOffsetOnAxis(slot[:, v:v + 1], 0)
                    pool.indirect_dma_start(ub[:, u, :], None, io["expert_u"][0], at).then_inc(u_in[u], 16)
                    pool.indirect_dma_start(vb[:, v, :], None, io["expert_v"][0], at).then_inc(v_in[v], 16)

            def boundary(r, end=False):
                if not end:
                    reached(pool, routed, routed.at(r))

            rounds(pool, lambda k, step: None, lambda k, step, more=True: None, spend, boundary)

        @block.tensor
        def _(pe):
            pe.sem_inc(added, NV)
            pe.wait_ge(sub_in, 32)
            pe.wait_ge(set_up, 1)
            pe.transpose(psP[:, 0:NK], cand2[:, 0:NK], ident[:, :])
            pe.transpose(psP[:, NK:2 * NK], cand2[:, NK:2 * NK], ident[:, :]).then_inc(sub_t, 1)
            pe.wait_ge(sub_c, 1)

            bank = lambda g, c: psP[:, (g % 2) * 512 + c * P:(g % 2) * 512 + (c + 1) * P]

            def half_query(k, i):
                u, part = i // 2, i % 2
                g = u // 4
                if u % 4 == 0 and part == 0 and g >= 2:
                    reached(pe, sc_copied, sc_copied.at(k, g - 1))
                for j in range(part * KD // 2, (part + 1) * KD // 2):
                    m = pe.matmul(bank(g, u % 4), w_q[:, j, u * DK:(u + 1) * DK], hfT[:, j, :], start=j == 0, stop=j == KD - 1)
                if i % 8 == 7:
                    m.then_inc(q_out.sem, 1)

            def score(k, g):
                reached(pe, q_copied, q_copied.at(k, g + 1))
                for c in range(4):
                    m = pe.matmul(bank(g, c), qT[:, 4 * (g % 2) + c, :], sub[:, c % 2, :], start=True, stop=True)
                m.then_inc(sc_out.sem, 1)

            def ask(k, step):
                if step == 6:
                    if not (isinstance(k, int) and k == 0):
                        reached(pe, sc_copied, sc_copied.at(k - 1))
                    reached(pe, h_d, h_d.at(k))
                    for j in range(KD):
                        t = pe.transpose(psP[:, j * P:(j + 1) * P], hf[:, j * P:(j + 1) * P], ident[:, :])
                    t.then_inc(h_t.sem, 1)
                if step == 8:
                    pe.wait_ge(wq_in, 16)
                    reached(pe, hT_a, hT_a.at(k))
                    reached(pe, hT_v, hT_v.at(k))
                for i in range(4 * PH):
                    if step == 8 + i * 24 // (4 * PH):
                        half_query(k, i)
                if step - 1 in group_step:
                    score(k, group_step[step - 1])

            def choose(k, step, more=True):
                if step == 1:
                    score(k, 3)
                if step == 29:
                    if more:
                        reached(pe, sc_copied, sc_copied.at(k + 1, 3))
                    else:
                        reached(pe, sc_copied, sc_copied.at(k))
                    reached(pe, made, made.at(k))
                    pe.transpose(psP[:, 0:P], found[:, 0, :], ident[:, :]).then_inc(made_t.sem, 1)
                    pe.transpose(psP[:, P:2 * P], gates_e[:, :, :].rearrange("p h k -> p (h k)"), ident[:, :]).then_inc(made_t.sem, 1)

            def spread_row(r, local):
                reached(pe, dotted, r * P + local + NU - 1)
                g, x0 = local // 32, local % 32
                if x0 == 0 and g > 0:
                    reached(pe, x3_in[g], x3_in[g].at(r))
                pick = sel3[:, x0:x0 + 1].broadcast_to([96, P])
                for half in range(2):
                    m = pe.matmul(psX[:, local % 2, half * 512:(half + 1) * 512], pick,
                                  x3[:, g, half * 512:(half + 1) * 512], start=True, stop=True)
                m.then_inc(spread, 1)

            def spend(r, step, last=False):
                for local in range(step * PT, (step + 1) * PT):
                    t, v = r * P + local, local % NV
                    if local + 2 < P and not (last and local % PT >= PT - 2):
                        spread_row(r, local + 2)
                    reached(pe, weighed, t + 1)
                    reached(pe, v_in[v], r * (16 * P // NV) + 16 * (local // NV + 1))
                    for half in range(2):
                        m = pe.matmul(psY[:, half * 512:(half + 1) * 512], W[:, local % NW, :], vb[:, v, half * 512:(half + 1) * 512],
                                      start=False, stop=False, skip_group_check=True)
                    m.then_inc(added, 1)

            def boundary(r, end=False):
                if end:
                    return
                reached(pe, x3_in[0], x3_in[0].at(r))
                reached(pe, y_read, y_read.ago(r))
                for half in range(2):
                    pe.matmul(psY[:, half * 512:(half + 1) * 512], zero_h[:, :], x3[:, 0, half * 512:(half + 1) * 512],
                              start=True, stop=False, skip_group_check=True)
                spread_row(r, 0)
                spread_row(r, 1)

            rounds(pe, ask, choose, spend, boundary)

        @block.scalar
        def _(act):
            act.preload_act_table_set(EXP_LN)

            half = lambda g: psP[:, (g % 2) * 512:(g % 2 + 1) * 512].rearrange("p (j t) -> p j t", t=P)

            def copy_queries(k, g):
                reached(act, q_out, q_out.at(k, g + 1))
                act.activation(qT[:, 4 * (g % 2):4 * (g % 2) + 4, :], half(g), ACT.Copy).then_inc(q_copied.sem, 1)

            def copy_scores(k, g):
                reached(act, sc_out, sc_out.at(k, g + 1))
                reached(act, taken, taken.ago(k, g + 1))
                act.activation(sc[:, 4 * g:4 * g + 4, :], half(g), ACT.Copy).then_inc(sc_copied.sem, 1)

            def ask(k, step):
                if step == 4:
                    reached(act, ssq_d, ssq_d.at(k))
                    act.activation(rstd[:, :], ssq[:, :], ACT.Ln, scale=1.0 / D, bias=EPS)
                    act.drain()
                    act.activation(rstd[:, :], rstd[:, :], ACT.Exp, scale=-0.5).then_inc(rstd_d.sem, 1)
                if step == 7:
                    reached(act, h_t, h_t.at(k))
                    act.activation(hfT[:, 0:4, :], psP[:, 0:512].rearrange("p (j t) -> p j t", t=P), ACT.Copy).then_inc(hT_a.sem, 1)
                if step in group_step:
                    copy_queries(k, group_step[step])
                if step - 2 in group_step:
                    copy_scores(k, group_step[step - 2])

            def choose(k, step, more=True):
                if step == 0:
                    copy_queries(k, 3)
                if step == 1:
                    if not (isinstance(k, int) and k == 0):
                        for g in range(NG):
                            reached(act, x3_in[g], x3_in[g].at(k - 1))
                    act.activation(parts[:, 0, :], hf[:, :], ACT.Copy).then_inc(part_a.sem, 1)
                if step == 2:
                    copy_scores(k, 3)
                if step in (2, 3):
                    reached(act, part_v, part_v.at(k, step - 1))
                    act.activation(parts[:, step - 1, :], rest[:, :], ACT.Copy).then_inc(part_a.sem, 1)
                if step == 28:
                    reached(act, soft_v, soft_v.at(k))
                    act.activation(gates_e[:, :, :], gates_e[:, :, :], ACT.Exp).then_inc(soft_a.sem, 1)

            def spend(r, step, last=False):
                for local in range(step * PT, (step + 1) * PT):
                    d = local % NV
                    reached(act, dotted, r * P + local + 1 + NU)
                    act.activation(act_o[:, d:d + 1], dot[:, d:d + 1], ACT.Gelu).then_inc(acted, 1)

            rounds(act, ask, choose, spend, lambda r, end=False: None)

        @block.vector
        def _(dve):
            prime(dve, x_free, y_read, taken)
            dve.sem_inc(dotted, NU)
            dve.wait_ge(sub_t, 1)
            dve.tensor_copy(sub[:, :, :], psP[:, 0:2 * NK].rearrange("p (a n) -> p a n", a=2)).then_inc(sub_c, 1)
            dve.wait_ge(set_up, 1)
            dve.tensor_copy(number[:, :], number_i[:, :])
            dve.drain()

            def top16(values, spare, top, at):
                dve.max(top[:, 0:8], values)
                dve.drain()
                dve.max_index(at[:, 0:8], top[:, 0:8], values)
                dve.match_replace(spare, top[:, 0:8], values, LOW)
                dve.drain()
                dve.max(top[:, 8:16], spare)
                dve.drain()
                dve.max_index(at[:, 8:16], top[:, 8:16], spare)
                dve.drain()

            def side(k, u):
                if u % 4 == 0:
                    reached(dve, sc_copied, sc_copied.at(k, u // 4 + 1))
                top16(sc[:, u, :], cand2[:, 0:NK], va[:, u, :], ia[:, u, :])
                if u % 4 == 3:
                    dve.sem_inc(taken.sem, 1)

            def pairs(h):
                dve.tensor_tensor(cand[:, :, :], va[:, 2 * h, :].unsqueeze(2).broadcast_to([P, TK, TK]),
                                  va[:, 2 * h + 1, :].unsqueeze(1).broadcast_to([P, TK, TK]), ALU.add)
                dve.drain()
                top16(cand[:, :, :].rearrange("p a b -> p (a b)"), cand2[:, :], ts[:, h, :], pos[:, h, :])

            def look_up(half, which):
                H4, w = PH // 2, PH // 2 * TK
                hs = slice(half * H4, (half + 1) * H4)
                cs = slice(half * w, (half + 1) * w)
                us = slice(half * 2 * H4, (half + 1) * 2 * H4)
                if which == 0:
                    flat_pos = pos[:, hs, :].rearrange("p h k -> p (h k)")
                    dve.tensor_scalar(pij[:, 0, cs], flat_pos, 4, None, ALU.logical_shift_right)
                    dve.tensor_scalar(pij[:, 1, cs], flat_pos, TK - 1, None, ALU.bitwise_and)
                    dve.tensor_copy(iaf[:, us, :], ia[:, us, :])
                    dve.drain()
                    dve.tensor_copy(pijf[:, :, cs], pij[:, :, cs])
                    dve.drain()
                hot = rest[:, :].rearrange("p (x k i) -> p x k i", k=TK, i=TK)
                flat = hot.rearrange("p x k i -> p (x k) i")
                table = iaf[:, us, :].rearrange("p (h s) i -> p h s i", s=2)[:, :, which, :]
                dve.tensor_tensor(flat, pijf[:, which, cs].unsqueeze(2).broadcast_to([P, w, TK]),
                                  number[:, :].unsqueeze(1).broadcast_to([P, w, TK]), ALU.is_equal)
                dve.drain()
                dve.tensor_tensor(hot, hot, table.unsqueeze(2).broadcast_to([P, H4, TK, TK]), ALU.mult)
                dve.drain()
                dve.tensor_reduce(found[:, which, cs], flat, AX.X, ALU.add)
                dve.drain()
                if which == 1:
                    dve.scalar_tensor_tensor(out=found[:, 0, cs], in0=found[:, 0, cs], scalar=float(NK), in1=found[:, 1, cs],
                                             op0=ALU.mult, op1=ALU.add)
                    dve.drain()

            def norm_sum(k):
                reached(dve, x_in, x_in.at(k))
                dve.tensor_tensor_reduce(junk[:, :], xp[:, :], xp[:, :], 1.0, 0.0, ALU.mult, ALU.add, ssq[:, :]).then_inc(ssq_d.sem, 1)
                dve.drain()

            def norm_scale(k):
                reached(dve, rstd_d, rstd_d.at(k))
                dve.drain()
                dve.scalar_tensor_tensor(out=hf[:, :], in0=xp[:, :], scalar=rstd[:, 0:1], in1=gain[:, :], op0=ALU.mult, op1=ALU.mult)
                dve.drain()
                dve.tensor_tensor(hf[:, :], hf[:, :], shift[:, :], ALU.add).then_inc(h_d.sem, 1)
                dve.drain()
                dve.sem_inc(x_free.sem, 1)

            def ask(k, step):
                if step == 4:
                    dve.wait_ge(mods_in, 48)
                    norm_sum(k)
                if step == 5:
                    norm_scale(k)
                if step == 7:
                    reached(dve, h_t, h_t.at(k))
                    dve.tensor_copy(hfT[:, 4:8, :], psP[:, 512:1024].rearrange("p (j t) -> p j t", t=P)).then_inc(hT_v.sem, 1)

            def choose(k, step, more=True):
                if step == 2:
                    reached(dve, part_a, part_a.at(k, 1))
                    dve.tensor_tensor(rest[:, :], hf[:, :], parts[:, 0, :], ALU.subtract).then_inc(part_v.sem, 1)
                if step == 3:
                    reached(dve, part_a, part_a.at(k, 2))
                    dve.drain()
                    dve.tensor_tensor(rest[:, :], rest[:, :], parts[:, 1, :], ALU.subtract).then_inc(part_v.sem, 1)
                if step < 3 * PH:
                    if step % 3 == 2:
                        pairs(step // 3)
                    else:
                        side(k, 2 * (step // 3) + step % 3)
                if 24 <= step <= 27:
                    look_up((step - 24) // 2, step % 2)
                if step == 28:
                    dve.tensor_tensor(gates_e[:, :, :], ts[:, :, :], ts[:, :, 0:1].broadcast_to([P, PH, TK]), ALU.subtract).then_inc(soft_v.sem, 1)
                    reached(dve, soft_a, soft_a.at(k))
                    dve.drain()
                    dve.tensor_reduce(gsum[:, :], gates_e[:, :, :], AX.X, ALU.add)
                    dve.drain()
                    dve.reciprocal(gsum[:, :], gsum[:, :])
                    dve.drain()
                    dve.tensor_tensor(gates_e[:, :, :], gates_e[:, :, :], gsum[:, :].unsqueeze(2).broadcast_to([P, PH, TK]), ALU.mult)
                    dve.drain()
                    dve.sem_inc(made.sem, 1)
                if step == 30:
                    reached(dve, made_t, made_t.at(k))
                    dve.tensor_copy(idx[:, ds(k * P, P)], psP[:, 0:P])
                    dve.tensor_copy(gT[:, ds(k * P, P)], psP[:, P:2 * P])
                    dve.drain()
                    dve.sem_inc(routed.sem, 1)

            def weigh(r, local):
                d = local % NV
                reached(dve, acted, r * P + local + 1)
                reached(dve, added, r * P + local + 1 + NV - NW)
                dve.tensor_scalar(W[:, local % NW, :], strip[:, P - local:2 * P - local], act_o[:, d:d + 1],
                                  gT[:, ds(r * P + local, 1)], ALU.mult, ALU.mult).then_inc(weighed, 1)

            def spend(r, step, last=False):
                for local in range(step * PT, (step + 1) * PT):
                    t, u, d = r * P + local, local % NU, local % NV
                    reached(dve, spread, t + 1)
                    reached(dve, u_in[u], r * (16 * P // NU) + 16 * (local // NU + 1))
                    dve.tensor_tensor_reduce(junk[:, :], ub[:, u, :], psX[:, local % 2, :], 1.0, 0.0, ALU.mult, ALU.add,
                                             dot[:, d:d + 1]).then_inc(dotted, 1)
                    if local % PT > 0:
                        weigh(r, local - 1)
                    dve.drain()
                weigh(r, (step + 1) * PT - 1)
                dve.drain()

            def boundary(r, end=False):
                if end:
                    last = isinstance(r, int) and r == NT
                    reached(dve, added, (SEQ + NS if last else (r + 1) * P) + NV)
                    reached(dve, xo_in, xo_in.at(r))
                    dve.tensor_tensor(rest[:, :], psY[:, :], gate[:, :], ALU.mult).then_inc(y_read.sem, 1)
                    dve.drain()
                    dve.tensor_tensor(xp[:, :], rest[:, :], xp[:, :], ALU.add).then_inc(out_set.sem, 1)
                    dve.drain()

            rounds(dve, ask, choose, spend, boundary)


_INS = ["x_prompt", "x_sample", "cache_sb_k", "cache_sb_v", "state_mlstm_C", "state_mlstm_n", "state_mlstm_m",
        "page_table", "c_prompt", "c_sample", "w_ada", "b_ada", "norm_mix_g", "norm_ffn_g", "w_in", "b_gates",
        "qnorm_g", "knorm_g", "sb_bias", "mlstm_head_g", "w_out", "w_query", "sub_keys_a", "sub_keys_b",
        "expert_u", "expert_v"]
_OUTS = [("y_prompt", (1, SEQ, D)), ("y_sample", (NB, SQ, D)),
         ("k_prompt", (1, 1, SEQ, HS, DS)), ("v_prompt", (1, 1, SEQ, HS, DS)),
         ("C_prompt", (1, 1, HM, DM, DM)), ("n_prompt", (1, 1, HM, DM)), ("m_prompt", (1, 1, HM)),
         ("k_sample", (1, NB, SQ, HS, DS)), ("v_sample", (1, NB, SQ, HS, DS)),
         ("C_sample", (1, NB, HM, DM, DM)), ("n_sample", (1, NB, HM, DM)), ("m_sample", (1, NB, HM))]


def kernel(**inputs):
    import concourse.bacc as bacc
    from concourse.bass_utils import run_bass_kernel_spmd as run

    nc = bacc.Bacc("TRN2", target_bir_lowering=False, num_devices=1)
    arrays, io = {}, {}
    for name in _INS:
        a = np.ascontiguousarray(inputs[name])
        arrays[f"in_{name}"] = a
        io[name] = nc.dram_tensor(f"in_{name}", a.shape, mybir.dt.from_np(a.dtype), kind="ExternalInput").ap()
    for name, shape in _OUTS:
        io[name] = nc.dram_tensor(f"out_{name}", shape, F32, kind="ExternalOutput").ap()
    build(nc, io)
    r = run(nc, [arrays], core_ids=[0])
    return tuple(r.results[0][f"out_{name}"] for name, _ in _OUTS)
```
